# Optimizing a Trainium2 kernel written in Bass

```python
import math
import jax
import jax.numpy as jnp
from jax import lax
import numpy as np
import jax, jax.numpy as jnp

D_MODEL = 1024
BATCH = 1
SEQ = 256
DEPTH = 2

HEAD_DIM = 64
N_HEADS = D_MODEL // HEAD_DIM
MOBA_HEADS = N_HEADS // 2
DIL_HEADS = N_HEADS - MOBA_HEADS
MOBA_BLOCK = 256
MOBA_TOPK = 3
MOBA_QCHUNK = 16
DIL_PAIRS = ((128, 1), (512, 4), (2048, 16))
DIL_BLOCK = 128
NSA_HEADS = N_HEADS
NSA_GROUPS = 4
NSA_HPG = NSA_HEADS // NSA_GROUPS
NSA_CMP_LEN = 32
NSA_CMP_STRIDE = 16
NSA_CMP_HIDDEN = 2 * HEAD_DIM
NSA_SEL_BLOCK = 64
NSA_SEL_TOPN = 16
NSA_WINDOW = 512
NSA_WIN_BLOCK = 128
NSA_QCHUNK = 32
NSA_FORCE = 1.0e6
REL_BUCKETS = 32
REL_MAX_DIST = 2048
FFN_HIDDEN = -((-8 * D_MODEL) // (3 * 256)) * 256
PLE_DIM = 256
N_EVEN = (DEPTH + 1) // 2
N_ODD = DEPTH // 2
RMS_EPS = 1e-6
ATTN_SCALE = HEAD_DIM ** -0.5
F32 = jnp.float32


def _rms(x, g):
    xf = x.astype(F32)
    y = xf * lax.rsqrt(jnp.mean(xf * xf, axis=-1, keepdims=True) + RMS_EPS)
    return (y * g.astype(F32)).astype(x.dtype)

def _heads(t, n):
    B, S, _ = t.shape
    return t.reshape(B, S, n, HEAD_DIM).transpose(0, 2, 1, 3)

def _rel_bucket(dist):
    n = jnp.maximum(dist, 0)
    exact = REL_BUCKETS // 2
    nf = jnp.maximum(n, 1).astype(F32)
    large = exact + (jnp.log(nf / exact) / math.log(REL_MAX_DIST / exact) * (REL_BUCKETS - exact)).astype(jnp.int32)
    return jnp.where(n < exact, n, jnp.minimum(large, REL_BUCKETS - 1))

def _masked_softmax(s, mask):
    s = jnp.where(mask, s.astype(F32), -jnp.inf)
    m = jnp.max(s, axis=-1, keepdims=True)
    m = jnp.where(jnp.isfinite(m), m, 0.0)
    e = jnp.exp(s - m)
    l = jnp.sum(e, axis=-1, keepdims=True)
    p = e / jnp.where(l > 0, l, 1.0)
    return p, (m + jnp.log(l))[..., 0]

def _moba(q, k, v, tab):
    B, H, S, hd = q.shape
    nb = -(-S // MOBA_BLOCK)
    padw = ((0, 0), (0, 0), (0, nb * MOBA_BLOCK - S), (0, 0))
    kb = jnp.pad(k, padw).reshape(B, H, nb, MOBA_BLOCK, hd)
    vb = jnp.pad(v, padw).reshape(B, H, nb, MOBA_BLOCK, hd)
    kmean = jnp.mean(kb.astype(F32), axis=3)
    own = jnp.arange(S) // MOBA_BLOCK
    gate = jnp.einsum('bhsd,bhnd->bhsn', q.astype(F32), kmean)
    gate = jnp.where(jnp.arange(nb)[None, :] < own[:, None], gate, -jnp.inf)
    n_sel = min(MOBA_TOPK, nb)
    _, sel = lax.top_k(gate, n_sel)
    sel_ok = sel < own[:, None]
    nc = S // MOBA_QCHUNK

    def to_chunks(t):
        return jnp.moveaxis(t.reshape(B, H, nc, MOBA_QCHUNK, *t.shape[3:]), 2, 0)

    b_ix = jnp.arange(B)[:, None, None, None]
    h_ix = jnp.arange(H)[None, :, None, None]
    a_blk = jnp.arange(MOBA_BLOCK)

    def chunk(args):
        c, qc, sc, okc = args
        t = c * MOBA_QCHUNK + jnp.arange(MOBA_QCHUNK)
        j = (c * MOBA_QCHUNK) // MOBA_BLOCK
        k_own = lax.dynamic_index_in_dim(kb, j, axis=2, keepdims=False)
        v_own = lax.dynamic_index_in_dim(vb, j, axis=2, keepdims=False)
        d_own = t[:, None] - (j * MOBA_BLOCK + a_blk)[None, :]
        s_own = jnp.einsum('bhqd,bhkd->bhqk', qc, k_own).astype(F32) * ATTN_SCALE + tab[:, _rel_bucket(d_own)].astype(F32)
        m_own = jnp.broadcast_to(d_own >= 0, s_own.shape)
        k_sel = kb[b_ix, h_ix, sc].reshape(B, H, MOBA_QCHUNK, n_sel * MOBA_BLOCK, hd)
        v_sel = vb[b_ix, h_ix, sc].reshape(B, H, MOBA_QCHUNK, n_sel * MOBA_BLOCK, hd)
        kpos = (sc[..., None] * MOBA_BLOCK + a_blk).reshape(B, H, MOBA_QCHUNK, n_sel * MOBA_BLOCK)
        s_sel = jnp.einsum('bhqd,bhqkd->bhqk', qc, k_sel).astype(F32) * ATTN_SCALE + tab[h_ix, _rel_bucket(t[:, None] - kpos)].astype(F32)
        m_sel = jnp.repeat(okc, MOBA_BLOCK, axis=-1)
        pr, _ = _masked_softmax(jnp.concatenate([s_own, s_sel], axis=-1), jnp.concatenate([m_own, m_sel], axis=-1))
        p_own = pr[..., :MOBA_BLOCK].astype(v.dtype)
        p_sel = pr[..., MOBA_BLOCK:].astype(v.dtype)
        return jnp.einsum('bhqk,bhkd->bhqd', p_own, v_own) + jnp.einsum('bhqk,bhqkd->bhqd', p_sel, v_sel)

    out = lax.map(chunk, (jnp.arange(nc), to_chunks(q), to_chunks(sel), to_chunks(sel_ok)))
    return jnp.moveaxis(out, 0, 2).reshape(B, H, S, hd)

def _stride_split(t, dil, L):
    B, H, S, hd = t.shape
    t = jnp.pad(t, ((0, 0), (0, 0), (0, L * dil - S), (0, 0)))
    return t.reshape(B, H, L, dil, hd).transpose(0, 1, 3, 2, 4)

def _band(t):
    prev = jnp.pad(t, ((0, 0), (0, 0), (0, 0), (1, 0), (0, 0), (0, 0)))[:, :, :, :-1]
    return jnp.concatenate([prev, t], axis=4)

def _dilated(q, k, v, tab):
    B, H, S, hd = q.shape
    blk = DIL_BLOCK
    outs, lses = [], []
    for window, dil in DIL_PAIRS:
        steps = window // dil
        L = -(-S // (dil * blk)) * blk
        nbk = L // blk
        qs = _stride_split(q, dil, L).reshape(B, H, dil, nbk, blk, hd)
        ks = _stride_split(k, dil, L).reshape(B, H, dil, nbk, blk, hd)
        vs = _stride_split(v, dil, L).reshape(B, H, dil, nbk, blk, hd)
        step = jnp.arange(blk)[:, None] + blk - jnp.arange(2 * blk)[None, :]
        key_ok = (jnp.arange(nbk)[:, None] * blk - blk + jnp.arange(2 * blk)[None, :]) >= 0
        mask = ((step >= 0) & (step <= steps))[None] & key_ok[:, None, :]
        bias = tab[:, _rel_bucket(step * dil)].astype(F32)
        s = jnp.einsum('bhrjqd,bhrjkd->bhrjqk', qs, _band(ks)).astype(F32) * ATTN_SCALE + bias[None, :, None, None]
        pr, lse = _masked_softmax(s, mask)
        o = jnp.einsum('bhrjqk,bhrjkd->bhrjqd', pr.astype(v.dtype), _band(vs))
        outs.append(o.reshape(B, H, dil, L, hd).transpose(0, 1, 3, 2, 4).reshape(B, H, L * dil, hd)[:, :, :S])
        lses.append(lse.reshape(B, H, dil, L).transpose(0, 1, 3, 2).reshape(B, H, L * dil)[:, :, :S])
    w = jax.nn.softmax(jnp.stack(lses), axis=0)
    o = jnp.einsum('nbhs,nbhsd->bhsd', w, jnp.stack(outs).astype(F32))
    return o.astype(q.dtype)

def _compress(t, pos_emb, w1, b1, w2, b2):
    B, G, S, hd = t.shape
    nc = (S - NSA_CMP_LEN) // NSA_CMP_STRIDE + 1
    idx = jnp.arange(nc)[:, None] * NSA_CMP_STRIDE + jnp.arange(NSA_CMP_LEN)[None, :]
    blocks = (t[:, :, idx] + pos_emb).reshape(B, G, nc, NSA_CMP_LEN * hd)
    return jax.nn.gelu(blocks @ w1 + b1) @ w2 + b2

def _nsa(q, kc, vc, ks, vs, kw, vw, gates, tab):
    B, H, S, hd = q.shape
    G, hpg = NSA_GROUPS, NSA_HPG
    qg = q.reshape(B, G, hpg, S, hd)
    tabg = tab.reshape(G, hpg, REL_BUCKETS)
    t = jnp.arange(S)
    nc = kc.shape[2]
    dc = t[:, None] - (jnp.arange(nc) * NSA_CMP_STRIDE + NSA_CMP_LEN - 1)[None, :]
    s = jnp.einsum('bghsd,bgcd->bghsc', qg, kc).astype(F32) * ATTN_SCALE + tabg[:, :, _rel_bucket(dc)].astype(F32)
    p_cmp, _ = _masked_softmax(s, dc >= 0)
    o_cmp = jnp.einsum('bghsc,bgcd->bghsd', p_cmp.astype(vc.dtype), vc)
    n_sel = -(-S // NSA_SEL_BLOCK)
    cstart = jnp.arange(nc) * NSA_CMP_STRIDE
    sstart = jnp.arange(n_sel) * NSA_SEL_BLOCK
    overlap = jnp.maximum(jnp.minimum(cstart[:, None] + NSA_CMP_LEN, sstart[None, :] + NSA_SEL_BLOCK) - jnp.maximum(cstart[:, None], sstart[None, :]), 0).astype(F32)
    imp = jnp.einsum('bghsc,cn->bgsn', p_cmp, overlap)
    cur = (t // NSA_SEL_BLOCK)[:, None]
    blk_id = jnp.arange(n_sel)[None, :]
    forced = (blk_id == 0) | (blk_id == cur) | (blk_id == cur - 1)
    imp = jnp.where(blk_id <= cur, imp + jnp.where(forced, NSA_FORCE, 0.0), -jnp.inf)
    n_top = min(NSA_SEL_TOPN, n_sel)
    _, sel = lax.top_k(imp, n_top)
    padw = ((0, 0), (0, 0), (0, n_sel * NSA_SEL_BLOCK - S), (0, 0))
    ksb = jnp.pad(ks, padw).reshape(B, G, n_sel, NSA_SEL_BLOCK, hd)
    vsb = jnp.pad(vs, padw).reshape(B, G, n_sel, NSA_SEL_BLOCK, hd)
    nq = S // NSA_QCHUNK
    b_ix = jnp.arange(B)[:, None, None, None]
    g_ix = jnp.arange(G)[None, :, None, None]
    h_ix = jnp.arange(hpg)[None, None, :, None, None]
    a_blk = jnp.arange(NSA_SEL_BLOCK)

    def sel_chunk(args):
        c, qc, sc = args
        tq = c * NSA_QCHUNK + jnp.arange(NSA_QCHUNK)
        kk = ksb[b_ix, g_ix, sc].reshape(B, G, NSA_QCHUNK, n_top * NSA_SEL_BLOCK, hd)
        vv = vsb[b_ix, g_ix, sc].reshape(B, G, NSA_QCHUNK, n_top * NSA_SEL_BLOCK, hd)
        kpos = (sc[..., None] * NSA_SEL_BLOCK + a_blk).reshape(B, G, NSA_QCHUNK, n_top * NSA_SEL_BLOCK)
        dist = tq[:, None] - kpos
        bias = tabg[g_ix[..., None], h_ix, _rel_bucket(dist)[:, :, None]].astype(F32)
        s = jnp.einsum('bghqd,bgqkd->bghqk', qc, kk).astype(F32) * ATTN_SCALE + bias
        pr, _ = _masked_softmax(s, (dist >= 0)[:, :, None])
        return jnp.einsum('bghqk,bgqkd->bghqd', pr.astype(vv.dtype), vv)

    qch = jnp.moveaxis(qg.reshape(B, G, hpg, nq, NSA_QCHUNK, hd), 3, 0)
    sch = jnp.moveaxis(sel.reshape(B, G, nq, NSA_QCHUNK, n_top), 2, 0)
    o_slc = jnp.moveaxis(lax.map(sel_chunk, (jnp.arange(nq), qch, sch)), 0, 3).reshape(B, G, hpg, S, hd)
    nw = S // NSA_WIN_BLOCK
    span = NSA_WINDOW + NSA_WIN_BLOCK
    kwp = jnp.pad(kw, ((0, 0), (0, 0), (NSA_WINDOW, 0), (0, 0)))
    vwp = jnp.pad(vw, ((0, 0), (0, 0), (NSA_WINDOW, 0), (0, 0)))
    kidx = jnp.arange(span)[None, :]
    dw = jnp.arange(NSA_WIN_BLOCK)[:, None] + NSA_WINDOW - kidx
    bias_w = tabg[:, :, _rel_bucket(dw)].astype(F32)

    def win_block(args):
        j, qb = args
        kb_ = lax.dynamic_slice_in_dim(kwp, j * NSA_WIN_BLOCK, span, axis=2)
        vb_ = lax.dynamic_slice_in_dim(vwp, j * NSA_WIN_BLOCK, span, axis=2)
        ok = (dw >= 0) & (dw < NSA_WINDOW) & (j * NSA_WIN_BLOCK - NSA_WINDOW + kidx >= 0)
        s = jnp.einsum('bghqd,bgkd->bghqk', qb, kb_).astype(F32) * ATTN_SCALE + bias_w
        pr, _ = _masked_softmax(s, ok)
        return jnp.einsum('bghqk,bgkd->bghqd', pr.astype(vb_.dtype), vb_)

    qwb = jnp.moveaxis(qg.reshape(B, G, hpg, nw, NSA_WIN_BLOCK, hd), 3, 0)
    o_win = jnp.moveaxis(lax.map(win_block, (jnp.arange(nw), qwb)), 0, 3).reshape(B, G, hpg, S, hd)
    o = (gates[..., 0:1] * o_cmp.reshape(B, H, S, hd) + gates[..., 1:2] * o_slc.reshape(B, H, S, hd)
         + gates[..., 2:3] * o_win.reshape(B, H, S, hd))
    return o.astype(q.dtype)

def _mixer_ab(xn, w_in, w_out, qn_a, kn_a, qn_b, kn_b, rel_bias):
    B, S, _ = xn.shape
    wa = MOBA_HEADS * HEAD_DIM
    wb = DIL_HEADS * HEAD_DIM
    qa, ka, va, qb, kb, vb = jnp.split(xn @ w_in, [wa, 2 * wa, 3 * wa, 3 * wa + wb, 3 * wa + 2 * wb], axis=-1)
    oa = _moba(_rms(_heads(qa, MOBA_HEADS), qn_a), _rms(_heads(ka, MOBA_HEADS), kn_a), _heads(va, MOBA_HEADS), rel_bias[:, :MOBA_HEADS].T)
    ob = _dilated(_rms(_heads(qb, DIL_HEADS), qn_b), _rms(_heads(kb, DIL_HEADS), kn_b), _heads(vb, DIL_HEADS), rel_bias[:, MOBA_HEADS:].T)
    o = jnp.concatenate([oa, ob], axis=1).transpose(0, 2, 1, 3).reshape(B, S, D_MODEL)
    return o @ w_out

def _mixer_nsa(xn, w_in, w_out, qn, kn_c, kn_s, kn_w, cmp_k, cmp_v, rel_bias):
    B, S, _ = xn.shape
    qw = NSA_HEADS * HEAD_DIM
    kvw = NSA_GROUPS * HEAD_DIM
    q, kc, vc, ks, vs, kw, vw, g = jnp.split(xn @ w_in, [qw + i * kvw for i in range(7)], axis=-1)
    q = _rms(_heads(q, NSA_HEADS), qn)
    kc = _rms(_compress(_heads(kc, NSA_GROUPS), *cmp_k), kn_c)
    vc = _compress(_heads(vc, NSA_GROUPS), *cmp_v)
    ks = _rms(_heads(ks, NSA_GROUPS), kn_s)
    kw = _rms(_heads(kw, NSA_GROUPS), kn_w)
    gates = jax.nn.sigmoid(g.astype(F32)).reshape(B, S, NSA_HEADS, 3).transpose(0, 2, 1, 3)
    o = _nsa(q, kc, vc, ks, _heads(vs, NSA_GROUPS), kw, _heads(vw, NSA_GROUPS), gates, rel_bias.T)
    return o.transpose(0, 2, 1, 3).reshape(B, S, D_MODEL) @ w_out

def _swiglu(x, wg, wu, wd):
    return (jax.nn.silu(x @ wg) * (x @ wu)) @ wd

def first_inputs(seed: int = 0) -> dict:
    key = jax.random.key(seed)
    keys = iter(jax.random.split(key, 40))

    def nrm(shape, scale):
        return jax.random.normal(next(keys), shape, F32) * scale

    def gain(shape):
        return 1.0 + nrm(shape, 0.02)

    D, hd, F, CH = D_MODEL, HEAD_DIM, FFN_HIDDEN, NSA_CMP_HIDDEN
    res = (2 * DEPTH) ** -0.5
    w_ab = 3 * (MOBA_HEADS + DIL_HEADS) * hd
    w_nsa = NSA_HEADS * hd + 6 * NSA_GROUPS * hd + 3 * NSA_HEADS
    cin = NSA_CMP_LEN * hd
    return {
        'x': nrm((BATCH, SEQ, D), 1.0),
        'p': nrm((DEPTH, BATCH, SEQ, PLE_DIM), 1.0),
        'rel_bias': nrm((REL_BUCKETS, N_HEADS), 0.5),
        'norm_mix': gain((DEPTH, D)),
        'norm_ffn': gain((DEPTH, D)),
        'norm_ple': gain((DEPTH, D)),
        'w_ffn_gate': nrm((DEPTH, D, F), D ** -0.5),
        'w_ffn_up': nrm((DEPTH, D, F), D ** -0.5),
        'w_ffn_down': nrm((DEPTH, F, D), F ** -0.5 * res),
        'w_ple_proj': nrm((DEPTH, PLE_DIM, D), PLE_DIM ** -0.5 * res),
        'w_ple_gate': nrm((DEPTH, D, D), D ** -0.5),
        'w_in_ab': nrm((N_EVEN, D, w_ab), D ** -0.5),
        'w_out_ab': nrm((N_EVEN, D, D), D ** -0.5 * res),
        'qn_moba': gain((N_EVEN, hd)),
        'kn_moba': gain((N_EVEN, hd)),
        'qn_dil': gain((N_EVEN, hd)),
        'kn_dil': gain((N_EVEN, hd)),
        'w_in_nsa': nrm((N_ODD, D, w_nsa), D ** -0.5),
        'w_out_nsa': nrm((N_ODD, D, D), D ** -0.5 * res),
        'qn_nsa': gain((N_ODD, hd)),
        'kn_cmp': gain((N_ODD, hd)),
        'kn_slc': gain((N_ODD, hd)),
        'kn_win': gain((N_ODD, hd)),
        'cmp_k_pos': nrm((N_ODD, NSA_CMP_LEN, hd), 0.1),
        'cmp_k_w1': nrm((N_ODD, cin, CH), cin ** -0.5),
        'cmp_k_b1': nrm((N_ODD, CH), 0.01),
        'cmp_k_w2': nrm((N_ODD, CH, hd), CH ** -0.5),
        'cmp_k_b2': nrm((N_ODD, hd), 0.01),
        'cmp_v_pos': nrm((N_ODD, NSA_CMP_LEN, hd), 0.1),
        'cmp_v_w1': nrm((N_ODD, cin, CH), cin ** -0.5),
        'cmp_v_b1': nrm((N_ODD, CH), 0.01),
        'cmp_v_w2': nrm((N_ODD, CH, hd), CH ** -0.5),
        'cmp_v_b2': nrm((N_ODD, hd), 0.01),
    }

def first_block(x, p, rel_bias, norm_mix, norm_ffn, norm_ple, w_ffn_gate, w_ffn_up, w_ffn_down,
              w_ple_proj, w_ple_gate, w_in_ab, w_out_ab, qn_moba, kn_moba, qn_dil, kn_dil,
              w_in_nsa, w_out_nsa, qn_nsa, kn_cmp, kn_slc, kn_win,
              cmp_k_pos, cmp_k_w1, cmp_k_b1, cmp_k_w2, cmp_k_b2,
              cmp_v_pos, cmp_v_w1, cmp_v_b1, cmp_v_w2, cmp_v_b2):
    h = x
    for i in range(DEPTH):
        e = i // 2
        xn = _rms(h, norm_mix[i])
        if i % 2 == 0:
            mix = _mixer_ab(xn, w_in_ab[e], w_out_ab[e], qn_moba[e], kn_moba[e], qn_dil[e], kn_dil[e], rel_bias)
        else:
            cmp_k = (cmp_k_pos[e], cmp_k_w1[e], cmp_k_b1[e], cmp_k_w2[e], cmp_k_b2[e])
            cmp_v = (cmp_v_pos[e], cmp_v_w1[e], cmp_v_b1[e], cmp_v_w2[e], cmp_v_b2[e])
            mix = _mixer_nsa(xn, w_in_nsa[e], w_out_nsa[e], qn_nsa[e], kn_cmp[e], kn_slc[e], kn_win[e], cmp_k, cmp_v, rel_bias)
        h = h + mix.astype(h.dtype)
        h = h + _swiglu(_rms(h, norm_ffn[i]), w_ffn_gate[i], w_ffn_up[i], w_ffn_down[i])
        gate = jax.nn.sigmoid(_rms(h, norm_ple[i]) @ w_ple_gate[i])
        h = h + gate * (p[i] @ w_ple_proj[i])
    return h


N_HEADS_2 = 8
N_KV_HEADS = 2
ATTN_WIDTH = N_HEADS_2 * HEAD_DIM
KV_WIDTH = N_KV_HEADS * HEAD_DIM
WINDOW = 128
BLOCK = 128
ROPE_DIM = HEAD_DIM // 4
ROPE_THETA = 500000.0
CONV_WIDTH = D_MODEL - ATTN_WIDTH
CONV_K = 3
MIX_WIDTH = ATTN_WIDTH + CONV_WIDTH
IN_WIDTH = ATTN_WIDTH + 2 * KV_WIDTH + 3 * CONV_WIDTH
SPLITS = (ATTN_WIDTH, ATTN_WIDTH + KV_WIDTH, ATTN_WIDTH + 2 * KV_WIDTH,
          ATTN_WIDTH + 2 * KV_WIDTH + CONV_WIDTH, ATTN_WIDTH + 2 * KV_WIDTH + 2 * CONV_WIDTH)
N_EXPERT_GROUPS = 4
EXPERTS_PER_GROUP = 8
N_EXPERTS = N_EXPERT_GROUPS * EXPERTS_PER_GROUP
TOP_K = 2
D_EXPERT = 512
MOE_BLOCK = 256
EPS = 1e-6
NEG_INF = -1e30


def rmsnorm(x, g):
    xf = x.astype(jnp.float32)
    y = xf * lax.rsqrt(jnp.mean(xf * xf, axis=-1, keepdims=True) + EPS)
    return (y * g.astype(jnp.float32)).astype(x.dtype)

def rope_tables(seq):
    pos = jnp.arange(seq, dtype=jnp.float32)
    inv_freq = ROPE_THETA ** (-jnp.arange(0, ROPE_DIM, 2, dtype=jnp.float32) / ROPE_DIM)
    ang = pos[:, None] * inv_freq[None, :]
    return jnp.cos(ang)[:, None, :], jnp.sin(ang)[:, None, :]

def partial_rope(x, cos, sin):
    half = ROPE_DIM // 2
    xf = x.astype(jnp.float32)
    x1, x2, rest = xf[..., :half], xf[..., half:ROPE_DIM], xf[..., ROPE_DIM:]
    out = jnp.concatenate([x1 * cos - x2 * sin, x2 * cos + x1 * sin, rest], axis=-1)
    return out.astype(x.dtype)

def windowed_gqa_with_sink(q, k, v, sink):
    b, s = q.shape[0], q.shape[1]
    nb = s // BLOCK
    grp = N_HEADS_2 // N_KV_HEADS
    qb = q.reshape(b, nb, BLOCK, N_KV_HEADS, grp, HEAD_DIM)

    def band(t):
        tp = jnp.pad(t, ((0, 0), (BLOCK, BLOCK), (0, 0), (0, 0)))
        tp = tp.reshape(b, nb + 2, BLOCK, N_KV_HEADS, HEAD_DIM)
        return jnp.concatenate([tp[:, :-2], tp[:, 1:-1], tp[:, 2:]], axis=2)

    kb, vb = band(k), band(v)
    scores = jnp.einsum('bnqhgd,bnkhd->bnhgqk', qb, kb,
                        preferred_element_type=jnp.float32) * (HEAD_DIM ** -0.5)
    qi = jnp.arange(BLOCK)[:, None]
    kj = jnp.arange(3 * BLOCK)[None, :]
    k_pos = (jnp.arange(nb)[:, None, None] - 1) * BLOCK + kj
    mask = (jnp.abs(kj - BLOCK - qi) <= WINDOW) & (k_pos >= 0) & (k_pos < s)
    scores = jnp.where(mask[None, :, None, None], scores, NEG_INF)
    sink_col = jnp.broadcast_to(
        sink.astype(jnp.float32).reshape(N_KV_HEADS, grp)[None, None, :, :, None, None],
        scores.shape[:-1] + (1,))
    probs = jax.nn.softmax(jnp.concatenate([scores, sink_col], axis=-1), axis=-1)[..., :-1]
    out = jnp.einsum('bnhgqk,bnkhd->bnqhgd', probs.astype(v.dtype), vb)
    return out.reshape(b, s, ATTN_WIDTH)

def centred_short_conv(u, w):
    up = jnp.pad(u, ((0, 0), (1, 1), (0, 0)))
    return up[:, :-2] * w[0] + up[:, 1:-1] * w[1] + up[:, 2:] * w[2]

def hybrid_mixer(h, w_in, sink, conv_w, g_attn, g_conv, w_out, cos, sin):
    b, s, _ = h.shape
    proj = h @ w_in
    q, k, v, gate_b, gate_c, u = jnp.split(proj, SPLITS, axis=-1)
    q = partial_rope(q.reshape(b, s, N_HEADS_2, HEAD_DIM), cos, sin)
    k = partial_rope(k.reshape(b, s, N_KV_HEADS, HEAD_DIM), cos, sin)
    v = v.reshape(b, s, N_KV_HEADS, HEAD_DIM)
    y_attn = windowed_gqa_with_sink(q, k, v, sink)
    y_conv = gate_b * centred_short_conv(gate_c * u, conv_w)
    y = jnp.concatenate([rmsnorm(y_attn, g_attn), rmsnorm(y_conv, g_conv)], axis=-1)
    return y @ w_out

def hierarchical_moe(h, w_rg, b_rg, w_re, b_re, w_gate, w_up, w_down):
    b, s, d = h.shape
    t = b * s
    xf = h.reshape(t, d)
    group_logits = (xf @ w_rg).astype(jnp.float32) + b_rg.astype(jnp.float32)
    group_prob = jax.nn.softmax(group_logits, axis=-1)
    grp = jnp.argmax(group_logits, axis=-1)
    p_grp = jnp.take_along_axis(group_prob, grp[:, None], axis=-1)
    expert_logits = ((xf @ w_re).astype(jnp.float32) + b_re.astype(jnp.float32)
                     ).reshape(t, N_EXPERT_GROUPS, EXPERTS_PER_GROUP)
    in_group = jnp.take_along_axis(expert_logits, grp[:, None, None], axis=1)[:, 0]
    top_logit, top_local = lax.top_k(in_group, TOP_K)
    gates = p_grp * jax.nn.softmax(top_logit, axis=-1)
    experts = grp[:, None] * EXPERTS_PER_GROUP + top_local

    a = t * TOP_K
    flat_e = experts.reshape(a)
    flat_tok = jnp.arange(a, dtype=jnp.int32) // TOP_K
    flat_g = gates.reshape(a)
    order = jnp.argsort(flat_e)
    e_sorted, tok_sorted, g_sorted = flat_e[order], flat_tok[order], flat_g[order]
    counts = jnp.bincount(flat_e, length=N_EXPERTS)
    starts = jnp.cumsum(counts) - counts
    padded = (counts + MOE_BLOCK - 1) // MOE_BLOCK * MOE_BLOCK
    padded_end = jnp.cumsum(padded)
    dest = (padded_end - padded)[e_sorted] + jnp.arange(a) - starts[e_sorted]
    n_blocks = -(-a // MOE_BLOCK) + N_EXPERTS
    cap = n_blocks * MOE_BLOCK
    slot_tok = jnp.zeros((cap,), jnp.int32).at[dest].set(tok_sorted)
    block_expert = jnp.minimum(
        jnp.searchsorted(padded_end, jnp.arange(n_blocks) * MOE_BLOCK, side='right'),
        N_EXPERTS - 1)
    x_slots = xf[slot_tok].reshape(n_blocks, MOE_BLOCK, d)

    def expert_block(args):
        xb, e = args
        return (jax.nn.silu(xb @ w_gate[e]) * (xb @ w_up[e])) @ w_down[e]

    y_slots = lax.map(expert_block, (x_slots, block_expert)).reshape(cap, d)
    y_assign = y_slots[dest] * g_sorted[:, None].astype(h.dtype)
    y = jax.ops.segment_sum(y_assign, tok_sorted, num_segments=t)
    return y.reshape(b, s, d)

def second_inputs(seed: int = 0) -> dict:
    key = jax.random.key(seed)
    ks = jax.random.split(key, 17)
    f32 = jnp.float32
    nrm = lambda k, shape, scale: jax.random.normal(k, shape, f32) * scale
    res_scale = (2.0 * DEPTH) ** -0.5
    return {
        "x": nrm(ks[0], (BATCH, SEQ, D_MODEL), 1.0),
        "norm_mix": 1.0 + nrm(ks[1], (DEPTH, D_MODEL), 0.02),
        "w_in": nrm(ks[2], (DEPTH, D_MODEL, IN_WIDTH), D_MODEL ** -0.5),
        "attn_sink": nrm(ks[3], (DEPTH, N_HEADS_2), 0.5),
        "conv_w": nrm(ks[4], (DEPTH, CONV_K, CONV_WIDTH), CONV_K ** -0.5),
        "norm_attn_out": 1.0 + nrm(ks[5], (DEPTH, ATTN_WIDTH), 0.02),
        "norm_conv_out": 1.0 + nrm(ks[6], (DEPTH, CONV_WIDTH), 0.02),
        "w_out": nrm(ks[7], (DEPTH, MIX_WIDTH, D_MODEL), MIX_WIDTH ** -0.5 * res_scale),
        "norm_ffn": 1.0 + nrm(ks[8], (DEPTH, D_MODEL), 0.02),
        "w_router_group": nrm(ks[9], (DEPTH, D_MODEL, N_EXPERT_GROUPS), D_MODEL ** -0.5),
        "b_router_group": nrm(ks[10], (DEPTH, N_EXPERT_GROUPS), 0.01),
        "w_router_expert": nrm(ks[11], (DEPTH, D_MODEL, N_EXPERTS), D_MODEL ** -0.5),
        "b_router_expert": nrm(ks[12], (DEPTH, N_EXPERTS), 0.01),
        "w_expert_gate": nrm(ks[13], (DEPTH, N_EXPERTS, D_MODEL, D_EXPERT), D_MODEL ** -0.5),
        "w_expert_up": nrm(ks[14], (DEPTH, N_EXPERTS, D_MODEL, D_EXPERT), D_MODEL ** -0.5),
        "w_expert_down": nrm(ks[15], (DEPTH, N_EXPERTS, D_EXPERT, D_MODEL), D_EXPERT ** -0.5 * res_scale),
        "norm_final": 1.0 + nrm(ks[16], (D_MODEL,), 0.02),
    }

def second_block(x, norm_mix, w_in, attn_sink, conv_w, norm_attn_out, norm_conv_out, w_out,
              norm_ffn, w_router_group, b_router_group, w_router_expert, b_router_expert,
              w_expert_gate, w_expert_up, w_expert_down, norm_final):
    cos, sin = rope_tables(x.shape[1])
    for l in range(DEPTH):
        x = x + hybrid_mixer(rmsnorm(x, norm_mix[l]), w_in[l], attn_sink[l], conv_w[l],
                             norm_attn_out[l], norm_conv_out[l], w_out[l], cos, sin)
        x = x + hierarchical_moe(rmsnorm(x, norm_ffn[l]), w_router_group[l], b_router_group[l],
                                 w_router_expert[l], b_router_expert[l], w_expert_gate[l],
                                 w_expert_up[l], w_expert_down[l])
    return rmsnorm(x, norm_final)


def setup_inputs(seed=0):
    out = dict(first_inputs(seed))
    for name, value in second_inputs(seed + 1).items():
        if name != "x":
            out[name + "_2"] = value
    return out


def reference(
    x, p, rel_bias, norm_mix, norm_ffn, norm_ple, w_ffn_gate, w_ffn_up, w_ffn_down, w_ple_proj,
    w_ple_gate, w_in_ab, w_out_ab, qn_moba, kn_moba, qn_dil, kn_dil, w_in_nsa, w_out_nsa,
    qn_nsa, kn_cmp, kn_slc, kn_win, cmp_k_pos, cmp_k_w1, cmp_k_b1, cmp_k_w2, cmp_k_b2,
    cmp_v_pos, cmp_v_w1, cmp_v_b1, cmp_v_w2, cmp_v_b2, norm_mix_2, w_in_2, attn_sink_2,
    conv_w_2, norm_attn_out_2, norm_conv_out_2, w_out_2, norm_ffn_2, w_router_group_2,
    b_router_group_2, w_router_expert_2, b_router_expert_2, w_expert_gate_2, w_expert_up_2,
    w_expert_down_2, norm_final_2,
):
    x = first_block(
        x, p, rel_bias, norm_mix, norm_ffn, norm_ple, w_ffn_gate, w_ffn_up, w_ffn_down,
        w_ple_proj, w_ple_gate, w_in_ab, w_out_ab, qn_moba, kn_moba, qn_dil, kn_dil, w_in_nsa,
        w_out_nsa, qn_nsa, kn_cmp, kn_slc, kn_win, cmp_k_pos, cmp_k_w1, cmp_k_b1, cmp_k_w2,
        cmp_k_b2, cmp_v_pos, cmp_v_w1, cmp_v_b1, cmp_v_w2, cmp_v_b2,
    )
    return second_block(
        x, norm_mix_2, w_in_2, attn_sink_2, conv_w_2, norm_attn_out_2, norm_conv_out_2, w_out_2,
        norm_ffn_2, w_router_group_2, b_router_group_2, w_router_expert_2, b_router_expert_2,
        w_expert_gate_2, w_expert_up_2, w_expert_down_2, norm_final_2,
    )


_drawn_inputs = setup_inputs


def setup_inputs(seed=0):
    import zlib

    import numpy as np

    out = dict(_drawn_inputs(seed))
    spreads = {}
    factors = {'norm_mix': 5.418,
     'norm_ffn': 2.821,
     'norm_ple': 8.0,
     'qn_moba': 8.0,
     'kn_moba': 8.0,
     'qn_dil': 8.0,
     'kn_dil': 8.0,
     'qn_nsa': 8.0,
     'kn_cmp': 8.0,
     'kn_slc': 8.0,
     'kn_win': 8.0,
     'cmp_k_pos': 7.999,
     'cmp_k_b1': 8.0,
     'cmp_k_b2': 8.0,
     'cmp_v_b1': 8.0,
     'cmp_v_b2': 5.48,
     'attn_sink_2': 8.0,
     'norm_attn_out_2': 4.325,
     'norm_conv_out_2': 4.967,
     'norm_ffn_2': 3.546,
     'b_router_group_2': 5.258,
     'b_router_expert_2': 4.737,
     'norm_final_2': 2.731}
    for name, (base, spread) in spreads.items():
        noise = np.random.default_rng([zlib.crc32(name.encode()), seed]).standard_normal(out[name].shape)
        drawn = base * np.exp(spread * noise) if base else spread * noise
        out[name] = jnp.asarray(drawn.astype(out[name].dtype))
    for name, factor in factors.items():
        out[name] = (out[name] * factor).astype(out[name].dtype)
    return out
```

```python
from contextlib import ExitStack

import concourse.bass as bass
from concourse import mybir
import numpy as np

F32 = mybir.dt.float32
I32 = mybir.dt.int32
ALU = mybir.AluOpType
ACT = mybir.ActivationFunctionType
AX = mybir.AxisListType.X

P = 128
S = 256
NT = S // P
D = 1024
KC = D // P
HD = 64
NH = 16
F = 2816
FJ = F // P
BUCKETS = 32
NCMP = 15
CMP_LEN, CMP_STRIDE = 32, 16
NG = 4
HEADS2, KV2 = 8, 2
CW = 512
NE, NEG = 32, 4
DE = 512
W = 64
NS = 2 * S
NSP = NS + W
SLOTS = 6
EPS = 1e-6
OFF = -1.0e30
BIG = 3.0e38
WHY = "an expert's window starts below the end of its slots"
NB = 384
GELU = 0.7978845608028654

G_NORM = [0, 16, 32, 8, 24, 40, 48, 64, 56, 72]
G_ATT, G_CONV, G_CW, G_B1, PRM_ROWS = 80, 88, 96, 120, 122
H_POS, HEAD_ROWS = 8, 72
C_ID, C_TRI, C_I512, C_I32, C_I4, C_VALID, C_COS, C_SIN, C_W = 0, 128, 256, 768, 800, 804, 805, 821, 837


def view(ap, off, dims):
    return bass.AP(tensor=ap.tensor, offset=ap.offset + off, ap=[list(ap.ap[0])] + [list(d) for d in dims])


def build(nc, A, out):
    ctx = ExitStack()
    with ctx:
        def sb(name, shape, dt=F32):
            return ctx.enter_context(nc.sbuf_tensor(name, shape, dt))

        def sem(name):
            return ctx.enter_context(nc.semaphore(name))

        ring = sb("ring", [P, SLOTS, 4096])
        h = sb("h", [P, NT, D])
        xT = sb("xT", [P, KC, S])
        xs = sb("xs", [P, NT, D])
        band = sb("band", [P, NH, NB])
        qkv = sb("qkv", [P, 6144])
        qk = sb("qk", [P, 16, S])
        sbuf_s = sb("sbuf_s", [P, 4, S])
        sbuf_p = sb("sbuf_p", [P, 4, S])
        cst = sb("cst", [P, C_W])
        ones = sb("ones", [P, P])
        mhalf = sb("mhalf", [P, 64])
        gT = sb("gT", [P, PRM_ROWS])
        g2T = sb("g2T", [P, HEAD_ROWS])
        pT = sb("pT", [P, 2, 2, S])
        sink = sb("sink", [P, 2, 2, HEADS2])
        brt = sb("brt", [P, 2, NEG + NE])
        relb = sb("relb", [BUCKETS, NH])
        w2 = sb("w2", [P, 2, HD])
        b2 = sb("b2", [P, 2, HD])
        rms = sb("rms", [P, 256])
        NU = 32 + 96 + 16 + 16
        nmax = sb("nmax", [P, NU])
        den = sb("den", [P, NU])
        rec = sb("rec", [P, 4])
        esink = sb("esink", [P, 32])
        gates = sb("gates", [P, NT, 48])
        cmpk = sb("cmpk", [16, 2, NG, HD])
        cmpT = sb("cmpT", [P, NG, 16])
        tab = sb("tab", [1, 3 * NE], I32)
        pb = [ctx.enter_context(nc.psum_tensor(f"pb{i}", [P, 512], F32)) for i in range(8)]
        scr = nc.dram_tensor("scr", [2 * NH, 512], F32, kind="Internal").ap()

        def qkv_t(t):
            return qkv[:, 3072 * t:3072 * (t + 1)]

        ident = cst[:, C_ID:C_ID + P]
        tri = cst[:, C_TRI:C_TRI + P]
        prm = xT[:, 0, :].rearrange("p (a b) -> p a b", a=2)
        rowsP = sbuf_s[:, :, :]
        oneh = qk[0:BUCKETS, 0:2, :].rearrange("p a b -> p (a b)")
        tmask = qk[0:NH, 2:6, :].rearrange("p a b -> p (a b)")
        trow = qk[0:NH, 6:10, :].rearrange("p a b -> p (a b)")
        hT = qk[:, 0:4, :]
        th = sbuf_s[:, 0:2, :]
        ga = sbuf_s[:, 2:4, :]
        cmph = sbuf_p[:, 0:2, :].rearrange("p a (b c) -> p a b c", b=4)
        cmpd = sbuf_p[0:16, 2:4, :].rearrange("p a b -> p (a b)").rearrange("p (g t d) -> p g t d", g=NG, t=2)
        cT = qk[0:HD, 0:8, :]
        kv2cols = 768
        qkv2 = qkv[:, 0:NT * kv2cols].rearrange("p (t c) -> p t c", t=NT)
        gbT = qkv[:, 1536:2560]
        gcT = qkv[:, 2560:3584]
        cuT = qkv[:, 3584:3584 + 4 * (S + 2)].rearrange("p (c s) -> p c s", c=4)
        yT = qkv[:, 4616:5640]
        bflat = band[:, :, :].rearrange("p a b -> p (a b)")
        ysT = bflat[:, NB:NB + KC * NSP].rearrange("p (k s) -> p k s", k=KC)
        wr = bflat[:, 4992:4992 + 2 * KC * 36].rearrange("p (l k n) -> p l k n", l=2, k=KC)
        gfin = bflat[:, NB:NB + D]
        xsT = qkv[:, 0:KC * NSP].rearrange("p (k s) -> p k s", k=KC)
        gcombT = qkv[:, 4608:5632].rearrange("p (c s) -> p c s", c=4)
        eh = qkv[:, 5632:5888]
        eg = qkv[:, 5888:6144]
        ysort = qkv[:, 0:4096].rearrange("p (c d) -> p c d", c=4)
        sel = sbuf_s[:, :, :].rearrange("p a b -> p (a b)").rearrange("p (t s) -> p t s", t=NT)
        gsel = sbuf_p[:, :, :].rearrange("p a b -> p (a b)").rearrange("p (t s) -> p t s", t=NT)
        rt = qk[:, 0:8, :].rearrange("p a b -> p (a b)")
        gtmp = qk[:, 8:10, :].rearrange("p a b -> p (a b)")

        x_loaded = sem("x_loaded")
        par_loaded = sem("par_loaded")
        cst_loaded = sem("cst_loaded")
        rel_loaded = sem("rel_loaded")
        arrived = [sem(f"arrived{i}") for i in range(SLOTS)]
        set_ready, set_done, dve_set = sem("set_ready"), sem("set_done"), sem("dve_set")
        trow_done, scr_written, band_loaded = sem("trow_done"), sem("scr_written"), sem("band_loaded")
        wr_loaded, gfin_loaded = sem("wr_loaded"), sem("gfin_loaded")
        dch, ach, pch = sem("dve_chain"), sem("act_chain"), sem("pool_chain")
        sq_done, rstd_done, xs_ready = sem("sq_done"), sem("rstd_done"), sem("xs_ready")
        ss_done = sem("ss_done")
        tp_ready, xT_a, xT_v = sem("tp_ready"), sem("xT_a"), sem("xT_v")
        pj_ready, pj_a, pj_v = sem("pj_ready"), sem("pj_a"), sem("pj_v")
        op_ready, h_done = sem("op_ready"), sem("h_done")
        gu_ready, th_done, hT_done, dn_done = sem("gu_ready"), sem("th_done"), sem("hT_done"), sem("dn_done")
        ple_ready, ple_th = sem("ple_ready"), sem("ple_th")
        hsq, hss, qn_ready = sem("head_squares"), sem("head_sums"), sem("qn_ready")
        qt_ready, qt_a, qt_v = sem("qt_ready"), sem("qt_a"), sem("qt_v")
        s_ready, s_max, e_done = sem("s_ready"), sem("s_max"), sem("e_done")
        pt_ready, pt_done, o_ready, o_done = sem("pt_ready"), sem("pt_done"), sem("o_ready"), sem("o_done")
        cT_ready, cT_done, hid_ready, gel_in, gel_th, gel_done = (sem("cT_ready"), sem("cT_done"), sem("hid_ready"),
                                                                 sem("gel_in"), sem("gel_th"), sem("gel_done"))
        cmp_ready, cmpn_done, cmpT_ready, cmpT_done = (sem("cmp_ready"), sem("cmpn_done"), sem("cmpT_ready"),
                                                       sem("cmpT_done"))
        g_th, gate_done = sem("g_th"), sem("gate_done")
        cv_ready, gb_done, cu_done, y_done = sem("cv_ready"), sem("gb_done"), sem("cu_done"), sem("y_done")
        ysq_done, yss_ready, yss_done = sem("ysq_done"), sem("yss_ready"), sem("yss_done")
        on_ready = sem("on_ready")
        rt_ready, rt_e, rt_x, as_done, cnt_ready, cnt_done = (sem("rt_ready"), sem("rt_e"), sem("rt_x"),
                                                              sem("as_done"), sem("cnt_ready"), sem("cnt_done"))
        pos_ready, tab_done, sel_done = sem("pos_ready"), sem("tab_done"), sem("sel_done")
        ga_ready, xsT_a, xsT_v = sem("ga_ready"), sem("xsT_a"), sem("xsT_v")
        gct_ready, gct_done = sem("gct_ready"), sem("gct_done")
        eg_ready = [sem(f"eg_ready{i}") for i in range(2)]
        eth_done = [sem(f"eth_done{i}") for i in range(2)]
        eh_done = [sem(f"eh_done{i}") for i in range(2)]
        ey_ready = [sem(f"ey_ready{i}") for i in range(2)]
        ey_done = [sem(f"ey_done{i}") for i in range(2)]
        eg_done = [sem(f"eg_done{i}") for i in range(2)]
        at_ready, cx_done, yt_v, op_ready2 = sem("at_ready"), sem("cx_done"), sem("yt_v"), sem("op_ready2")
        e_released = sem("e_released")
        yt_ready, yt_done = sem("yt_ready"), sem("yt_done")
        out_ready, stored = sem("out_ready"), sem("stored")

        stream = []

        def slot(i):
            return ring[:, i % SLOTS, :]

        def arrival(i):
            return arrived[i % SLOTS], 16 * (i // SLOTS + 1)

        def kcols(w, c0, n):
            return w[:, c0:c0 + n].rearrange("(k p) n -> p k n", p=P)

        def add(src, shape, release, parts=P):
            i = len(stream)
            k, n = shape
            stream.append((slot(i)[0:parts, 0:k * n].rearrange("p (k n) -> p k n", k=k), src, release))
            return i

        def weights(i):
            return stream[i][0]

        PJ = []
        PJ_AT = {}

        def add_proj(layer, w, cols):
            PJ_AT[layer] = len(PJ)
            for c0, n, dst in cols:
                g = len(PJ)
                PJ.append((add(kcols(w, c0, n), (KC, n), (pj_ready, 2 * g + 2)), n, dst))

        OPW, FFW, PLW, CMPW, CVW, EXP0 = {}, {}, {}, {}, {}, {}

        def add_out(k, w):
            OPW[k] = [add(kcols(w, 512 * c, 512), (KC, 512), (op_ready, 4 * k + 2 * c + 2)) for c in range(2)]

        def add_ffn(f):
            FFW[f] = []
            for g0 in range(0, FJ, 4):
                n = min(4, FJ - g0)
                last = FJ * f + g0 + n
                FFW[f].append((
                    add(kcols(A["w_ffn_gate"][f], g0 * P, n * P), (KC, n * P), (gu_ready, last)),
                    add(kcols(A["w_ffn_up"][f], g0 * P, n * P), (KC, n * P), (gu_ready, last)),
                    add(A["w_ffn_down"][f][g0 * P:(g0 + n) * P, :].rearrange("(k p) n -> p k n", p=P), (n, D),
                        (dn_done, last))))

        def add_ple(f):
            g0 = add(kcols(A["w_ple_gate"][f], 0, 512), (KC, 512), (ple_ready, 4 * f + 2))
            pr = add(A["w_ple_proj"][f].rearrange("(k p) n -> p k n", p=P), (2, D), (ple_ready, 4 * f + 4))
            g1 = add(kcols(A["w_ple_gate"][f], 512, 512), (KC, 512), (ple_ready, 4 * f + 4))
            PLW[f] = (g0, g1, pr)

        add_proj(0, A["w_in_ab"][0], [(512 * c, 512, 512 * c) for c in range(6)])
        add_out(0, A["w_out_ab"][0])
        add_ffn(0)
        add_ple(0)
        add_proj(1, A["w_in_nsa"][0], [(512 * c, 512, 512 * c) for c in range(5)] + [(2560, 48, 2560)])
        for kv, name in enumerate(("cmp_k_w1", "cmp_v_w1")):
            CMPW[kv] = add(A[name][0].rearrange("(l d) n -> d l n", d=HD), (CMP_LEN, P), (hid_ready, kv + 1), parts=HD)
        add_out(1, A["w_out_nsa"][0])
        add_ffn(1)
        add_ple(1)
        for l in range(2):
            add_proj(2 + l, A["w_in_2"][l], [(0, 512, 0), (512, 256, 512)])
            CVW[l] = [add(kcols(A["w_in_2"][l], 768 + 512 * c, 512), (KC, 512), (cv_ready, 6 * l + 2 * c + 2))
                      for c in range(3)]
            add_out(2 + l, A["w_out_2"][l])
            EXP0[l] = len(stream)
            for e in range(NE):
                for name in ("w_expert_gate_2", "w_expert_up_2"):
                    add(A[name][l, e].rearrange("(k p) n -> p k n", p=P), (KC, DE), (e_released, NE * l + e + 1))
                add(A["w_expert_down_2"][l, e].rearrange("(k p) n -> p k n", p=P), (DE // P, D),
                    (e_released, NE * l + e + 1))

        TP = [("norm", 0), ("attn", 0), ("norm", 1), ("norm", 2), ("norm", 3), ("attn", 1), ("norm", 4), ("norm", 5),
              ("norm", 6), ("attn2", 0), ("norm", 7), ("norm", 8), ("attn2", 1), ("norm", 9)]
        TPN = [8 if kind != "attn2" else 4 for kind, _ in TP]

        def tp_chunks(m):
            return sum(TPN[:m])

        def head_list(layer):
            z = []
            if layer == 0:
                for c in range(8):
                    z.append(([qkv_t(t)[:, (128 * c if c < 4 else 1024 + 128 * c):][:, 0:P] for t in range(NT)],
                              qk[:, c, :], 0 if c < 4 else 2))
                for c in range(8):
                    z.append(([qkv_t(t)[:, (512 + 128 * c if c < 4 else 1536 + 128 * c):][:, 0:P] for t in range(NT)],
                              qk[:, 8 + c, :], 1 if c < 4 else 3))
            elif layer == 1:
                for c in range(8):
                    z.append(([qkv_t(t)[:, 128 * c:128 * c + P] for t in range(NT)], qk[:, c, :], 4))
                for c in range(8):
                    z.append(([xs[:, t, 128 * c:128 * c + P] for t in range(NT)], qk[:, 8 + c, :], 5 + c // 4))
            else:
                for c in range(4):
                    z.append(([qkv2[:, t, 128 * c:128 * c + P] for t in range(NT)], qk[:, c, :], None))
                for c in range(KV2):
                    z.append(([xs[:, t, 128 * c:128 * c + P] for t in range(NT)], qk[:, 8 + c, :], None))
            return z

        QN = [4, 10, 4, 4]
        QT = [head_list(l) for l in range(4)]
        QT_AT = [sum(len(q) for q in QT[:l]) for l in range(5)]

        QT_V = [sum(2 * (len(q) // 4) for q in QT[:l]) for l in range(5)]
        QT_A = [QT_AT[l] - QT_V[l] for l in range(5)]

        class Unit:
            pass

        def unit_list(layer):
            us = []
            for hh in range(NH if layer < 2 else HEADS2):
                lo = HD * (hh % 2)
                for t in range(NT):
                    for br in range(3 if layer == 1 else 1):
                        u = Unit()
                        u.t, u.h, u.br, u.layer = t, hh, br, layer
                        u.q = qk[lo:lo + HD, hh // 2, P * t:P * (t + 1)]
                        u.nk = P * (t + 1) if layer < 2 else S
                        u.bias = view(band[:, hh if layer < 2 else 0, :], 255 + P * t, [[-1, u.nk]])
                        kt = range(u.nk // P)
                        if layer == 0:
                            u.k = qk[lo:lo + HD, 8 + hh // 2, 0:u.nk]
                            vc = 1024 + HD * hh if hh < 8 else 2560 + HD * (hh - 8)
                            u.v = [qkv_t(i)[:, vc:vc + HD] for i in kt]
                        elif layer == 1 and br < 2:
                            g = hh // (NH // NG)
                            u.k = qk[lo:lo + HD, 8 + 4 * br + g, 0:u.nk]
                            vc = (1792 if br == 0 else 2304) + HD * g
                            u.v = [qkv_t(i)[:, vc:vc + HD] for i in kt]
                        elif layer == 1:
                            g = hh // (NH // NG)
                            u.nk = NCMP
                            u.k = cmpT[lo:lo + HD, g, 0:NCMP]
                            u.bias = view(band[:, hh, :], 224 + P * t, [[-CMP_STRIDE, NCMP]])
                            u.v = [cmpk[0:NCMP, 1, g, :]]
                        else:
                            g = hh // (HEADS2 // KV2)
                            u.k = qk[lo:lo + HD, 8 + g, 0:u.nk]
                            u.v = [qkv2[:, i, 640 + HD * g:640 + HD * (g + 1)] for i in kt]
                        u.o = xs[:, t, HD * hh:HD * (hh + 1)]
                        us.append(u)
            return us

        UN = [unit_list(l) for l in range(4)]
        U_AT = [sum(len(u) for u in UN[:l]) for l in range(5)]

        R_NORM = [2 * n for n in range(11)]
        R_HEAD = {0: 22, 1: 86}
        R_CMP = 134
        R_ATT = [138, 142]
        R_CONV = [140, 144]
        ROOTS, ROOT_AT = [], {}

        def root(key, wait, col, n, width, parts=P):
            ROOT_AT[key] = len(ROOTS) + 1
            ROOTS.append((wait, col, n, parts, width))

        root(("norm", 0), (sq_done, 2), R_NORM[0], 2, D)
        root(("head", 0), (hss, 4), R_HEAD[0], 64, HD)
        for n in range(1, 4):
            root(("norm", n), (sq_done, 2 * n + 2), R_NORM[n], 2, D)
        root("cmp", (ss_done, 1), R_CMP, 4, HD, NCMP)
        root(("head", 1), (hss, 8), R_HEAD[1], 48, HD)
        for n in range(4, 7):
            root(("norm", n), (sq_done, 2 * n + 2), R_NORM[n], 2, D)
        root(("conv", 0), (yss_done, 1), R_CONV[0], 2, CW)
        root(("att", 0), (on_ready, 2), R_ATT[0], 2, CW)
        for n in range(7, 9):
            root(("norm", n), (sq_done, 2 * n + 2), R_NORM[n], 2, D)
        root(("conv", 1), (yss_done, 2), R_CONV[1], 2, CW)
        root(("att", 1), (on_ready, 4), R_ATT[1], 2, CW)
        for n in range(9, 11):
            root(("norm", n), (sq_done, 2 * n + 2), R_NORM[n], 2, D)

        PARS = []

        def par(dst, src):
            PARS.append((dst, src))

        for r0, name in ((0, "norm_mix"), (16, "norm_ffn"), (32, "norm_ple"), (48, "norm_mix_2"), (64, "norm_ffn_2")):
            par(prm[r0:r0 + 16, 0, :], A[name].rearrange("l (k p) -> (l k) p", p=P))
        par(prm[G_ATT:G_ATT + 8, 0, :], A["norm_attn_out_2"].rearrange("l (k p) -> (l k) p", p=P))
        par(prm[G_CONV:G_CONV + 8, 0, :], A["norm_conv_out_2"].rearrange("l (k p) -> (l k) p", p=P))
        par(prm[G_CW:G_CW + 24, 0, :], A["conv_w_2"].rearrange("l j (k p) -> (l j k) p", p=P))
        for kv, name in enumerate(("cmp_k_b1", "cmp_v_b1")):
            par(prm[G_B1 + kv:G_B1 + kv + 1, 0, :], A[name])
        for half in range(2):
            cols = slice(HD * half, HD * (half + 1))
            for r, name in enumerate(("qn_moba", "kn_moba", "qn_dil", "kn_dil", "qn_nsa", "kn_slc", "kn_win", "kn_cmp")):
                par(prm[r:r + 1, 1, cols], A[name])
            for kv, name in enumerate(("cmp_k_pos", "cmp_v_pos")):
                par(prm[H_POS + 32 * kv:H_POS + 32 * (kv + 1), 1, cols], A[name][0])
        for l in range(2):
            par(sink[:, l, 0, :], A["attn_sink_2"][l:l + 1, :].broadcast_to([P, HEADS2]))
            par(brt[:, l, 0:NEG], A["b_router_group_2"][l:l + 1, :].broadcast_to([P, NEG]))
            par(brt[:, l, NEG:NEG + NE], A["b_router_expert_2"][l:l + 1, :].broadcast_to([P, NE]))
        for kv, c in enumerate("kv"):
            par(w2[:, kv, :], A[f"cmp_{c}_w2"][0])
            par(b2[:, kv, :], A[f"cmp_{c}_b2"].broadcast_to([P, HD]))

        block = ctx.enter_context(nc.Block())

        @block.sync
        def _(sp):
            sp.dma_start(h[:], A["x"][0].rearrange("(t p) d -> p t d", p=P)).then_inc(x_loaded, 16)

            def load(i):
                dst, src, _ = stream[i]
                if i >= SLOTS:
                    s, v = stream[i - SLOTS][2]
                    sp.wait_ge(s, v)
                sp.dma_start(dst, src).then_inc(arrival(i)[0], 16)

            def load_experts(l):
                for i in range(EXP0[l], EXP0[l] + SLOTS):
                    load(i)
                ws = [A[n][l] for n in ("w_expert_gate_2", "w_expert_up_2", "w_expert_down_2")]
                with sp.Fori(1, NE // 2) as it:
                    for q in range(2):
                        sp.wait_ge(e_released, it * 2 + (NE * l + q - 1))
                        for m in range(3):
                            i = EXP0[l] + 3 * q + m
                            src = ws[m][bass.ds(it * 2 + q, 1), :, :].rearrange("e (k p) n -> p (e k) n", p=P)
                            sp.dma_start(stream[i][0], src).then_inc(arrival(i)[0], 16)

            i = 0
            for l in range(2):
                while i < EXP0[l]:
                    load(i)
                    i += 1
                load_experts(l)
                i += 3 * NE
            sp.wait_ge(out_ready, 2)
            sp.dma_start(out[0].rearrange("(t p) d -> p t d", p=P), xs[:]).then_inc(stored, 16)
            sp.wait_ge(stored, 16)

        @block.gpsimd
        def _(pool):
            pool.wait_ge(trow_done, 2)
            for m in range(2):
                nc.gpsimd.dma_start(scr[NH * m:NH * (m + 1), :], trow[:, 512 * m:512 * (m + 1)]).then_inc(scr_written, 16)
            pool.wait_ge(scr_written, 32)

            def load_bands(h0, n, row):
                src = bass.AP(tensor=scr.tensor, offset=512 * row, ap=[[1, P], [512, n], [1, NB]])
                nc.gpsimd.dma_start(band[:, h0:h0 + n, :], src).then_inc(band_loaded, 16)

            load_bands(0, 8, 0)
            load_bands(8, 8, NH + 8)
            for r, (wait, col, n, parts, width) in enumerate(ROOTS):
                if r == ROOT_AT[("norm", 1)] - 1:
                    pool.wait_ge(s_max, U_AT[1])
                    load_bands(8, 8, 8)
                if r == ROOT_AT[("norm", 4)] - 1:
                    pool.wait_ge(s_max, U_AT[2])
                    wb = A["window_band"]
                    nc.gpsimd.dma_start(band[:, 0, :], bass.AP(tensor=wb.tensor, offset=0, ap=[[1, P], [1, NB]]))\
                        .then_inc(band_loaded, 16)
                    for l in range(2):
                        nc.gpsimd.dma_start(wr[:, l, :, 0:NEG], A["w_router_group_2"][l].rearrange(
                            "(k p) n -> p k n", p=P)).then_inc(wr_loaded, 16)
                        nc.gpsimd.dma_start(wr[:, l, :, NEG:], A["w_router_expert_2"][l].rearrange(
                            "(k p) n -> p k n", p=P)).then_inc(wr_loaded, 16)
                if r == ROOT_AT[("norm", 10)] - 1:
                    pool.wait_ge(yt_ready, 16)
                    nc.gpsimd.dma_start(gfin, A["norm_final_2"].rearrange("(a d) -> a d", a=1).broadcast_to([P, D]))\
                        .then_inc(gfin_loaded, 16)
                pool.wait_ge(*wait)
                a = rms[0:parts, col:col + n]
                nc.gpsimd.tensor_scalar(a, a, float(width * EPS), None, ALU.add).then_inc(pch, 1)
                pool.wait_ge(pch, r + 1)
                nc.gpsimd.tensor_tensor(a, a, mhalf[0:parts, 0:n], ALU.pow).then_inc(rstd_done, 1)

        @block.scalar
        def _(act):
            act.dma_start(cst[:], A["consts"]).then_inc(cst_loaded, 16)
            act.dma_start(rowsP, A["p"].rearrange("l a (t p) c -> p (l a t) c", p=P)).then_inc(cst_loaded, 16)
            act.dma_start(oneh, A["onehot"]).then_inc(rel_loaded, 16)
            act.dma_start(tmask, A["row_masks"]).then_inc(rel_loaded, 16)
            act.dma_start(relb[:], A["rel_bias"]).then_inc(rel_loaded, 16)
            for dst, src in PARS:
                act.dma_start(dst, src).then_inc(par_loaded, 16)

            def squares(n):
                if n:
                    act.wait_ge(h_done, 4 * n)
                else:
                    act.wait_ge(x_loaded, 16)
                for t in range(NT):
                    nc.scalar.activation(xs[:, t, :], h[:, t, :], ACT.Square,
                                         accum_out=rms[:, R_NORM[n] + t:R_NORM[n] + t + 1]).then_inc(sq_done, 1)

            def evac_tp(m):
                kind, n = TP[m]
                if m == 0:
                    act.wait_ge(set_done, 1)
                for c in [c for c in range(TPN[m]) if c // 2 % 2 == 0]:
                    act.wait_ge(tp_ready, (tp_chunks(m) + c) // 2 + 1)
                    src = pb[4 + c // 2][:, S * (c % 2):S * (c % 2 + 1)]
                    if kind == "attn":
                        i = nc.scalar.activation(xT[:, c, :], src, ACT.Copy)
                    else:
                        col = G_NORM[n] if kind == "norm" else G_ATT + 4 * n
                        i = nc.scalar.activation(xT[:, c, :], src, ACT.Copy, scale=gT[:, col + c:col + c + 1])
                    i.then_inc(xT_a, 1)

            def evac_proj(layer, hi):
                for g in range(PJ_AT[layer], hi):
                    _, n, dst = PJ[g]
                    act.wait_ge(pj_ready, 2 * g + 1)
                    d = qkv_t(0)[:, dst:dst + n] if layer < 2 else qkv2[:, 0, dst:dst + n]
                    nc.scalar.activation(d, pb[(2 * g) % 4][:, 0:n], ACT.Copy).then_inc(pj_a, 1)

            def head_squares(layer):
                act.wait_ge(pj_a, PJ_AT[layer + 1])
                act.wait_ge(pj_v, PJ_AT[layer + 1])
                for t in range(NT):
                    for part in range(2):
                        if t:
                            act.wait_ge(hss, 4 * layer + part + 1)
                        if layer == 0:
                            src, dst = qkv_t(t)[:, 1536 * part:1536 * part + D], xs[:, part, :]
                        elif part == 0:
                            src, dst = qkv_t(t)[:, 0:D], xs[:, 0, :]
                        else:
                            src = qkv_t(t)[:, 1536:2560].rearrange("p (b c) -> p b c", b=2)[:, :, 0:256]
                            dst = xs[:, 1, 0:512].rearrange("p (b c) -> p b c", b=2)
                        nc.scalar.activation(dst, src, ACT.Square).then_inc(hsq, 1)

            def evac_heads(layer):
                for z, (_, dst, gain) in enumerate(QT[layer]):
                    g = QT_AT[layer] + z
                    if z // 2 % 2 == 0:
                        act.wait_ge(qt_ready, g // 2 + 1)
                        src = pb[4 + (z // 2) % 4][:, S * (z % 2):S * (z % 2 + 1)]
                        if gain is None:
                            i = nc.scalar.activation(dst, src, ACT.Copy)
                        else:
                            i = nc.scalar.activation(dst, src, ACT.Copy, scale=g2T[:, gain:gain + 1])
                        i.then_inc(qt_a, 1)

            def attention(layer):
                us = UN[layer]
                for i in range(len(us) + 1):
                    if i < len(us):
                        u, g = us[i], U_AT[layer] + i
                        act.wait_ge(s_max, g + 1)
                        if layer >= 2:
                            c = U_AT[2]
                            nc.scalar.activation(esink[:, g - c:g - c + 1], sink[:, layer - 2, 0, u.h:u.h + 1], ACT.Exp,
                                                 bias=nmax[:, g:g + 1])
                        s = sbuf_s[:, g % 4, 0:u.nk]
                        nc.scalar.activation(s, s, ACT.Exp, scale=-1.0, bias=nmax[:, g:g + 1],
                                             accum_out=den[:, g:g + 1]).then_inc(e_done, 1)
                    if i >= 1:
                        u, g = us[i - 1], U_AT[layer] + i - 1
                        act.wait_ge(pt_ready, g + 1)
                        if g >= 4:
                            act.wait_ge(o_ready, g - 3)
                        n, kp = (P * len(u.v), P) if u.nk > NCMP else (P, NCMP)
                        nc.scalar.activation(
                            sbuf_p[0:kp, g % 4, 0:n], pb[2 + g % 2][0:kp, 0:n], ACT.Copy).then_inc(pt_done, 1)

            def ffn(f):
                for j in range(FJ):
                    g = FJ * f + j
                    act.wait_ge(gu_ready, g + 1)
                    if g >= 2:
                        act.wait_ge(hT_done, g - 1)
                    nc.scalar.activation(th[:, g % 2, :], pb[4 + g % 4][:, 0:S], ACT.Tanh, scale=0.5).then_inc(th_done, 1)

            def ple(f):
                for c in range(2):
                    for t in range(NT):
                        act.wait_ge(ple_ready, 4 * f + 2 * c + t + 1)
                        nc.scalar.activation(xs[:, t, 512 * c:512 * (c + 1)], pb[2 * c + t][:], ACT.Tanh,
                                             scale=0.5).then_inc(ple_th, 1)

            def conv(l):
                for c in range(4):
                    act.wait_ge(cv_ready, 6 * l + c + 1)
                    dst = (gbT if c < 2 else gcT)[:, 512 * (c % 2):512 * (c % 2 + 1)]
                    nc.scalar.activation(dst, pb[4 + c][:], ACT.Copy).then_inc(gb_done, 1)
                act.wait_ge(y_done, l + 1)
                nc.scalar.activation(gcT, yT, ACT.Square).then_inc(ysq_done, 1)

            def moe(l):
                squares(7 + 2 * l)
                evac_tp(10 + 3 * l)
                act.wait_ge(rt_x, 2 * l + 1)
                nc.scalar.activation(rt[:, 112:120], rt[:, 112:120], ACT.Exp).then_inc(rt_e, 1)
                act.wait_ge(rt_x, 2 * l + 2)
                nc.scalar.activation(rt[:, 364:366], rt[:, 364:366], ACT.Exp).then_inc(rt_e, 1)
                col = G_NORM[7 + 2 * l]
                for k in range(0, KC, 2):
                    act.wait_ge(ga_ready, KC * l + k + 1)
                    nc.scalar.activation(xsT[:, k, 0:NS], pb[4 + k % 4][:], ACT.Copy,
                                         scale=gT[:, col + k:col + k + 1]).then_inc(xsT_a, 1)
                with act.Fori(0, NE) as e:
                    n = act.value_load(tab[0:1, bass.ds(e + 2 * NE, 1)], min_val=1, max_val=4)
                    w0 = act.value_load(tab[0:1, bass.ds(e + NE, 1)], min_val=0, max_val=4 * NE)
                    s0 = act.value_load(tab[0:1, bass.ds(e, 1)], min_val=0, max_val=NS)
                    with act.Fori(0, n) as k:
                        act.wait_ge(eg_ready[l], w0 + k + 1)
                        nc.scalar.activation(eg, pb[0][:, 0:S], ACT.Tanh, scale=0.5).then_inc(eth_done[l], 1)
                        act.wait_ge(ey_ready[l], w0 + k + 1)
                        nc.scalar.activation(ysT[:, :, bass.ds(nc.s_assert_within(s0 + k * W, 0, NS, skip_runtime_bounds_check_because=WHY), W)],
                                             pb[2][:].rearrange("p (k s) -> p k s", k=KC), ACT.Copy)\
                            .then_inc(ey_done[l], 1)
                for i in range(0, 8, 2):
                    act.wait_ge(yt_ready, 8 * l + i + 1)
                    nc.scalar.activation(ysort[:, i // 2, 0:512], pb[4 + i % 4][:], ACT.Copy).then_inc(yt_done, 1)

            squares(0)
            evac_tp(0)
            act.wait_ge(scr_written, 32)
            evac_proj(0, PJ_AT[1])
            head_squares(0)
            evac_heads(0)
            act.wait_ge(band_loaded, 32)
            attention(0)
            evac_tp(1)
            squares(1)
            evac_tp(2)
            ffn(0)
            squares(2)
            evac_tp(3)
            ple(0)
            squares(3)
            evac_tp(4)
            evac_proj(1, PJ_AT[2])
            for kv in range(2):
                act.wait_ge(gel_in, kv + 1)
                nc.scalar.activation(cmph[:, kv, 2, 0:60], cmph[:, kv, 1, 0:60], ACT.Tanh, scale=GELU).then_inc(gel_th, 1)
            head_squares(1)
            evac_heads(1)
            for t in range(NT):
                nc.scalar.activation(gates[:, t, :], qkv_t(t)[:, 2560:2608], ACT.Tanh, scale=0.5).then_inc(g_th, 1)
            attention(1)
            evac_tp(5)
            squares(4)
            evac_tp(6)
            ffn(1)
            squares(5)
            evac_tp(7)
            ple(1)
            for l in range(2):
                squares(6 + 2 * l)
                evac_tp(8 + 3 * l)
                evac_proj(2 + l, PJ_AT[2 + l] + 2)
                conv(l)
                evac_heads(2 + l)
                attention(2 + l)
                for t in range(NT):
                    act.wait_ge(o_done, U_AT[3 + l])
                    nc.scalar.activation(sbuf_s[:, 2 * t:2 * t + 2, :], xs[:, t, 0:CW].rearrange("p (a b) -> p a b", a=2),
                                         ACT.Square, accum_out=rms[:, R_ATT[l] + t:R_ATT[l] + t + 1]).then_inc(on_ready, 1)
                evac_tp(9 + 3 * l)
                moe(l)
            squares(10)

        @block.tensor
        def _(pe):
            mm = nc.tensor.matmul
            pe.wait_ge(cst_loaded, 32)
            pe.wait_ge(rel_loaded, 48)
            pe.wait_ge(par_loaded, 16 * len(PARS))
            mm(pb[1][0:NH, :], relb[:], oneh, start=True, stop=True).then_inc(set_ready, 1)
            nc.tensor.transpose(pb[0][:, 0:PRM_ROWS], prm[0:PRM_ROWS, 0, :], ident[0:PRM_ROWS, 0:PRM_ROWS])
            nc.tensor.transpose(pb[0][:, 128:128 + HEAD_ROWS], prm[0:HEAD_ROWS, 1, :], ident[0:HEAD_ROWS, 0:HEAD_ROWS])\
                .then_inc(set_ready, 1)
            for l in range(2):
                for k in range(2):
                    for t in range(NT):
                        i = nc.tensor.transpose(pb[2 + l][:, S * k + P * t:S * k + P * (t + 1)],
                                                rowsP[:, 2 * l + t, P * k:P * (k + 1)], ident)
            i.then_inc(set_ready, 1)

            def transposes(m):
                kind, n = TP[m]
                if kind == "norm":
                    pe.wait_ge(xs_ready, 2 * n + 2)
                elif kind == "attn":
                    pe.wait_ge(o_done, U_AT[n + 1])
                else:
                    pe.wait_ge(at_ready, 2 * n + 2)
                for c in range(TPN[m]):
                    b = pb[4 + c // 2]
                    for t in range(NT):
                        i = nc.tensor.transpose(b[:, S * (c % 2) + P * t:S * (c % 2) + P * (t + 1)],
                                                xs[:, t, P * c:P * (c + 1)], ident)
                    if c % 2:
                        i.then_inc(tp_ready, 1)

            def wait_xT(m):
                pe.wait_ge(xT_a, (tp_chunks(m + 1)) // 2)
                pe.wait_ge(xT_v, (tp_chunks(m + 1)) // 2)

            def project(layer, m):
                wait_xT(m)
                if layer == 0:
                    pe.wait_ge(set_done, 3)
                for g in range(PJ_AT[layer], PJ_AT[layer] + (6 if layer < 2 else 2)):
                    i, n, _ = PJ[g]
                    pe.wait_ge(*arrival(i))
                    for t in range(NT):
                        if g >= 2:
                            pe.wait_ge(pj_v if t else pj_a, g - 1)
                        for k in range(KC):
                            ins = mm(pb[(2 * g + t) % 4][:, 0:n], xT[:, k, P * t:P * (t + 1)], weights(i)[:, k, :],
                                     start=(k == 0), stop=(k == KC - 1))
                        ins.then_inc(pj_ready, 1)

            def heads(layer):
                for z, (src, _, _) in enumerate(QT[layer]):
                    if z in (0, 8) and layer < 2 or z == 0:
                        pe.wait_ge(qn_ready, sum(QN[:layer]) + QN[layer])
                    if z >= 8 and z % 2 == 0:
                        if z // 2 % 2 == 0:
                            pe.wait_ge(qt_a, QT_A[layer] + z // 2 - 2)
                        else:
                            pe.wait_ge(qt_v, QT_V[layer] + z // 2 - 3)
                    b = pb[4 + (z // 2) % 4]
                    for t in range(NT):
                        i = nc.tensor.transpose(b[:, S * (z % 2) + P * t:S * (z % 2) + P * (t + 1)], src[t], ident)
                    if z % 2:
                        i.then_inc(qt_ready, 1)

            def attention(layer):
                us = UN[layer]
                pe.wait_ge(qt_a, QT_A[layer + 1])
                pe.wait_ge(qt_v, QT_V[layer + 1])
                if layer == 1:
                    pe.wait_ge(cmpT_done, 1)
                n = len(us)
                for i in range(n + 3):
                    if i < n:
                        u, g = us[i], U_AT[layer] + i
                        if g >= 3:
                            pe.wait_ge(s_max, g - 2)
                        mm(pb[4 + g % 3][:, 0:u.nk], u.q, u.k, start=True, stop=True).then_inc(s_ready, 1)
                    if 0 <= i - 2 < n:
                        u, g = us[i - 2], U_AT[layer] + i - 2
                        pe.wait_ge(e_done, g + 1)
                        if g >= 2:
                            pe.wait_ge(pt_done, g - 1)
                        if u.nk == NCMP:
                            ins = nc.tensor.transpose(pb[2 + g % 2][0:NCMP, 0:P], sbuf_s[:, g % 4, 0:NCMP], ident)
                        else:
                            for kt in range(len(u.v)):
                                ins = nc.tensor.transpose(pb[2 + g % 2][:, P * kt:P * (kt + 1)],
                                                          sbuf_s[:, g % 4, P * kt:P * (kt + 1)], ident)
                        ins.then_inc(pt_ready, 1)
                    if 0 <= i - 3 < n:
                        u, g = us[i - 3], U_AT[layer] + i - 3
                        pe.wait_ge(pt_done, g + 1)
                        if g >= 2:
                            pe.wait_ge(o_done, g - 1)
                        ob = pb[g % 2][:, 0:HD]
                        kp = P if u.nk > NCMP else NCMP
                        for kt in range(len(u.v)):
                            ins = mm(ob, sbuf_p[0:kp, g % 4, P * kt:P * (kt + 1)], u.v[kt],
                                     start=(kt == 0), stop=(kt == len(u.v) - 1))
                        ins.then_inc(o_ready, 1)

            def out_proj(k, m):
                wait_xT(m)
                if k >= 2:
                    pe.wait_ge(cx_done, 4 * (k - 1))
                for c in range(2):
                    pe.wait_ge(*arrival(OPW[k][c]))
                    w = weights(OPW[k][c])
                    for t in range(NT):
                        for kk in range(KC):
                            half = kk // 4 if k >= 2 else 0
                            b = pb[2 * c + t + 4 * half]
                            ins = mm(b[:], xT[:, kk, P * t:P * (t + 1)], w[:, kk, :],
                                     start=(kk == 0 or (k >= 2 and kk == 4)),
                                     stop=(kk == KC - 1 or (k >= 2 and kk == 3)))
                        ins.then_inc(op_ready, 1)

            def ffn(f, m):
                wait_xT(m)

                def down(j):
                    g = FJ * f + j
                    if j % 4 == 0:
                        pe.wait_ge(*arrival(FFW[f][j // 4][2]))
                    pe.wait_ge(hT_done, g + 1)
                    wd = weights(FFW[f][j // 4][2])
                    for t in range(NT):
                        for c in range(2):
                            ins = mm(pb[2 * c + t][:], hT[:, g % 4, P * t:P * (t + 1)],
                                     wd[:, j % 4, 512 * c:512 * (c + 1)], start=(j == 0), stop=(j == FJ - 1))
                    ins.then_inc(dn_done, 1)

                for j in range(FJ):
                    g = FJ * f + j
                    if j % 4 == 0:
                        pe.wait_ge(*arrival(FFW[f][j // 4][0]))
                        pe.wait_ge(*arrival(FFW[f][j // 4][1]))
                    if g >= 4:
                        pe.wait_ge(hT_done, g - 3)
                    for half in range(2):
                        wg = weights(FFW[f][j // 4][half])
                        for k in range(KC):
                            ins = mm(pb[4 + g % 4][:, S * half:S * (half + 1)], wg[:, k, P * (j % 4):P * (j % 4 + 1)],
                                     xT[:, k, :], start=(k == 0), stop=(k == KC - 1))
                    ins.then_inc(gu_ready, 1)
                    if j:
                        down(j - 1)
                down(FJ - 1)

            def ple(f, m):
                wait_xT(m)
                g0, g1, pr = PLW[f]
                pe.wait_ge(*arrival(pr))
                for c in range(2):
                    pe.wait_ge(*arrival((g0, g1)[c]))
                    for t in range(NT):
                        for k in range(KC):
                            mm(pb[2 * c + t][:], xT[:, k, P * t:P * (t + 1)], weights((g0, g1)[c])[:, k, :],
                               start=(k == 0), stop=(k == KC - 1))
                        for k in range(2):
                            ins = mm(pb[4 + 2 * c + t][:], pT[:, f, k, P * t:P * (t + 1)],
                                     weights(pr)[:, k, 512 * c:512 * (c + 1)], start=(k == 0), stop=(k == 1))
                        ins.then_inc(ple_ready, 1)

            def compress():
                pe.wait_ge(pj_a, PJ_AT[2])
                pe.wait_ge(pj_v, PJ_AT[2])
                for kv in range(2):
                    for g in range(NG):
                        b = pb[4 + 2 * kv + g // 2]
                        for t in range(NT):
                            c0 = 1024 + 256 * kv + HD * g
                            ins = nc.tensor.transpose(b[0:HD, S * (g % 2) + P * t:S * (g % 2) + P * (t + 1)],
                                                      qkv_t(t)[:, c0:c0 + HD], ident)
                ins.then_inc(cT_ready, 1)
                pe.wait_ge(cT_done, 1)
                for kv in range(2):
                    pe.wait_ge(*arrival(CMPW[kv]))
                    w1 = weights(CMPW[kv])
                    for l in range(CMP_LEN):
                        mm(pb[kv][:, 0:60], w1[:, l, :], view(cT[:, 4 * kv, :], l, [[S, NG], [CMP_STRIDE, NCMP]]),
                           start=(l == 0), stop=(l == CMP_LEN - 1))
                    for l in range(CMP_LEN):
                        ins = mm(pb[kv][:, 64:65], w1[:, l, :], g2T[0:HD, H_POS + 32 * kv + l:H_POS + 32 * kv + l + 1],
                                 start=(l == 0), stop=(l == CMP_LEN - 1))
                    ins.then_inc(hid_ready, 1)
                for kv in range(2):
                    pe.wait_ge(gel_done, kv + 1)
                    for g in range(NG):
                        ins = mm(pb[2][0:NCMP, 256 * kv + HD * g:256 * kv + HD * (g + 1)],
                                 cmph[:, kv, 3, NCMP * g:NCMP * (g + 1)], w2[:, kv, :], start=True, stop=True)
                ins.then_inc(cmp_ready, 1)
                pe.wait_ge(cmpn_done, 2)
                for g in range(NG):
                    ins = nc.tensor.transpose(pb[3][:, 16 * g:16 * g + NCMP],
                                              cmpd[0:NCMP, g, :, :].rearrange("p a b -> p (a b)"), ident[0:NCMP, 0:NCMP])
                ins.then_inc(cmpT_ready, 1)

            def conv(l):
                for c in range(3):
                    pe.wait_ge(*arrival(CVW[l][c]))
                    w = weights(CVW[l][c])
                    for half in range(2):
                        if c == 2:
                            pe.wait_ge(gb_done, 4 * l + half + 1)
                        b = pb[4 + (2 * c + half) % 4]
                        for q in range(2):
                            cc = 2 * half + q
                            for k in range(KC):
                                ins = mm(b[:, S * q:S * (q + 1)], w[:, k, P * cc:P * (cc + 1)], xT[:, k, :],
                                         start=(k == 0), stop=(k == KC - 1))
                        ins.then_inc(cv_ready, 1)

            def conv_sums(l):
                pe.wait_ge(ysq_done, l + 1)
                for t in range(NT):
                    for c in range(4):
                        ins = mm(pb[7][:, t:t + 1], gcT[:, S * c + P * t:S * c + P * (t + 1)], ones[:, 0:1],
                                 start=(c == 0), stop=(c == 3))
                ins.then_inc(yss_ready, 1)

            def moe(l):
                transposes(10 + 3 * l)
                wait_xT(10 + 3 * l)
                pe.wait_ge(wr_loaded, 64)
                for t in range(NT):
                    for k in range(KC):
                        ins = mm(pb[0][:, 64 * t:64 * t + 36], xT[:, k, P * t:P * (t + 1)], wr[:, l, k, :],
                                 start=(k == 0), stop=(k == KC - 1))
                ins.then_inc(rt_ready, 1)
                a = [rt[:, 384 + NE * t:384 + NE * (t + 1)] for t in range(NT)]
                pe.wait_ge(as_done, l + 1)
                for t in range(NT):
                    ins = mm(pb[1][0:NE, 0:P], a[t], ones[:], start=(t == 0), stop=(t == 1))
                ins.then_inc(cnt_ready, 1)
                mm(pb[2][:, 0:NE], tri, a[0], start=True, stop=True)
                mm(pb[2][:, NE:2 * NE], ones[:], a[0], start=True, stop=False)
                mm(pb[2][:, NE:2 * NE], tri, a[1], start=False, stop=True)
                pe.wait_ge(cnt_done, 2 * l + 2)
                cm, wm = rt[0:NE, 512:640], rt[0:NE, 640:768]
                mm(pb[3][:, 0:NE], cm, tri[0:NE, 0:NE], start=True, stop=True)
                mm(pb[3][:, NE:2 * NE], wm, tri[0:NE, 0:NE], start=True, stop=True)
                mm(pb[3][:, 2 * NE:3 * NE], wm, ident[0:NE, 0:NE], start=True, stop=True)\
                    .then_inc(pos_ready, 1)
                pe.wait_ge(sel_done, 2 * l + 1)
                for k in range(KC):
                    if k >= 4:
                        if k % 2:
                            pe.wait_ge(xsT_v, 5 * l + 2 + (k - 4) // 2)
                        else:
                            pe.wait_ge(xsT_a, 4 * l + 1 + (k - 4) // 2)
                    for t in range(NT):
                        ins = mm(pb[4 + k % 4][:], xs[:, t, P * k:P * (k + 1)], sel[:, t, :],
                                 start=(t == 0), stop=(t == 1))
                    ins.then_inc(ga_ready, 1)
                pe.wait_ge(sel_done, 2 * l + 2)
                for c in range(4):
                    b = pb[c // 2]
                    for t in range(NT):
                        ins = nc.tensor.transpose(b[:, S * (c % 2) + P * t:S * (c % 2) + P * (t + 1)],
                                                  gsel[:, t, P * c:P * (c + 1)], ident)
                    if c % 2:
                        ins.then_inc(gct_ready, 1)
                pe.wait_ge(gct_done, 2 * l + 2)
                pe.wait_ge(xsT_a, (KC // 2) * (l + 1))
                pe.wait_ge(xsT_v, (KC // 2) * (l + 1) + l + 1)
                with pe.Fori(0, NE // 2) as it:
                    for q in range(2):
                        n = pe.value_load(tab[0:1, bass.ds(it * 2 + (q + 2 * NE), 1)], min_val=1, max_val=4)
                        w0 = pe.value_load(tab[0:1, bass.ds(it * 2 + (q + NE), 1)], min_val=0, max_val=4 * NE)
                        s0 = pe.value_load(tab[0:1, bass.ds(it * 2 + q, 1)], min_val=0, max_val=NS)
                        wg, wu, wd = (weights(EXP0[l] + 3 * q + m) for m in range(3))
                        ar = [arrival(EXP0[l] + 3 * q + m) for m in range(3)]
                        with pe.Fori(0, n) as k:
                            for half, w in enumerate((wg, wu)):
                                pe.wait_ge(ar[half][0], it * 16 + ar[half][1])
                                for j in range(DE // P):
                                    for kk in range(KC):
                                        ins = mm(pb[half][:, W * j:W * (j + 1)], w[:, kk, P * j:P * (j + 1)],
                                                 xsT[:, kk, bass.ds(nc.s_assert_within(s0 + k * W, 0, NS, skip_runtime_bounds_check_because=WHY), W)], start=(kk == 0), stop=(kk == KC - 1))
                            ins.then_inc(eg_ready[l], 1)
                            pe.wait_ge(ar[2][0], it * 16 + ar[2][1])
                            pe.wait_ge(eh_done[l], w0 + k + 1)
                            for c in range(KC):
                                for j in range(DE // P):
                                    ins = mm(pb[2][:, W * c:W * (c + 1)], wd[:, j, P * c:P * (c + 1)],
                                             eh[:, W * j:W * (j + 1)], start=(j == 0), stop=(j == DE // P - 1))
                            ins.then_inc(ey_ready[l], 1)
                            pe.wait_ge(ey_done[l], w0 + k + 1)
                        pe.sem_inc(e_released, 1)
                for c in range(4):
                    for half in range(2):
                        i = 2 * c + half
                        if i >= 4:
                            pe.wait_ge(yt_done if half == 0 else yt_v, 4 * l + (i - 4) // 2 + 1)
                        for kk in range(4):
                            ins = nc.tensor.transpose(pb[4 + i % 4][:, P * kk:P * (kk + 1)],
                                                      ysT[:, 4 * half + kk, P * c:P * (c + 1)], ident)
                        ins.then_inc(yt_ready, 1)
                pe.wait_ge(yt_done, 4 * l + 4)
                pe.wait_ge(yt_v, 4 * l + 4)
                for c in range(2):
                    for t in range(NT):
                        for sc in range(4):
                            ins = mm(pb[2 * c + t][:], gcombT[:, sc, P * t:P * (t + 1)], ysort[:, sc, 512 * c:512 * (c + 1)],
                                     start=(sc == 0), stop=(sc == 3))
                        ins.then_inc(op_ready2, 1)

            transposes(0)
            project(0, 0)
            heads(0)
            attention(0)
            transposes(1)
            out_proj(0, 1)
            transposes(2)
            ffn(0, 2)
            transposes(3)
            ple(0, 3)
            transposes(4)
            project(1, 4)
            compress()
            heads(1)
            attention(1)
            transposes(5)
            out_proj(1, 5)
            transposes(6)
            ffn(1, 6)
            transposes(7)
            ple(1, 7)
            for l in range(2):
                transposes(8 + 3 * l)
                project(2 + l, 8 + 3 * l)
                conv(l)
                conv_sums(l)
                heads(2 + l)
                attention(2 + l)
                transposes(9 + 3 * l)
                out_proj(2 + l, 9 + 3 * l)
                moe(l)

        @block.vector
        def _(dve):
            v = nc.vector
            chain = [0]

            def link(ins):
                chain[0] += 1
                ins.then_inc(dch, 1)
                dve.wait_ge(dch, chain[0])

            def root_wait(key):
                dve.wait_ge(rstd_done, ROOT_AT[key])

            def bc(ap, dims):
                return view(ap, 0, dims)

            link(v.memset(ones[:], 1.0))
            link(v.memset(mhalf[:], -0.5))
            dve.wait_ge(set_ready, 1)
            dve.wait_ge(rel_loaded, 48)
            for m in range(2):
                v.scalar_tensor_tensor(trow[:, 512 * m:512 * (m + 1)], pb[1][0:NH, :], 8.0, tmask[:, 512 * m:512 * (m + 1)],
                                       ALU.mult, ALU.add).then_inc(trow_done, 1)
            dve.wait_ge(set_ready, 2)
            link(v.tensor_copy(gT[:], pb[0][:, 0:PRM_ROWS]))
            link(v.tensor_scalar(g2T[:, 0:H_POS], pb[0][:, 128:128 + H_POS], 8.0, None, ALU.mult))
            v.tensor_copy(g2T[:, H_POS:], pb[0][:, 128 + H_POS:128 + HEAD_ROWS]).then_inc(set_done, 1)
            dve.wait_ge(set_done, 1)
            dve.wait_ge(set_ready, 3)
            for l in range(2):
                v.tensor_copy(pT[:, l, :, :], pb[2 + l][:].rearrange("p (k s) -> p k s", k=2)).then_inc(set_done, 1)
            dve.wait_ge(par_loaded, 16 * len(PARS))
            link(v.tensor_scalar(sink[:, :, 1, :], sink[:, :, 0, :], -1.0, None, ALU.mult))

            def normalise(n):
                root_wait(("norm", n))
                for t in range(NT):
                    v.tensor_scalar(xs[:, t, :], h[:, t, :], rms[:, R_NORM[n] + t:R_NORM[n] + t + 1], float(D ** 0.5),
                                    ALU.mult, ALU.mult).then_inc(xs_ready, 1)

            def evac_tp(m):
                kind, n = TP[m]
                for c in [c for c in range(TPN[m]) if c // 2 % 2]:
                    dve.wait_ge(tp_ready, (tp_chunks(m) + c) // 2 + 1)
                    src = pb[4 + c // 2][:, S * (c % 2):S * (c % 2 + 1)]
                    if kind == "attn":
                        i = v.tensor_copy(xT[:, c, :], src)
                    else:
                        col = G_NORM[n] if kind == "norm" else G_ATT + 4 * n
                        i = v.tensor_scalar(xT[:, c, :], src, gT[:, col + c:col + c + 1], None, ALU.mult)
                    i.then_inc(xT_v, 1)

            def evac_proj(layer, hi):
                for g in range(PJ_AT[layer], hi):
                    _, n, dst = PJ[g]
                    dve.wait_ge(pj_ready, 2 * g + 2)
                    d = qkv_t(1)[:, dst:dst + n] if layer < 2 else qkv2[:, 1, dst:dst + n]
                    v.tensor_copy(d, pb[(2 * g + 1) % 4][:, 0:n]).then_inc(pj_v, 1)

            def head_norms(layer):
                base = R_HEAD[layer]
                per = 32 if layer == 0 else 24
                for t in range(NT):
                    for part in range(2):
                        dve.wait_ge(hsq, 4 * layer + 2 * t + part + 1)
                        nh = 16 if layer == 0 or part == 0 else 8
                        c0 = base + per * t + 16 * part
                        v.tensor_reduce(rms[:, c0:c0 + nh], xs[:, part, 0:HD * nh].rearrange("p (a b) -> p a b", b=HD),
                                        AX, ALU.add).then_inc(hss, 1)
                root_wait(("head", layer))
                for t in range(NT):
                    r = rms[:, base + per * t:base + per * (t + 1)]
                    if layer == 0:
                        for part in range(2):
                            x = qkv_t(t)[:, 1536 * part:1536 * part + D].rearrange("p (a b) -> p a b", b=HD)
                            v.tensor_tensor(x, x, view(r, 16 * part, [[1, 16], [0, HD]]), ALU.mult).then_inc(qn_ready, 1)
                    else:
                        x = qkv_t(t)[:, 0:D].rearrange("p (a b) -> p a b", b=HD)
                        v.tensor_tensor(x, x, view(r, 0, [[1, 16], [0, HD]]), ALU.mult).then_inc(qn_ready, 1)
                        for br in range(2):
                            kx = view(qkv_t(t), 1536 + 512 * br, [[HD, NG], [1, HD]])
                            for twice in range(2):
                                v.tensor_tensor(view(xs[:, t, :], 512 * br + HD * twice, [[2 * HD, NG], [1, HD]]), kx,
                                                view(r, 16 + 4 * br, [[1, NG], [0, HD]]), ALU.mult).then_inc(qn_ready, 1)

            def evac_heads(layer):
                for z, (_, dst, gain) in enumerate(QT[layer]):
                    if z // 2 % 2:
                        dve.wait_ge(qt_ready, (QT_AT[layer] + z) // 2 + 1)
                        src = pb[4 + (z // 2) % 4][:, S * (z % 2):S * (z % 2 + 1)]
                        if gain is None:
                            i = v.tensor_copy(dst, src)
                        else:
                            i = v.tensor_scalar(dst, src, g2T[:, gain:gain + 1], None, ALU.mult)
                        i.then_inc(qt_v, 1)

            def attention(layer):
                us = UN[layer]
                n = len(us)
                dve.wait_ge(band_loaded, (32, 48, 64, 64)[layer])
                for i in range(n + 4):
                    if i < n:
                        u, g = us[i], U_AT[layer] + i
                        dve.wait_ge(s_ready, g + 1)
                        if g >= 4:
                            dve.wait_ge(pt_ready, g - 3)
                        init = BIG if layer < 2 else sink[:, layer - 2, 1, u.h:u.h + 1]
                        v.tensor_tensor_reduce(sbuf_s[:, g % 4, 0:u.nk], pb[4 + g % 3][:, 0:u.nk], u.bias, -0.125, init,
                                               ALU.add, ALU.min, nmax[:, g:g + 1]).then_inc(s_max, 1)
                    if i >= 4:
                        u, g = us[i - 4], U_AT[layer] + i - 4
                        dve.wait_ge(e_done, g + 1)
                        r = rec[:, g % 4:g % 4 + 1]
                        if layer >= 2:
                            c = g - U_AT[2]
                            link(v.tensor_tensor(den[:, g:g + 1], den[:, g:g + 1], esink[:, c:c + 1], ALU.add))
                        link(v.reciprocal(r, den[:, g:g + 1]))
                        ob = pb[g % 2][:, 0:HD]
                        dve.wait_ge(o_ready, g + 1)
                        if layer != 1:
                            v.tensor_scalar(u.o, ob, r, None, ALU.mult).then_inc(o_done, 1)
                            continue
                        gate = gates[:, u.t, 3 * u.h + (1, 2, 0)[u.br]:][:, 0:1]
                        if u.br == 0:
                            v.tensor_scalar(u.o, ob, r, gate, ALU.mult, ALU.mult).then_inc(o_done, 1)
                        else:
                            link(v.tensor_tensor(r, r, gate, ALU.mult))
                            dve.wait_ge(o_done, g)
                            v.scalar_tensor_tensor(u.o, ob, r, u.o, ALU.mult, ALU.add).then_inc(o_done, 1)

            def residual(ready, first):
                for c in range(2):
                    for t in range(NT):
                        dve.wait_ge(ready, first + 2 * c + t + 1)
                        hh = h[:, t, 512 * c:512 * (c + 1)]
                        v.tensor_tensor(hh, hh, pb[2 * c + t][:], ALU.add).then_inc(h_done, 1)

            def ffn(f):
                for j in range(FJ):
                    g = FJ * f + j
                    b = pb[4 + g % 4]
                    dve.wait_ge(th_done, g + 1)
                    link(v.scalar_tensor_tensor(ga[:, g % 2, :], th[:, g % 2, :], 1.0, b[:, 0:S], ALU.add, ALU.mult))
                    if g >= 4:
                        dve.wait_ge(dn_done, g - 3)
                    v.scalar_tensor_tensor(hT[:, g % 4, :], ga[:, g % 2, :], 0.5, b[:, S:2 * S], ALU.mult, ALU.mult)\
                        .then_inc(hT_done, 1)
                dve.wait_ge(dn_done, FJ * (f + 1))
                for c in range(2):
                    for t in range(NT):
                        hh = h[:, t, 512 * c:512 * (c + 1)]
                        v.tensor_tensor(hh, hh, pb[2 * c + t][:], ALU.add).then_inc(h_done, 1)

            def ple(f):
                for c in range(2):
                    for t in range(NT):
                        dve.wait_ge(ple_th, 4 * f + 2 * c + t + 1)
                        x = xs[:, t, 512 * c:512 * (c + 1)]
                        hh = h[:, t, 512 * c:512 * (c + 1)]
                        link(v.scalar_tensor_tensor(x, x, 1.0, pb[4 + 2 * c + t][:], ALU.add, ALU.mult))
                        v.scalar_tensor_tensor(hh, x, 0.5, hh, ALU.mult, ALU.add).then_inc(h_done, 1)

            def compress():
                dve.wait_ge(cT_ready, 1)
                for kv in range(2):
                    for half in range(2):
                        i = v.tensor_copy(cT[:, 4 * kv + 2 * half:4 * kv + 2 * half + 2, :],
                                          pb[4 + 2 * kv + half][0:HD, :].rearrange("p (a b) -> p a b", a=2))
                        if kv * half == 0:
                            link(i)
                i.then_inc(cT_done, 1)
                x = [cmph[:, kv, 0, 0:60] for kv in range(2)]
                for kv in range(2):
                    dve.wait_ge(hid_ready, kv + 1)
                    hb = cmph[:, kv, 0, 60:61]
                    link(v.tensor_tensor(hb, pb[kv][:, 64:65], gT[:, G_B1 + kv:G_B1 + kv + 1], ALU.add))
                    link(v.tensor_scalar(x[kv], pb[kv][:, 0:60], hb, None, ALU.add))
                    y = cmph[:, kv, 1, 0:60]
                    link(v.tensor_tensor(y, x[kv], x[kv], ALU.mult))
                    link(v.tensor_scalar(y, y, 0.044715, 1.0, ALU.mult, ALU.add))
                    v.tensor_tensor(y, y, x[kv], ALU.mult).then_inc(gel_in, 1)
                for kv in range(2):
                    dve.wait_ge(gel_th, kv + 1)
                    v.scalar_tensor_tensor(cmph[:, kv, 3, 0:60], cmph[:, kv, 2, 0:60], 1.0, x[kv], ALU.add, ALU.mult)\
                        .then_inc(gel_done, 1)
                dve.wait_ge(cmp_ready, 1)
                for kv in range(2):
                    link(v.scalar_tensor_tensor(cmpk[0:NCMP, kv, :, :], pb[2][0:NCMP, 256 * kv:256 * (kv + 1)].rearrange(
                        "p (g d) -> p g d", g=NG), 0.5, view(b2[0:NCMP, kv, :], 0, [[0, NG], [1, HD]]), ALU.mult, ALU.add))
                link(v.tensor_tensor(cmpd[0:NCMP, :, 0, :], cmpk[0:NCMP, 0, :, :], cmpk[0:NCMP, 0, :, :], ALU.mult))
                v.tensor_reduce(rms[0:NCMP, R_CMP:R_CMP + 4], cmpd[0:NCMP, :, 0, :], AX, ALU.add).then_inc(ss_done, 1)
                root_wait("cmp")
                for twice in range(2):
                    v.tensor_tensor(cmpd[0:NCMP, :, twice, :], cmpk[0:NCMP, 0, :, :],
                                    view(rms[0:NCMP, R_CMP:R_CMP + 4], 0, [[1, NG], [0, HD]]), ALU.mult).then_inc(cmpn_done, 1)
                dve.wait_ge(cmpT_ready, 1)
                v.tensor_scalar(cmpT[:, :, 0:NCMP], pb[3][:, 0:64].rearrange("p (g c) -> p g c", g=NG)[:, :, 0:NCMP],
                                g2T[:, 7:8], None, ALU.mult).then_inc(cmpT_done, 1)

            def nsa_gates():
                dve.wait_ge(g_th, 2)
                link(v.tensor_scalar(gates[:], gates[:], 0.5, 0.5, ALU.mult, ALU.add))
                g0 = view(gates[:, 0, :], 0, [[3, NH]])
                link(v.tensor_scalar(g0, g0, cst[:, C_VALID:C_VALID + 1], None, ALU.mult))

            def rope(l):
                dve.wait_ge(pj_a, PJ_AT[2 + l] + 2)
                dve.wait_ge(pj_v, PJ_AT[2 + l] + 2)
                nh = HEADS2 + KV2
                cos, sin = (cst[:, c:c + 16] for c in (C_COS, C_SIN))
                tmp = sbuf_p[:, :, :].rearrange("p a b -> p (a b)")
                for t in range(NT):
                    x1, x2 = (view(qkv2[:, t, :], o, [[HD, nh], [1, 8]]) for o in (0, 8))
                    cb, sbb = (view(a, 8 * t, [[0, nh], [1, 8]]) for a in (cos, sin))
                    k = [tmp[:, 80 * i:80 * (i + 1)].rearrange("p (a b) -> p a b", b=8) for i in range(4)]
                    v.tensor_tensor(k[0], x1, cb, ALU.mult)
                    v.tensor_tensor(k[1], x2, sbb, ALU.mult)
                    v.tensor_tensor(k[2], x2, cb, ALU.mult)
                    link(v.tensor_tensor(k[3], x1, sbb, ALU.mult))
                    v.tensor_tensor(x1, k[0], k[1], ALU.subtract)
                    link(v.tensor_tensor(x2, k[2], k[3], ALU.add))
                for t in range(NT):
                    for twice in range(2):
                        v.tensor_copy(view(xs[:, t, :], HD * twice, [[2 * HD, KV2], [1, HD]]),
                                      view(qkv2[:, t, :], 512, [[HD, KV2], [1, HD]])).then_inc(qn_ready, 1)

            def conv(l):
                v.memset(cuT[:, :, 0:1], 0.0)
                link(v.memset(cuT[:, :, S + 1:S + 2], 0.0))
                for half in range(2):
                    dve.wait_ge(cv_ready, 6 * l + 5 + half)
                    dve.wait_ge(gb_done, 4 * l + 4)
                    link(v.tensor_tensor(cuT[:, 2 * half:2 * half + 2, 1:S + 1],
                                         gcT[:, 512 * half:512 * (half + 1)].rearrange("p (a b) -> p a b", a=2),
                                         pb[4 + half][:].rearrange("p (a b) -> p a b", a=2), ALU.mult))
                for j in range(3):
                    for c in range(4):
                        y = yT[:, S * c:S * (c + 1)]
                        w = gT[:, G_CW + 12 * l + 4 * j + c:][:, 0:1]
                        x = cuT[:, c, j:j + S]
                        if j == 0:
                            i = v.tensor_scalar(y, x, w, None, ALU.mult)
                        else:
                            i = v.scalar_tensor_tensor(y, x, w, y, ALU.mult, ALU.add)
                    link(i)
                v.tensor_tensor(yT, yT, gbT, ALU.mult).then_inc(y_done, 1)
                dve.wait_ge(y_done, l + 1)
                for c in range(4):
                    v.tensor_scalar(xT[:, 4 + c, :], yT[:, S * c:S * (c + 1)], gT[:, G_CONV + 4 * l + c:][:, 0:1], None,
                                    ALU.mult).then_inc(cx_done, 1)
                dve.wait_ge(yss_ready, l + 1)
                v.tensor_copy(rms[:, R_CONV[l]:R_CONV[l] + 2], pb[7][:, 0:2]).then_inc(yss_done, 1)

            def attn_out(l):
                root_wait(("att", l))
                for t in range(NT):
                    x = xs[:, t, 0:CW]
                    v.tensor_scalar(x, x, rms[:, R_ATT[l] + t:R_ATT[l] + t + 1], float(CW ** 0.5), ALU.mult, ALU.mult)\
                        .then_inc(at_ready, 1)

            def residual2(l):
                root_wait(("conv", l))
                r = rms[:, R_CONV[l]:R_CONV[l] + 2]
                link(v.tensor_scalar(r, r, float(CW ** 0.5), None, ALU.mult))
                for c in range(2):
                    for t in range(NT):
                        dve.wait_ge(op_ready, 4 * (2 + l) + 2 * c + t + 1)
                        hh = h[:, t, 512 * c:512 * (c + 1)]
                        link(v.tensor_tensor(hh, hh, pb[2 * c + t][:], ALU.add))
                        v.scalar_tensor_tensor(hh, pb[4 + 2 * c + t][:], r[:, t:t + 1], hh, ALU.mult, ALU.add)\
                            .then_inc(h_done, 1)

            def route(l):
                dve.wait_ge(rt_ready, l + 1)

                def cols(a, n):
                    return rt[:, a:a + 2 * n].rearrange("p (t n) -> p t n", t=NT)

                lg = cols(0, 36)
                gmax, gidx = rt[:, 72:74], rt[:, 74:76]
                gcmp, goh, gx = cols(80, 4), cols(96, 4), cols(112, 4)
                gsum = rt[:, 120:122]
                elm, ecmp = cols(128, NE), cols(192, NE)
                oh = [cols(256, NE), cols(448, NE)]
                mx = [rt[:, 368:370], rt[:, 370:372]]
                idx = [rt[:, 372:374], rt[:, 374:376]]
                dz = rt[:, 364:366]
                asg = cols(384, NE)
                i4, i32 = cst[:, C_I4:C_I4 + 4], cst[:, C_I32:C_I32 + NE]

                def spread(x, n):
                    return view(x, 0, [[1, NT], [0, n]])

                link(v.tensor_tensor(lg, pb[0][:, 0:128].rearrange("p (t n) -> p t n", t=NT)[:, :, 0:36],
                                     view(brt[:, l, :], 0, [[0, NT], [1, 36]]), ALU.add))
                gl, el = lg[:, :, 0:NEG], lg[:, :, NEG:36]
                link(v.tensor_reduce(gmax, gl, AX, ALU.max))
                link(v.tensor_tensor(gcmp, gl, spread(gmax, 4), ALU.is_lt))
                link(v.scalar_tensor_tensor(gcmp, gcmp, 1.0e6, view(i4, 0, [[0, NT], [1, 4]]), ALU.mult, ALU.add))
                link(v.tensor_reduce(gidx, gcmp, AX, ALU.min))
                link(v.tensor_tensor(goh, view(i4, 0, [[0, NT], [1, 4]]), spread(gidx, 4), ALU.is_equal))
                v.tensor_tensor(gx, gl, spread(gmax, 4), ALU.subtract).then_inc(rt_x, 1)
                link(v.tensor_scalar(gcmp, goh, -1.0, BIG, ALU.add, ALU.mult))
                for t in range(NT):
                    o8 = view(goh, 4 * t, [[1, 4], [0, 8]])
                    e8 = view(elm, NE * t, [[8, 4], [1, 8]])
                    link(v.tensor_tensor(e8, view(el, 36 * t, [[8, 4], [1, 8]]), o8, ALU.mult))
                    link(v.tensor_tensor(e8, e8, view(gcmp, 4 * t, [[1, 4], [0, 8]]), ALU.add))
                for k in range(2):
                    link(v.tensor_reduce(mx[k], elm, AX, ALU.max))
                    link(v.tensor_tensor(ecmp, elm, spread(mx[k], NE), ALU.is_lt))
                    link(v.scalar_tensor_tensor(ecmp, ecmp, 1.0e6, view(i32, 0, [[0, NT], [1, NE]]), ALU.mult, ALU.add))
                    link(v.tensor_reduce(idx[k], ecmp, AX, ALU.min))
                    link(v.tensor_tensor(oh[k], view(i32, 0, [[0, NT], [1, NE]]), spread(idx[k], NE), ALU.is_equal))
                    if k == 0:
                        link(v.scalar_tensor_tensor(elm, oh[0], -BIG, elm, ALU.mult, ALU.add))
                v.tensor_tensor(asg, oh[0], oh[1], ALU.add).then_inc(as_done, 1)
                v.tensor_tensor(dz, mx[1], mx[0], ALU.subtract).then_inc(rt_x, 1)
                dve.wait_ge(cnt_ready, l + 1)
                cm, wm = rt[0:NE, 512:640], rt[0:NE, 640:768]
                v.tensor_copy(cm, pb[1][0:NE, 0:P]).then_inc(cnt_done, 1)
                link(v.tensor_scalar(wm, pb[1][0:NE, 0:P], float(W), 1.0, ALU.is_gt, ALU.add))
                wt = rt[0:NE, 768:896]
                link(v.tensor_scalar(wt, pb[1][0:NE, 0:P], float(2 * W), None, ALU.is_gt))
                link(v.tensor_tensor(wm, wm, wt, ALU.add))
                link(v.tensor_scalar(wt, pb[1][0:NE, 0:P], float(3 * W), None, ALU.is_gt))
                v.tensor_tensor(wm, wm, wt, ALU.add).then_inc(cnt_done, 1)
                dve.wait_ge(rt_e, 2 * l + 2)
                link(v.tensor_reduce(gsum, gx, AX, ALU.add))
                g1, g2 = rt[:, 376:378], rt[:, 378:380]
                link(v.tensor_scalar(g1, dz, 1.0, None, ALU.add))
                link(v.tensor_tensor(g1, g1, gsum, ALU.mult))
                link(v.reciprocal(g1, g1))
                link(v.tensor_tensor(g2, dz, g1, ALU.mult))
                dve.wait_ge(pos_ready, l + 1)
                v.tensor_copy(tab[:], pb[3][0:1, 0:3 * NE]).then_inc(tab_done, 1)
                st = rt[:, 896:896 + NE]
                link(v.tensor_copy(st, pb[3][:, 0:NE]))
                pos = cols(928, NE)
                link(v.tensor_tensor(pos, pb[2][:, 0:2 * NE].rearrange("p (t n) -> p t n", t=NT),
                                     view(st, 0, [[0, NT], [1, NE]]), ALU.add))
                sl = [rt[:, 992:994], rt[:, 994:996]]
                for k in range(2):
                    link(v.tensor_tensor(ecmp, oh[k], pos, ALU.mult))
                    link(v.tensor_reduce(sl[k], ecmp, AX, ALU.add))
                i512 = cst[:, C_I512:C_I512 + NS]
                for t in range(NT):
                    link(v.tensor_scalar(sel[:, t, :], i512, sl[0][:, t:t + 1], None, ALU.is_equal))
                    i = v.scalar_tensor_tensor(sel[:, t, :], i512, sl[1][:, t:t + 1], sel[:, t, :], ALU.is_equal, ALU.add)
                    if t == 0:
                        link(i)
                i.then_inc(sel_done, 1)
                for t in range(NT):
                    link(v.tensor_scalar(gsel[:, t, :], i512, sl[0][:, t:t + 1], g1[:, t:t + 1], ALU.is_equal, ALU.mult))
                    link(v.tensor_scalar(gtmp, i512, sl[1][:, t:t + 1], g2[:, t:t + 1], ALU.is_equal, ALU.mult))
                    i = v.tensor_tensor(gsel[:, t, :], gsel[:, t, :], gtmp, ALU.add)
                    if t == 0:
                        link(i)
                i.then_inc(sel_done, 1)

            def moe(l):
                normalise(7 + 2 * l)
                evac_tp(10 + 3 * l)
                route(l)
                col = G_NORM[7 + 2 * l]
                v.memset(xsT[:, :, NS:NSP], 0.0).then_inc(xsT_v, 1)
                for k in range(1, KC, 2):
                    dve.wait_ge(ga_ready, KC * l + k + 1)
                    v.tensor_scalar(xsT[:, k, 0:NS], pb[4 + k % 4][:], gT[:, col + k:col + k + 1], None, ALU.mult)\
                        .then_inc(xsT_v, 1)
                for c in range(2):
                    dve.wait_ge(gct_ready, 2 * l + c + 1)
                    v.tensor_copy(gcombT[:, 2 * c:2 * c + 2, :], pb[c][:].rearrange("p (a b) -> p a b", a=2))\
                        .then_inc(gct_done, 1)
                with dve.Fori(0, NE) as e:
                    n = dve.value_load(tab[0:1, bass.ds(e + 2 * NE, 1)], min_val=1, max_val=4)
                    w0 = dve.value_load(tab[0:1, bass.ds(e + NE, 1)], min_val=0, max_val=4 * NE)
                    with dve.Fori(0, n) as k:
                        dve.wait_ge(eth_done[l], w0 + k + 1)
                        v.scalar_tensor_tensor(eg, eg, 1.0, pb[0][:, 0:S], ALU.add, ALU.mult).then_inc(eg_done[l], 1)
                        dve.wait_ge(eg_done[l], w0 + k + 1)
                        v.scalar_tensor_tensor(eh, eg, 0.5, pb[1][:, 0:S], ALU.mult, ALU.mult).then_inc(eh_done[l], 1)
                for i in range(1, 8, 2):
                    dve.wait_ge(yt_ready, 8 * l + i + 1)
                    v.tensor_copy(ysort[:, i // 2, 512:1024], pb[4 + i % 4][:]).then_inc(yt_v, 1)
                residual(op_ready2, 4 * l)

            normalise(0)
            evac_tp(0)
            dve.wait_ge(scr_written, 32)
            evac_proj(0, PJ_AT[1])
            head_norms(0)
            evac_heads(0)
            attention(0)
            evac_tp(1)
            residual(op_ready, 0)
            normalise(1)
            evac_tp(2)
            ffn(0)
            normalise(2)
            evac_tp(3)
            ple(0)
            normalise(3)
            evac_tp(4)
            evac_proj(1, PJ_AT[2])
            compress()
            head_norms(1)
            evac_heads(1)
            nsa_gates()
            attention(1)
            evac_tp(5)
            residual(op_ready, 4)
            normalise(4)
            evac_tp(6)
            ffn(1)
            normalise(5)
            evac_tp(7)
            ple(1)
            for l in range(2):
                normalise(6 + 2 * l)
                evac_tp(8 + 3 * l)
                evac_proj(2 + l, PJ_AT[2 + l] + 2)
                rope(l)
                conv(l)
                evac_heads(2 + l)
                attention(2 + l)
                attn_out(l)
                evac_tp(9 + 3 * l)
                residual2(l)
                moe(l)
            root_wait(("norm", 10))
            dve.wait_ge(gfin_loaded, 16)
            for t in range(NT):
                link(v.tensor_scalar(xs[:, t, :], h[:, t, :], rms[:, R_NORM[10] + t:R_NORM[10] + t + 1], float(D ** 0.5),
                                     ALU.mult, ALU.mult))
                v.tensor_tensor(xs[:, t, :], xs[:, t, :], gfin, ALU.mult).then_inc(out_ready, 1)


def shape_constants():
    c = np.zeros((P, C_W), np.float32)
    c[:, C_ID:C_ID + P] = np.eye(P)
    c[:, C_TRI:C_TRI + P] = np.triu(np.ones((P, P)), 1)
    c[:, C_I512:C_I512 + NS] = np.arange(NS)
    c[:, C_I32:C_I32 + NE] = np.arange(NE)
    c[:, C_I4:C_I4 + NEG] = np.arange(NEG)
    c[:, C_VALID] = np.arange(P) >= CMP_LEN - 1
    inv = np.float32(500000.0) ** (-np.arange(0, 16, 2, dtype=np.float32) / np.float32(16))
    ang = np.arange(S, dtype=np.float32)[:, None] * inv[None, :].astype(np.float32)
    for col, f in ((C_COS, np.cos), (C_SIN, np.sin)):
        a = f(ang.astype(np.float64)).astype(np.float32).reshape(NT, P, 8)
        c[:, col:col + 16] = a.transpose(1, 0, 2).reshape(P, 16)
    d = np.arange(512) - 255
    exact = BUCKETS // 2
    nf = np.maximum(d, 1).astype(np.float32)
    large = exact + (np.log(nf / np.float32(exact)) / np.float32(np.log(2048 / exact)) * np.float32(BUCKETS - exact)).astype(np.int32)
    bucket = np.where(d < exact, np.maximum(d, 0), np.minimum(large, BUCKETS - 1))
    onehot = ((bucket[None, :] == np.arange(BUCKETS)[:, None]) & (d >= 0)[None, :]).astype(np.float32)
    causal = np.where(d >= 0, 0.0, OFF)
    times = np.where(d >= 0, (d <= 128) * 1 + (d % 4 == 0) * 1 + (d % 16 == 0) * 1, 0)
    dilated = np.where(times > 0, 8.0 * np.log(np.maximum(times, 1)), OFF)
    masks = np.tile(np.concatenate([causal, dilated]).astype(np.float32), (NH, 1))
    window = np.where(np.abs(d) <= 128, 0.0, OFF).astype(np.float32)
    return {"consts": c, "onehot": onehot, "row_masks": masks, "window_band": window}


_INS = ["x", "p", "rel_bias", "norm_mix", "norm_ffn", "norm_ple", "w_ffn_gate", "w_ffn_up", "w_ffn_down", "w_ple_proj",
        "w_ple_gate", "w_in_ab", "w_out_ab", "qn_moba", "kn_moba", "qn_dil", "kn_dil", "w_in_nsa", "w_out_nsa",
        "qn_nsa", "kn_cmp", "kn_slc", "kn_win", "cmp_k_pos", "cmp_k_w1", "cmp_k_b1", "cmp_k_w2", "cmp_k_b2",
        "cmp_v_pos", "cmp_v_w1", "cmp_v_b1", "cmp_v_w2", "cmp_v_b2", "norm_mix_2", "w_in_2", "attn_sink_2",
        "conv_w_2", "norm_attn_out_2", "norm_conv_out_2", "w_out_2", "norm_ffn_2", "w_router_group_2",
        "b_router_group_2", "w_router_expert_2", "b_router_expert_2", "w_expert_gate_2", "w_expert_up_2",
        "w_expert_down_2", "norm_final_2"]


def kernel(**inputs):
    import numpy as _np
    import concourse.bacc as _bacc
    from concourse import mybir as _mybir
    from concourse.bass_utils import run_bass_kernel_spmd as _run

    nc = _bacc.Bacc("TRN2", target_bir_lowering=False, num_devices=1)
    arrays, args = {}, {}
    for name, a in [(n, inputs[n]) for n in _INS] + list(shape_constants().items()):
        a = _np.ascontiguousarray(a)
        arrays[f"in_{name}"] = a
        args[name] = nc.dram_tensor(f"in_{name}", a.shape, _mybir.dt.from_np(a.dtype), kind="ExternalInput").ap()
    out = nc.dram_tensor("out_0", (1, S, D), F32, kind="ExternalOutput").ap()
    build(nc, args, out)
    r = _run(nc, [arrays], core_ids=[0])
    return r.results[0]["out_0"]
```

```python
from contextlib import ExitStack

import concourse.bass as bass
from concourse import mybir
import numpy as np

F32 = mybir.dt.float32
F32R = mybir.dt.float32r
I32 = mybir.dt.int32
ALU = mybir.AluOpType
ACT = mybir.ActivationFunctionType
AX = mybir.AxisListType.X

P = 128
S = 256
NT = S // P
D = 1024
KC = D // P
HD = 64
NH = 16
F = 2816
FJ = F // P
BUCKETS = 32
NCMP = 15
CMP_LEN, CMP_STRIDE = 32, 16
NG = 4
HEADS2, KV2 = 8, 2
CW = 512
NE, NEG = 32, 4
DE = 512
W = 64
NS = 2 * S
NSP = NS + W
RAW = 6
SPL = 3
HALF = 2048
JOBS = NE + NS // W
EPS = 1e-6
OFF = -1.0e30
BIG = 3.0e38
WHY = "a job's window starts below the end of its expert's slots"
NB = 384
GELU = 0.7978845608028654

G_NORM = [0, 16, 32, 8, 24, 40, 48, 64, 56, 72]
G_ATT, G_CONV, G_CW, G_B1, PRM_ROWS = 80, 88, 96, 120, 122
H_POS, HEAD_ROWS = 8, 72
C_ID, C_TRI, C_I512, C_I32, C_I4, C_VALID, C_COS, C_SIN, C_W = 0, 128, 256, 768, 800, 804, 805, 821, 837


def view(ap, off, dims):
    return bass.AP(tensor=ap.tensor, offset=ap.offset + off, ap=[list(ap.ap[0])] + [list(d) for d in dims])


def build(nc, A, out):
    ctx = ExitStack()
    with ctx:
        def sb(name, shape, dt=F32):
            return ctx.enter_context(nc.sbuf_tensor(name, shape, dt))

        def sem(name):
            return ctx.enter_context(nc.semaphore(name))

        raw = sb("raw", [P, RAW, HALF])
        parts = sb("parts", [P, SPL, 2, HALF], F32R)
        h = sb("h", [P, NT, D])
        xT = sb("xT", [P, 2, KC, S], F32R)
        xs = sb("xs", [P, NT, D])
        NBAND = 8
        work = sb("work", [P, NBAND * NB + 2 * 4 * S])
        band = work[:, 0:NBAND * NB].rearrange("p (a b) -> p a b", a=NBAND)
        qkv = sb("qkv", [P, 6144])
        qk = sb("qk", [P, 16, S])
        sbuf_s = work[:, NBAND * NB:NBAND * NB + 4 * S].rearrange("p (a b) -> p a b", a=4)
        sbuf_p = work[:, NBAND * NB + 4 * S:].rearrange("p (a b) -> p a b", a=4)
        hidT = sb("hidT", [P, 2, 2, S], F32R)
        wr = sb("wr", [P, 2, KC, NEG + NE])
        cst = sb("cst", [P, C_W])
        ones = sb("ones", [P, P])
        mhalf = sb("mhalf", [P, 64])
        gT = sb("gT", [P, PRM_ROWS])
        g2T = sb("g2T", [P, HEAD_ROWS])
        sink = sb("sink", [P, 2, 2, HEADS2])
        brt = sb("brt", [P, 2, NEG + NE])
        relb = sb("relb", [BUCKETS, NH])
        w2 = sb("w2", [P, 2, HD])
        b2 = sb("b2", [P, 2, HD])
        rms = sb("rms", [P, 256])
        NU = 32 + 96 + 16 + 16
        nmax = sb("nmax", [P, NU])
        den = sb("den", [P, NU])
        rec = sb("rec", [P, 4])
        esink = sb("esink", [P, 32])
        gates = sb("gates", [P, NT, 48])
        cmpk = sb("cmpk", [16, 2, NG, HD])
        cmpT = sb("cmpT", [P, NG, 16])
        tab = sb("tab", [1, 2 * JOBS + 1], I32)
        pb = [ctx.enter_context(nc.psum_tensor(f"pb{i}", [P, 512], F32)) for i in range(8)]
        scr = nc.dram_tensor("scr", [2 * NH, 512], F32, kind="Internal").ap()

        def qkv_t(t):
            return qkv[:, 3072 * t:3072 * (t + 1)]

        ident = cst[:, C_ID:C_ID + P]
        tri = cst[:, C_TRI:C_TRI + P]
        prm = qkv[:, 0:2 * P].rearrange("p (a b) -> p a b", a=2)
        oneh = qk[0:BUCKETS, 0:2, :].rearrange("p a b -> p (a b)")
        tmask = qk[0:NH, 2:6, :].rearrange("p a b -> p (a b)")
        trow = qk[0:NH, 6:10, :].rearrange("p a b -> p (a b)")
        rowsP = sbuf_p[:, 0:2, :]
        fh = sbuf_p[:, 2:4, :]
        th = sbuf_s[:, 0:2, :]
        ga = sbuf_s[:, 2:4, :]
        cmph = sbuf_p[:, 0:2, :].rearrange("p a (b c) -> p a b c", b=4)
        cmpd = sbuf_p[0:16, 2:4, :].rearrange("p a b -> p (a b)").rearrange("p (g t d) -> p g t d", g=NG, t=2)
        cT = qk[0:HD, 0:8, :]
        kv2cols = 768
        qkv2 = qkv[:, 0:NT * kv2cols].rearrange("p (t c) -> p t c", t=NT)
        gbT = qkv[:, 1536:2560]
        gcT = qkv[:, 2560:3584]
        cuT = qkv[:, 3584:3584 + 4 * (S + 2)].rearrange("p (c s) -> p c s", c=4)
        yT = qkv[:, 4616:5640]
        ysT = work[:, NB:NB + KC * NSP].rearrange("p (k s) -> p k s", k=KC)
        qkf = qk[:, :, :].rearrange("p a b -> p (a b)")
        xsT = qkv[:, 0:KC * NSP].rearrange("p (k s) -> p k s", k=KC)
        gcombT = qkv[:, 4608:5632].rearrange("p (c s) -> p c s", c=4)
        ysort = qkv[:, 0:4096].rearrange("p (c d) -> p c d", c=4)
        sel = sbuf_s.rearrange("p a b -> p (a b)").rearrange("p (t s) -> p t s", t=NT)
        gsel = sbuf_p.rearrange("p a b -> p (a b)").rearrange("p (t s) -> p t s", t=NT)
        rt = qkf[:, 0:2048]
        gtmp = qkf[:, 2048:2560]
        gs, us, ys = qkf[:, 0:512], qkf[:, 512:1024], qkf[:, 1024:2048]
        eg, ea, eu, eh = (qkf[:, 2048 + 256 * i:2304 + 256 * i] for i in range(4))
        xw = xT[:, 0, 0:4, :].rearrange("p a b -> p (a b)").rearrange("p (k s) -> p k s", k=KC)
        ehl = xT[:, 1, 0:2, :].rearrange("p a b -> p (a b)").rearrange("p (j s) -> p j s", j=DE // P)
        gfin = qkf[:, 0:D]

        x_loaded = sem("x_loaded")
        par_loaded = sem("par_loaded")
        cst_loaded = sem("cst_loaded")
        rel_loaded = sem("rel_loaded")
        arrived = [[sem(f"arrived{g}_{i}") for i in range(RAW)] for g in range(4)]
        hi_done = [sem(f"hi_done{g}") for g in range(4)]
        lo_done = [sem(f"lo_done{g}") for g in range(4)]
        used = [sem(f"used{g}") for g in range(4)]
        par2_loaded, p_loaded, p_ready = sem("par2_loaded"), sem("p_loaded"), sem("p_ready")
        pT_done, pT_v = sem("pT_done"), sem("pT_v")
        set_ready, set_done = sem("set_ready"), sem("set_done")
        trow_done, scr_written, band_loaded = sem("trow_done"), sem("scr_written"), [sem(f"band_loaded{i}") for i in range(2)]
        wr_loaded, gfin_loaded = sem("wr_loaded"), sem("gfin_loaded")
        dch, ach, pch = sem("dve_chain"), sem("act_chain"), sem("pool_chain")
        sq_done, rstd_done, xs_ready = sem("sq_done"), sem("rstd_done"), sem("xs_ready")
        ss_done = sem("ss_done")
        tp_ready, xT_a, xT_v = sem("tp_ready"), sem("xT_a"), sem("xT_v")
        pj_ready, pj_a, pj_v = sem("pj_ready"), sem("pj_a"), sem("pj_v")
        op_ready, h_done = sem("op_ready"), sem("h_done")
        gu_ready, th_done, hT_done, dn_done = sem("gu_ready"), sem("th_done"), sem("hT_done"), sem("dn_done")
        ple_ready, ple_th = sem("ple_ready"), sem("ple_th")
        hsq, hss, qn_ready = sem("head_squares"), sem("head_sums"), sem("qn_ready")
        qt_ready, qt_a, qt_v = sem("qt_ready"), sem("qt_a"), sem("qt_v")
        s_ready, s_max, e_done = sem("s_ready"), sem("s_max"), sem("e_done")
        pt_ready, pt_done, o_ready, o_done = sem("pt_ready"), sem("pt_done"), sem("o_ready"), sem("o_done")
        cT_ready, cT_done, hid_ready, gel_in, gel_th, gel_done = (sem("cT_ready"), sem("cT_done"), sem("hid_ready"),
                                                                 sem("gel_in"), sem("gel_th"), sem("gel_done"))
        cmp_ready, cmpn_done, cmpT_ready, cmpT_done = (sem("cmp_ready"), sem("cmpn_done"), sem("cmpT_ready"),
                                                       sem("cmpT_done"))
        g_th = sem("g_th")
        gb_done, y_done = sem("gb_done"), sem("y_done")
        ysq_done, yss_ready, yss_done = sem("ysq_done"), sem("yss_ready"), sem("yss_done")
        on_ready = sem("on_ready")
        rt_ready, rt_e, rt_x, as_done, cnt_ready, cnt_done = (sem("rt_ready"), sem("rt_e"), sem("rt_x"),
                                                              sem("as_done"), sem("cnt_ready"), sem("cnt_done"))
        pos_ready, tab_done, sel_done = sem("pos_ready"), sem("tab_done"), sem("sel_done")
        ga_ready, xsT_a, xsT_v = sem("ga_ready"), sem("xsT_a"), sem("xsT_v")
        gct_ready, gct_done = sem("gct_ready"), sem("gct_done")
        at_ready, cx_done, yt_v, op_ready2 = sem("at_ready"), sem("cx_done"), sem("yt_v"), sem("op_ready2")
        xw_ready, ys_done, gs_done, us_done, gt_ready, yt2_ready = ([sem(f"{n}{i}") for i in range(2)] for n in (
            "xw_ready", "ys_done", "gs_done", "us_done", "gt_ready", "yt2_ready"))
        g_added, eth_done, eh_done, yadd_done, ech, xw_rounded = ([sem(f"{n}{i}") for i in range(2)] for n in (
            "g_added", "eth_done", "eh_done", "yadd_done", "job_chain", "xw_rounded"))
        y_first, eg_first = ([sem(f"{n}{i}") for i in range(2)] for n in ("y_first", "eg_first"))
        job_ready, job_cols = sem("job_ready"), sem("job_cols")
        yt_ready, yt_done = sem("yt_ready"), sem("yt_done")
        out_ready, stored = sem("out_ready"), sem("stored")

        stream = {0: [], 2: []}
        splits = {0: [], 2: []}

        def kcols(w, c0, n, k0=0, k=KC):
            return w[k0 * P:(k0 + k) * P, c0:c0 + n].rearrange("(k p) n -> p k n", p=P)

        RAW0 = [0, 0, 0, 0]

        def add(seg, src, k, n, parts_n=P, release=None):
            i = len(stream[seg])
            place = (RAW0[seg] + i) % RAW
            if release is None:
                splits[seg].append(i)
                done = (lo_done[seg], len(splits[seg]))
            else:
                done = release
            stream[seg].append((raw[0:parts_n, place, 0:k * n].rearrange("p (k n) -> p k n", k=k), src, place, done, (k, n)))
            return len(splits[seg]) - 1 if release is None else i

        def both(seg, s):
            k, n = stream[seg][splits[seg][s]][4]
            return [parts[:, (SPL0[seg] + s) % SPL, i, 0:k * n].rearrange("p (k n) -> p k n", k=k) for i in range(2)]

        SPL0 = [0, 0, 0, 0]
        PJ = []
        PJ_AT = {}
        SEG = [0, 0, 0, 2]

        def add_proj(layer, w, cols):
            PJ_AT[layer] = len(PJ)
            for c0, n, dst in cols:
                PJ.append(([add(SEG[layer], kcols(w, c0, n, 4 * hf, 4), 4, n) for hf in range(2)], n, dst))

        OPW, FFW, PLW, CMPW, CVW = {}, {}, {}, {}, {}

        def add_out(k, w):
            OPW[k] = [[add(SEG[k], kcols(w, 512 * c, 512, 4 * hf, 4), 4, 512) for hf in range(2)] for c in range(2)]

        def add_ffn(f):
            FFW[f] = []
            for q in range(FJ // 2):
                FFW[f].append((add(0, kcols(A["w_ffn_gate"][f], q * S, S), KC, S),
                               add(0, kcols(A["w_ffn_up"][f], q * S, S), KC, S),
                               add(0, A["w_ffn_down"][f][q * S:(q + 1) * S, :].rearrange("(k p) n -> p k n", p=P), 2, D)))

        def add_ple(f):
            pr = add(0, A["w_ple_proj"][f].rearrange("(k p) n -> p k n", p=P), 2, D)
            PLW[f] = (pr, [[add(0, kcols(A["w_ple_gate"][f], 512 * c, 512, 4 * hf, 4), 4, 512) for hf in range(2)]
                           for c in range(2)])

        add_proj(0, A["w_in_ab"][0], [(512 * c, 512, 512 * c) for c in range(6)])
        add_out(0, A["w_out_ab"][0])
        add_ffn(0)
        add_ple(0)
        add_proj(1, A["w_in_nsa"][0], [(512 * c, 512, 512 * c) for c in range(5)] + [(2560, 48, 2560)])
        for kv, name in enumerate(("cmp_k_w1", "cmp_v_w1")):
            CMPW[kv] = []
            for hf in range(2):
                src = A[name][0].rearrange("(l d) n -> d l n", d=HD)[:, 16 * hf:16 * (hf + 1), :]
                CMPW[kv].append(add(0, src, CMP_LEN // 2, P, parts_n=HD, release=(hid_ready, kv + 1)))
        add_out(1, A["w_out_nsa"][0])
        add_ffn(1)
        add_ple(1)
        for l in range(2):
            seg = SEG[2 + l]
            if l:
                RAW0[2] = RAW0[1]
                SPL0[2] = SPL0[1]
            add_proj(2 + l, A["w_in_2"][l], [(0, 512, 0), (512, 256, 512)])
            CVW[l] = [[add(seg, kcols(A["w_in_2"][l], 768 + 512 * c + S * hf, S), KC, S) for hf in range(2)]
                      for c in range(3)]
            add_out(2 + l, A["w_out_2"][l])
            RAW0[seg + 1] = (RAW0[seg] + len(stream[seg])) % RAW
            SPL0[seg + 1] = (SPL0[seg] + len(splits[seg])) % SPL

        def at(j, per_job, more):
            return j * per_job + more if isinstance(j, int) else j * per_job + (2 * per_job + more)

        def gate_up(j):
            q0 = 2 if isinstance(j, int) and j == 0 else 0
            return [(q0 + 2 * m + hf, m, hf) for m in range(2) for hf in range(2)]

        def down_at(last):
            return 0 if last else 4

        def job_place(l, q):
            return (RAW0[2 * l + 1] + q - 2) % RAW

        def job_parts(l, q, shape=None):
            two = [parts[:, (SPL0[2 * l + 1] + q - 2) % SPL, i, :] for i in range(2)]
            return [x.rearrange("p (k n) -> p k n", k=shape[0]) for x in two] if shape else two

        SHAPES = [(4, DE), (4, DE), (2, D)]

        TP = [("norm", 0), ("attn", 0), ("norm", 1), ("norm", 2), ("norm", 3), ("attn", 1), ("norm", 4), ("norm", 5),
              ("norm", 6), ("attn2", 0), ("norm", 7), ("norm", 8), ("attn2", 1), ("norm", 9)]
        TPN = [8 if kind != "attn2" else 4 for kind, _ in TP]

        def tp_chunks(m):
            return sum(TPN[:m])

        def head_list(layer):
            z = []
            if layer == 0:
                for c in range(8):
                    z.append(([qkv_t(t)[:, (128 * c if c < 4 else 1024 + 128 * c):][:, 0:P] for t in range(NT)],
                              qk[:, c, :], 0 if c < 4 else 2))
                for c in range(8):
                    z.append(([qkv_t(t)[:, (512 + 128 * c if c < 4 else 1536 + 128 * c):][:, 0:P] for t in range(NT)],
                              qk[:, 8 + c, :], 1 if c < 4 else 3))
            elif layer == 1:
                for c in range(8):
                    z.append(([qkv_t(t)[:, 128 * c:128 * c + P] for t in range(NT)], qk[:, c, :], 4))
                for c in range(8):
                    z.append(([xs[:, t, 128 * c:128 * c + P] for t in range(NT)], qk[:, 8 + c, :], 5 + c // 4))
            else:
                for c in range(4):
                    z.append(([qkv2[:, t, 128 * c:128 * c + P] for t in range(NT)], qk[:, c, :], None))
                for c in range(KV2):
                    z.append(([xs[:, t, 128 * c:128 * c + P] for t in range(NT)], qk[:, 8 + c, :], None))
            return z

        QN = [4, 10, 4, 4]
        QT = [head_list(l) for l in range(4)]
        QT_AT = [sum(len(q) for q in QT[:l]) for l in range(5)]

        QT_V = [sum(2 * (len(q) // 4) for q in QT[:l]) for l in range(5)]
        QT_A = [QT_AT[l] - QT_V[l] for l in range(5)]

        class Unit:
            pass

        def unit_list(layer):
            us = []
            for hh in range(NH if layer < 2 else HEADS2):
                lo = HD * (hh % 2)
                for t in range(NT):
                    for br in range(3 if layer == 1 else 1):
                        u = Unit()
                        u.t, u.h, u.br, u.layer = t, hh, br, layer
                        u.q = qk[lo:lo + HD, hh // 2, P * t:P * (t + 1)]
                        u.nk = P * (t + 1) if layer < 2 else S
                        u.bias = view(band[:, hh % NBAND if layer < 2 else 0, :], 255 + P * t, [[-1, u.nk]])
                        kt = range(u.nk // P)
                        if layer == 0:
                            u.k = qk[lo:lo + HD, 8 + hh // 2, 0:u.nk]
                            vc = 1024 + HD * hh if hh < 8 else 2560 + HD * (hh - 8)
                            u.v = [qkv_t(i)[:, vc:vc + HD] for i in kt]
                        elif layer == 1 and br < 2:
                            g = hh // (NH // NG)
                            u.k = qk[lo:lo + HD, 8 + 4 * br + g, 0:u.nk]
                            vc = (1792 if br == 0 else 2304) + HD * g
                            u.v = [qkv_t(i)[:, vc:vc + HD] for i in kt]
                        elif layer == 1:
                            g = hh // (NH // NG)
                            u.nk = NCMP
                            u.k = cmpT[lo:lo + HD, g, 0:NCMP]
                            u.bias = view(band[:, hh % NBAND, :], 224 + P * t, [[-CMP_STRIDE, NCMP]])
                            u.v = [cmpk[0:NCMP, 1, g, :]]
                        else:
                            g = hh // (HEADS2 // KV2)
                            u.k = qk[lo:lo + HD, 8 + g, 0:u.nk]
                            u.v = [qkv2[:, i, 640 + HD * g:640 + HD * (g + 1)] for i in kt]
                        u.o = xs[:, t, HD * hh:HD * (hh + 1)]
                        us.append(u)
            return us

        UN = [unit_list(l) for l in range(4)]
        U_AT = [sum(len(u) for u in UN[:l]) for l in range(5)]

        R_NORM = [2 * n for n in range(11)]
        R_HEAD = {0: 22, 1: 86}
        R_CMP = 134
        R_ATT = [138, 142]
        R_CONV = [140, 144]
        ROOTS, ROOT_AT = [], {}

        def root(key, wait, col, n, width, parts=P):
            ROOT_AT[key] = len(ROOTS) + 1
            ROOTS.append((wait, col, n, parts, width))

        root(("norm", 0), (sq_done, 2), R_NORM[0], 2, D)
        root(("head", 0), (hss, 4), R_HEAD[0], 64, HD)
        for n in range(1, 4):
            root(("norm", n), (sq_done, 2 * n + 2), R_NORM[n], 2, D)
        root("cmp", (ss_done, 1), R_CMP, 4, HD, NCMP)
        root(("head", 1), (hss, 8), R_HEAD[1], 48, HD)
        for n in range(4, 7):
            root(("norm", n), (sq_done, 2 * n + 2), R_NORM[n], 2, D)
        root(("conv", 0), (yss_done, 1), R_CONV[0], 2, CW)
        root(("att", 0), (on_ready, 2), R_ATT[0], 2, CW)
        for n in range(7, 9):
            root(("norm", n), (sq_done, 2 * n + 2), R_NORM[n], 2, D)
        root(("conv", 1), (yss_done, 2), R_CONV[1], 2, CW)
        root(("att", 1), (on_ready, 4), R_ATT[1], 2, CW)
        for n in range(9, 11):
            root(("norm", n), (sq_done, 2 * n + 2), R_NORM[n], 2, D)

        PARS = []

        def par(dst, src):
            PARS.append((dst, src))

        for r0, name in ((0, "norm_mix"), (16, "norm_ffn"), (32, "norm_ple"), (48, "norm_mix_2"), (64, "norm_ffn_2")):
            par(prm[r0:r0 + 16, 0, :], A[name].rearrange("l (k p) -> (l k) p", p=P))
        par(prm[G_ATT:G_ATT + 8, 0, :], A["norm_attn_out_2"].rearrange("l (k p) -> (l k) p", p=P))
        par(prm[G_CONV:G_CONV + 8, 0, :], A["norm_conv_out_2"].rearrange("l (k p) -> (l k) p", p=P))
        par(prm[G_CW:G_CW + 24, 0, :], A["conv_w_2"].rearrange("l j (k p) -> (l j k) p", p=P))
        for kv, name in enumerate(("cmp_k_b1", "cmp_v_b1")):
            par(prm[G_B1 + kv:G_B1 + kv + 1, 0, :], A[name])
        NPAR0 = len(PARS)
        for half in range(2):
            cols = slice(HD * half, HD * (half + 1))
            for r, name in enumerate(("qn_moba", "kn_moba", "qn_dil", "kn_dil", "qn_nsa", "kn_slc", "kn_win", "kn_cmp")):
                par(prm[r:r + 1, 1, cols], A[name])
            for kv, name in enumerate(("cmp_k_pos", "cmp_v_pos")):
                par(prm[H_POS + 32 * kv:H_POS + 32 * (kv + 1), 1, cols], A[name][0])
        for l in range(2):
            par(sink[:, l, 0, :], A["attn_sink_2"][l:l + 1, :].broadcast_to([P, HEADS2]))
            par(brt[:, l, 0:NEG], A["b_router_group_2"][l:l + 1, :].broadcast_to([P, NEG]))
            par(brt[:, l, NEG:NEG + NE], A["b_router_expert_2"][l:l + 1, :].broadcast_to([P, NE]))
        for kv, c in enumerate("kv"):
            par(w2[:, kv, :], A[f"cmp_{c}_w2"][0])
            par(b2[:, kv, :], A[f"cmp_{c}_b2"].broadcast_to([P, HD]))

        def jobs_work():
            return rt[0:NE, 1024:1024 + JOBS], rt[0:NE, 1088:1088 + JOBS], rt[0:NE, 1150:1151]

        block = ctx.enter_context(nc.Block())

        @block.sync
        def _(sp):
            sp.dma_start(h[:], A["x"][0].rearrange("(t p) d -> p t d", p=P)).then_inc(x_loaded, 16)

            def load(seg, i):
                dst, src, place, _, _ = stream[seg][i]
                if i >= RAW:
                    sp.wait_ge(*stream[seg][i - RAW][3])
                elif seg:
                    sp.wait_ge(lo_done[1], at(more, 6, i - RAW + 1))
                sp.dma_start(dst, src).then_inc(arrived[seg][place], 16)

            ws = [[A[n][l] for n in ("w_expert_gate_2", "w_expert_up_2", "w_expert_down_2")] for l in range(2)]

            def load_job(l, j, e, q, m, hf):
                if isinstance(j, int) and 6 * j - 2 + q < RAW:
                    sp.wait_ge(*stream[2 * l][len(stream[2 * l]) - RAW + 6 * j - 2 + q][3])
                else:
                    sp.wait_ge(lo_done[2 * l + 1], at(j, 6, q - 7))
                k, n = SHAPES[m]
                place = job_place(l, q)
                w = ws[l][m][bass.ds(e, 1), :, :] if not isinstance(e, int) else ws[l][m][e:e + 1, :, :]
                src = w[:, P * k * hf:P * k * (hf + 1), :].rearrange("e (k p) n -> p (e k) n", p=P)
                sp.dma_start(raw[:, place, :].rearrange("p (k n) -> p k n", k=k), src).then_inc(arrived[2 * l + 1][place], 16)

            def expert(j):
                return sp.value_load(tab[0:1, bass.ds(j, 1)], min_val=0, max_val=NE - 1)

            for l in range(2):
                seg = 2 * l
                for i in range(len(stream[seg])):
                    load(seg, i)
                for q, m, hf in gate_up(0):
                    load_job(l, 0, 0, q, m, hf)
                sp.wait_ge(tab_done, l + 1)
                more = sp.value_load(tab[0:1, 2 * JOBS:2 * JOBS + 1], min_val=NS // W - 2, max_val=JOBS - 2)

                def step(j):
                    e, e1 = expert(at(j, 1, 0)), expert(at(j, 1, -1))
                    for q, m, hf in gate_up(j):
                        load_job(l, j, e, q, m, hf)
                    for hf in range(2):
                        load_job(l, j, e1, down_at(False) + hf, 2, hf)

                step(1)
                with sp.Fori(0, more) as j:
                    step(j)
                e1 = expert(at(more, 1, -1))
                for hf in range(2):
                    load_job(l, more, e1, down_at(True) + hf, 2, hf)
            sp.wait_ge(out_ready, 2)
            sp.dma_start(out[0].rearrange("(t p) d -> p t d", p=P), xs[:]).then_inc(stored, 16)
            sp.wait_ge(stored, 16)

        @block.gpsimd
        def _(pool):
            def bands(layer):
                for q in range(4 * layer, 4 * layer + 4):
                    if q >= 2:
                        pool.wait_ge(s_max, U_AT[(q - 2) // 4] + ((q - 2) % 4 + 1) * (len(UN[(q - 2) // 4]) // 4))
                    row = 4 * (q % 4) + (NH if 2 <= q < 4 else 0)
                    src = bass.AP(tensor=scr.tensor, offset=512 * row, ap=[[1, P], [512, 4], [1, NB]])
                    nc.gpsimd.dma_start(band[:, 4 * (q % 2):4 * (q % 2 + 1), :], src).then_inc(band_loaded[q % 2], 16)

            def load_p(l):
                nc.gpsimd.dma_start(rowsP, A["p"][l, 0].rearrange("(t p) c -> p t c", p=P)).then_inc(p_loaded, 16)

            nc.gpsimd.memset(mhalf[:], -0.5).then_inc(pch, 1)
            for dst, src in PARS[NPAR0:]:
                nc.gpsimd.dma_start(dst, src).then_inc(par2_loaded, 16)
            for r, (wait, col, n, parts_n, width) in enumerate(ROOTS):
                for l in range(2):
                    if r == ROOT_AT[("head", l)]:
                        bands(l)
                        pool.wait_ge(o_ready, U_AT[l + 1])
                        load_p(l)
                if r == ROOT_AT[("norm", 0)]:
                    pool.wait_ge(trow_done, 2)
                    for m in range(2):
                        nc.gpsimd.dma_start(scr[NH * m:NH * (m + 1), :], trow[:, 512 * m:512 * (m + 1)]).then_inc(scr_written, 16)
                    pool.wait_ge(scr_written, 32)
                if r == ROOT_AT[("norm", 3)]:
                    for l in range(2):
                        nc.gpsimd.dma_start(wr[:, l, :, 0:NEG], A["w_router_group_2"][l].rearrange(
                            "(k p) n -> p k n", p=P)).then_inc(wr_loaded, 16)
                        nc.gpsimd.dma_start(wr[:, l, :, NEG:], A["w_router_expert_2"][l].rearrange(
                            "(k p) n -> p k n", p=P)).then_inc(wr_loaded, 16)
                if r == ROOT_AT[("norm", 4)] - 1:
                    pool.wait_ge(s_max, U_AT[2])
                    wb = A["window_band"]
                    nc.gpsimd.dma_start(band[:, 0, :], bass.AP(tensor=wb.tensor, offset=0, ap=[[1, P], [1, NB]]))\
                        .then_inc(band_loaded[0], 16)
                if r == ROOT_AT[("norm", 10)] - 1:
                    pool.wait_ge(yt_ready, 16)
                    nc.gpsimd.dma_start(gfin, A["norm_final_2"].rearrange("(a d) -> a d", a=1).broadcast_to([P, D]))\
                        .then_inc(gfin_loaded, 16)
                pool.wait_ge(*wait)
                a = rms[0:parts_n, col:col + n]
                nc.gpsimd.tensor_scalar(a, a, float(width * EPS), None, ALU.add).then_inc(pch, 1)
                pool.wait_ge(pch, r + 2)
                nc.gpsimd.tensor_tensor(a, a, mhalf[0:parts_n, 0:n], ALU.pow).then_inc(rstd_done, 1)

        @block.scalar
        def _(act):
            for dst, src in PARS[:NPAR0]:
                act.dma_start(dst, src).then_inc(par_loaded, 16)
            act.dma_start(cst[:], A["consts"]).then_inc(cst_loaded, 16)
            act.dma_start(oneh, A["onehot"]).then_inc(rel_loaded, 16)
            act.dma_start(tmask, A["row_masks"]).then_inc(rel_loaded, 16)
            act.dma_start(relb[:], A["rel_bias"]).then_inc(rel_loaded, 16)

            split = {0: 0, 2: 0}

            def split_to(seg, n):
                while split[seg] < min(n, len(splits[seg])):
                    k = split[seg]
                    _, _, place, _, (kk, nn) = stream[seg][splits[seg][k]]
                    i = splits[seg][k]
                    act.wait_ge(arrived[seg][place], 16 * (i // RAW + 1))
                    if k >= SPL:
                        act.wait_ge(used[seg], k - SPL + 1)
                    elif seg:
                        act.wait_ge(yt_ready, 8)
                    nc.scalar.activation(parts[:, (SPL0[seg] + k) % SPL, 0, 0:kk * nn], raw[:, place, 0:kk * nn],
                                         ACT.Copy).then_inc(hi_done[seg], 1)
                    split[seg] += 1

            def squares(n):
                if n:
                    act.wait_ge(h_done, 4 * n)
                else:
                    act.wait_ge(x_loaded, 16)
                for t in range(NT):
                    nc.scalar.activation(xs[:, t, :], h[:, t, :], ACT.Square,
                                         accum_out=rms[:, R_NORM[n] + t:R_NORM[n] + t + 1]).then_inc(sq_done, 1)

            def evac_tp(m):
                kind, n = TP[m]
                if m == 0:
                    act.wait_ge(set_done, 1)
                for c in range(TPN[m]):
                    act.wait_ge(tp_ready, (tp_chunks(m) + c) // 2 + 1)
                    src = pb[4 + c // 2][:, S * (c % 2):S * (c % 2 + 1)]
                    if kind == "attn":
                        i = nc.scalar.activation(xT[:, 0, c, :], src, ACT.Copy)
                    else:
                        col = G_NORM[n] if kind == "norm" else G_ATT + 4 * n
                        i = nc.scalar.activation(xT[:, 0, c, :], src, ACT.Copy, scale=gT[:, col + c:col + c + 1])
                    i.then_inc(xT_a, 1)

            def evac_proj(layer, hi):
                seg = SEG[layer]
                for g in range(PJ_AT[layer], hi):
                    halves, n, dst = PJ[g]
                    split_to(seg, halves[1] + 3)
                    act.wait_ge(pj_ready, g + 1)
                    d = qkv_t(0)[:, dst:dst + n] if layer < 2 else qkv2[:, 0, dst:dst + n]
                    nc.scalar.activation(d, pb[(2 * g) % 4][:, 0:n], ACT.Copy).then_inc(pj_a, 1)

            def head_squares(layer):
                act.wait_ge(pj_a, PJ_AT[layer + 1])
                act.wait_ge(pj_v, PJ_AT[layer + 1])
                for t in range(NT):
                    for part in range(2):
                        if t:
                            act.wait_ge(hss, 4 * layer + part + 1)
                        if layer == 0:
                            src, dst = qkv_t(t)[:, 1536 * part:1536 * part + D], xs[:, part, :]
                        elif part == 0:
                            src, dst = qkv_t(t)[:, 0:D], xs[:, 0, :]
                        else:
                            src = qkv_t(t)[:, 1536:2560].rearrange("p (b c) -> p b c", b=2)[:, :, 0:256]
                            dst = xs[:, 1, 0:512].rearrange("p (b c) -> p b c", b=2)
                        nc.scalar.activation(dst, src, ACT.Square).then_inc(hsq, 1)

            def evac_heads(layer):
                for z, (_, dst, gain) in enumerate(QT[layer]):
                    g = QT_AT[layer] + z
                    if z // 2 % 2 == 0:
                        act.wait_ge(qt_ready, g // 2 + 1)
                        src = pb[4 + (z // 2) % 4][:, S * (z % 2):S * (z % 2 + 1)]
                        if gain is None:
                            i = nc.scalar.activation(dst, src, ACT.Copy)
                        else:
                            i = nc.scalar.activation(dst, src, ACT.Copy, scale=g2T[:, gain:gain + 1])
                        i.then_inc(qt_a, 1)

            def attention(layer):
                us = UN[layer]
                for i in range(len(us) + 1):
                    if i < len(us):
                        u, g = us[i], U_AT[layer] + i
                        act.wait_ge(s_max, g + 1)
                        if layer >= 2:
                            c = U_AT[2]
                            nc.scalar.activation(esink[:, g - c:g - c + 1], sink[:, layer - 2, 0, u.h:u.h + 1], ACT.Exp,
                                                 bias=nmax[:, g:g + 1])
                        s = sbuf_s[:, g % 4, 0:u.nk]
                        nc.scalar.activation(s, s, ACT.Exp, scale=-1.0, bias=nmax[:, g:g + 1],
                                             accum_out=den[:, g:g + 1]).then_inc(e_done, 1)
                    if i >= 1:
                        u, g = us[i - 1], U_AT[layer] + i - 1
                        act.wait_ge(pt_ready, g + 1)
                        if g >= 4:
                            act.wait_ge(o_ready, g - 3)
                        n, kp = (P * len(u.v), P) if u.nk > NCMP else (P, NCMP)
                        nc.scalar.activation(
                            sbuf_p[0:kp, g % 4, 0:n], pb[2 + g % 2][0:kp, 0:n], ACT.Copy).then_inc(pt_done, 1)

            def ffn(f):
                for j in range(FJ):
                    g = FJ * f + j
                    q, odd = j // 2, j % 2
                    sg, su, sd = FFW[f][q]
                    split_to(0, sd + 1 if odd == 0 else su + 1)
                    if odd:
                        act.wait_ge(used[0], su + 1)
                    else:
                        act.wait_ge(gu_ready, g // 2 + 1)
                    if g >= 2:
                        act.wait_ge(hT_done, g - 1)
                    nc.scalar.activation(th[:, g % 2, :], pb[4 + g % 4][:, 0:S], ACT.Tanh, scale=0.5).then_inc(th_done, 1)
                    if odd:
                        split_to(0, su + 3)

            def out_splits(layer):
                split_to(SEG[layer], OPW[layer][1][1] + 1)

            def transpose_p(f):
                act.wait_ge(p_ready, f + 1)
                nc.scalar.activation(hidT[:, :, 0, :], pb[4][:].rearrange("p (a b) -> p a b", a=2), ACT.Copy)\
                    .then_inc(pT_done, 1)

            def ple(f):
                split_to(0, PLW[f][1][1][1] + 1)
                for c in range(2):
                    for t in range(NT):
                        if t:
                            act.wait_ge(used[0], PLW[f][1][c][1] + 1)
                        else:
                            act.wait_ge(ple_ready, 2 * f + c + 1)
                        nc.scalar.activation(xs[:, t, 512 * c:512 * (c + 1)], pb[4 + 2 * c + t][:], ACT.Tanh,
                                             scale=0.5).then_inc(ple_th, 1)

            def conv(l):
                seg = SEG[2 + l]
                for c in range(4):
                    split_to(seg, CVW[l][c // 2][c % 2] + 3)
                    act.wait_ge(used[seg], CVW[l][c // 2][c % 2] + 1)
                    dst = (gbT if c < 2 else gcT)[:, 512 * (c % 2):512 * (c % 2 + 1)]
                    nc.scalar.activation(dst, pb[4 + c][:], ACT.Copy).then_inc(gb_done, 1)
                split_to(seg, OPW[2 + l][0][1] + 2)
                act.wait_ge(y_done, l + 1)
                nc.scalar.activation(gcT, yT, ACT.Square).then_inc(ysq_done, 1)

            def moe(l):
                squares(7 + 2 * l)
                evac_tp(10 + 3 * l)
                act.wait_ge(rt_x, 2 * l + 1)
                nc.scalar.activation(rt[:, 112:120], rt[:, 112:120], ACT.Exp).then_inc(rt_e, 1)
                act.wait_ge(rt_x, 2 * l + 2)
                nc.scalar.activation(rt[:, 364:366], rt[:, 364:366], ACT.Exp).then_inc(rt_e, 1)
                col = G_NORM[7 + 2 * l]
                for k in range(0, KC, 2):
                    act.wait_ge(ga_ready, KC * l + k + 1)
                    nc.scalar.activation(xsT[:, k, 0:NS], pb[4 + k % 4][:], ACT.Copy,
                                         scale=gT[:, col + k:col + k + 1]).then_inc(xsT_a, 1)
                more = act.value_load(tab[0:1, 2 * JOBS:2 * JOBS + 1], min_val=NS // W - 2, max_val=JOBS - 2)
                seg = 2 * l + 1
                act.wait_ge(xsT_a, 4 * (l + 1))
                act.wait_ge(xsT_v, 5 * (l + 1))

                def window(j):
                    s0 = act.value_load(tab[0:1, bass.ds(at(j, 1, JOBS), 1)], min_val=0, max_val=NS)
                    if not isinstance(j, int):
                        act.wait_ge(used[seg], at(j, 6, -4))
                    elif j:
                        act.wait_ge(used[seg], 4)
                    nc.scalar.activation(xw[:, :, 0:W], xsT[:, :, bass.ds(s0, W)], ACT.Copy).then_inc(xw_rounded[l], 1)

                def round_half(j, q):
                    place = job_place(l, q)
                    act.wait_ge(arrived[seg][place], at(j, 16, 0 if q < 2 else 16))
                    if isinstance(j, int) and j == 0 and q < SPL + 2:
                        act.wait_ge(used[2 * l], len(splits[2 * l]) - SPL + q - 1)
                    else:
                        act.wait_ge(used[seg], at(j, 6, q - SPL - 1))
                    nc.scalar.activation(job_parts(l, q)[0], raw[:, place, :], ACT.Copy).then_inc(hi_done[seg], 1)

                def products(j, dst, done, bank, q):
                    act.wait_ge(used[seg], at(j, 6, q - 1))
                    nc.scalar.activation(dst, pb[bank][:], ACT.Copy).then_inc(done[l], 1)

                def first_parts(j, back, m, dst):
                    act.wait_ge(gt_ready[l], at(j, 2, m + 1 - 2 * back))
                    nc.scalar.activation(dst.rearrange("p (k s) -> p k s", k=4),
                                         pb[2 + m][:].rearrange("p (k i s) -> p k i s", k=4, i=2)[:, :, 0, :],
                                         ACT.Copy).then_inc(eg_first[l], 1)

                def tanh(j, back):
                    act.wait_ge(g_added[l], at(j, 1, 1 - back))
                    nc.scalar.activation(ea, eg, ACT.Tanh, scale=0.5).then_inc(eth_done[l], 1)

                def results(j, back):
                    act.wait_ge(used[seg], at(j, 6, -2 if back == 2 else 0))
                    for c in range(2):
                        nc.scalar.activation(ys[:, 512 * c:512 * (c + 1)], pb[4 + c][:], ACT.Copy).then_inc(ys_done[l], 1)

                def to_slots(j, back):
                    s0 = act.value_load(tab[0:1, bass.ds(at(j, 1, JOBS - back), 1)], min_val=0, max_val=NS)
                    for b in range(2):
                        act.wait_ge(yt2_ready[l], at(j, 2, b + 1 - 2 * back))
                        nc.scalar.activation(ysT[:, 4 * b:4 * b + 4, bass.ds(s0, W)],
                                             pb[6 + b][:].rearrange("p (k i s) -> p k i s", k=4, i=2)[:, :, 0, :],
                                             ACT.Copy).then_inc(y_first[l], 1)

                def step(j):
                    later = not isinstance(j, int)
                    g0, g1, u0, u1 = (q for q, _, _ in gate_up(j))
                    window(j)
                    round_half(j, g0)
                    round_half(j, g1)
                    if later:
                        results(j, 2)
                    round_half(j, u0)
                    if later or j:
                        first_parts(j, 1, 0, eg)
                        first_parts(j, 1, 1, eu)
                    round_half(j, u1)
                    if later or j:
                        tanh(j, 1)
                    if later:
                        to_slots(j, 2)
                    if later or j:
                        round_half(j, down_at(False))
                    products(j, gs, gs_done, 0, g1)
                    if later or j:
                        round_half(j, down_at(False) + 1)
                    products(j, us, us_done, 1, u1)

                step(0)
                step(1)
                with act.Fori(0, more) as j:
                    step(j)
                results(more, 2)
                first_parts(more, 1, 0, eg)
                first_parts(more, 1, 1, eu)
                tanh(more, 1)
                round_half(more, down_at(True))
                round_half(more, down_at(True) + 1)
                to_slots(more, 2)
                results(more, 1)
                to_slots(more, 1)
                for i in range(0, 8, 2):
                    act.wait_ge(yt_ready, 8 * l + i + 1)
                    nc.scalar.activation(ysort[:, i // 2, 0:512], pb[4 + i % 4][:], ACT.Copy).then_inc(yt_done, 1)

            squares(0)
            evac_tp(0)
            evac_proj(0, PJ_AT[1])
            split_to(0, OPW[0][0][0] + SPL)
            head_squares(0)
            act.wait_ge(scr_written, 32)
            evac_heads(0)
            attention(0)
            evac_tp(1)
            out_splits(0)
            squares(1)
            evac_tp(2)
            ffn(0)
            transpose_p(0)
            squares(2)
            evac_tp(3)
            ple(0)
            squares(3)
            evac_tp(4)
            evac_proj(1, PJ_AT[2])
            split_to(0, OPW[1][0][0] + RAW - 4)
            for kv in range(2):
                act.wait_ge(gel_in, kv + 1)
                nc.scalar.activation(cmph[:, kv, 2, 0:60], cmph[:, kv, 1, 0:60], ACT.Tanh, scale=GELU).then_inc(gel_th, 1)
            head_squares(1)
            evac_heads(1)
            for t in range(NT):
                nc.scalar.activation(gates[:, t, :], qkv_t(t)[:, 2560:2608], ACT.Tanh, scale=0.5).then_inc(g_th, 1)
            attention(1)
            evac_tp(5)
            out_splits(1)
            squares(4)
            evac_tp(6)
            ffn(1)
            transpose_p(1)
            squares(5)
            evac_tp(7)
            ple(1)
            for l in range(2):
                squares(6 + 2 * l)
                evac_tp(8 + 3 * l)
                evac_proj(2 + l, PJ_AT[2 + l] + 2)
                conv(l)
                evac_heads(2 + l)
                attention(2 + l)
                for t in range(NT):
                    act.wait_ge(o_done, U_AT[3 + l])
                    nc.scalar.activation(sbuf_s[:, 2 * t:2 * t + 2, :], xs[:, t, 0:CW].rearrange("p (a b) -> p a b", a=2),
                                         ACT.Square, accum_out=rms[:, R_ATT[l] + t:R_ATT[l] + t + 1]).then_inc(on_ready, 1)
                evac_tp(9 + 3 * l)
                out_splits(2 + l)
                moe(l)
            squares(10)

        @block.tensor
        def _(pe):
            mm = nc.tensor.matmul
            pe.wait_ge(cst_loaded, 16)
            pe.wait_ge(par_loaded, 16 * NPAR0)
            nc.tensor.transpose(pb[0][:, 0:PRM_ROWS], prm[0:PRM_ROWS, 0, :], ident[0:PRM_ROWS, 0:PRM_ROWS])\
                .then_inc(set_ready, 1)

            def setup_rest():
                pe.wait_ge(rel_loaded, 48)
                mm(pb[1][0:NH, :], relb[:], oneh, start=True, stop=True).then_inc(set_ready, 1)
                pe.wait_ge(par2_loaded, 16 * (len(PARS) - NPAR0))
                nc.tensor.transpose(pb[2][:, 0:HEAD_ROWS], prm[0:HEAD_ROWS, 1, :], ident[0:HEAD_ROWS, 0:HEAD_ROWS])\
                    .then_inc(set_ready, 1)

            def three(out_ap, x, w, k, kw, xcols, wcols, first, last, flip=False):
                for n, (i, j) in enumerate(((0, 0), (1, 0), (0, 1))):
                    a, b = x[:, i, k, xcols], w[j][:, kw, wcols]
                    ins = mm(out_ap, b if flip else a, a if flip else b, start=first and n == 0, stop=last and n == 2)
                return ins

            def transposes(m):
                kind, n = TP[m]
                if kind == "norm":
                    pe.wait_ge(xs_ready, 2 * n + 2)
                elif kind == "attn":
                    pe.wait_ge(o_done, U_AT[n + 1])
                else:
                    pe.wait_ge(at_ready, 2 * n + 2)
                for c in range(TPN[m]):
                    b = pb[4 + c // 2]
                    for t in range(NT):
                        i = nc.tensor.transpose(b[:, S * (c % 2) + P * t:S * (c % 2) + P * (t + 1)],
                                                xs[:, t, P * c:P * (c + 1)], ident)
                    if c % 2:
                        i.then_inc(tp_ready, 1)

            def wait_xT(m):
                pe.wait_ge(xT_v, tp_chunks(m + 1))

            def project(layer, m):
                wait_xT(m)
                seg = SEG[layer]
                if layer == 0:
                    pe.wait_ge(set_done, 3)
                for g in range(PJ_AT[layer], PJ_AT[layer] + (6 if layer < 2 else 2)):
                    halves, n, _ = PJ[g]
                    for hf, s in enumerate(halves):
                        pe.wait_ge(lo_done[seg], s + 1)
                        w = both(seg, s)
                        for t in range(NT):
                            if g >= 2 and hf == 0:
                                pe.wait_ge(pj_v if t else pj_a, g - 1)
                            for k in range(4):
                                ins = three(pb[(2 * g + t) % 4][:, 0:n], xT, w, 4 * hf + k, k, slice(P * t, P * (t + 1)),
                                            slice(0, n), hf == 0 and k == 0, hf == 1 and k == 3)
                            if t:
                                ins.then_inc(used[seg], 1)
                            elif hf:
                                ins.then_inc(pj_ready, 1)

            def heads(layer):
                for z, (src, _, _) in enumerate(QT[layer]):
                    if z in (0, 8) and layer < 2 or z == 0:
                        pe.wait_ge(qn_ready, sum(QN[:layer]) + QN[layer])
                    if z >= 8 and z % 2 == 0:
                        if z // 2 % 2 == 0:
                            pe.wait_ge(qt_a, QT_A[layer] + z // 2 - 2)
                        else:
                            pe.wait_ge(qt_v, QT_V[layer] + z // 2 - 3)
                    b = pb[4 + (z // 2) % 4]
                    for t in range(NT):
                        i = nc.tensor.transpose(b[:, S * (z % 2) + P * t:S * (z % 2) + P * (t + 1)], src[t], ident)
                    if z % 2:
                        i.then_inc(qt_ready, 1)

            def attention(layer):
                us = UN[layer]
                pe.wait_ge(qt_a, QT_A[layer + 1])
                pe.wait_ge(qt_v, QT_V[layer + 1])
                if layer == 1:
                    pe.wait_ge(cmpT_done, 1)
                n = len(us)
                for i in range(n + 3):
                    if i < n:
                        u, g = us[i], U_AT[layer] + i
                        if g >= 3:
                            pe.wait_ge(s_max, g - 2)
                        mm(pb[4 + g % 3][:, 0:u.nk], u.q, u.k, start=True, stop=True).then_inc(s_ready, 1)
                    if 0 <= i - 2 < n:
                        u, g = us[i - 2], U_AT[layer] + i - 2
                        pe.wait_ge(e_done, g + 1)
                        if g >= 2:
                            pe.wait_ge(pt_done, g - 1)
                        if u.nk == NCMP:
                            ins = nc.tensor.transpose(pb[2 + g % 2][0:NCMP, 0:P], sbuf_s[:, g % 4, 0:NCMP], ident)
                        else:
                            for kt in range(len(u.v)):
                                ins = nc.tensor.transpose(pb[2 + g % 2][:, P * kt:P * (kt + 1)],
                                                          sbuf_s[:, g % 4, P * kt:P * (kt + 1)], ident)
                        ins.then_inc(pt_ready, 1)
                    if 0 <= i - 3 < n:
                        u, g = us[i - 3], U_AT[layer] + i - 3
                        pe.wait_ge(pt_done, g + 1)
                        if g >= 2:
                            pe.wait_ge(o_done, g - 1)
                        ob = pb[g % 2][:, 0:HD]
                        kp = P if u.nk > NCMP else NCMP
                        for kt in range(len(u.v)):
                            ins = mm(ob, sbuf_p[0:kp, g % 4, P * kt:P * (kt + 1)], u.v[kt],
                                     start=(kt == 0), stop=(kt == len(u.v) - 1))
                        ins.then_inc(o_ready, 1)

            def out_proj(k, m):
                wait_xT(m)
                seg = SEG[k]
                if k >= 2:
                    pe.wait_ge(cx_done, 8 * (k - 1))
                for c in range(2):
                    for hf, s in enumerate(OPW[k][c]):
                        pe.wait_ge(lo_done[seg], s + 1)
                        w = both(seg, s)
                        apart = k >= 2
                        for t in range(NT):
                            b = pb[2 * c + t + (4 * hf if apart else 0)]
                            for kk in range(4):
                                ins = three(b[:], xT, w, 4 * hf + kk, kk, slice(P * t, P * (t + 1)), slice(0, 512),
                                            kk == 0 and (hf == 0 or apart), kk == 3 and (hf == 1 or apart))
                            if t:
                                ins.then_inc(used[seg], 1)
                            elif hf:
                                ins.then_inc(op_ready, 1)

            def ffn(f, m):
                wait_xT(m)

                def down(j):
                    g = FJ * f + j
                    sd = FFW[f][j // 2][2]
                    pe.wait_ge(lo_done[0], sd + 1)
                    pe.wait_ge(hT_done, g + 1)
                    w = both(0, sd)
                    x = hidT[:, g % 2, :, :]
                    for t in range(NT):
                        for c in range(2):
                            for n, (i, p) in enumerate(((0, 0), (1, 0), (0, 1))):
                                ins = mm(pb[2 * c + t][:], x[:, i, P * t:P * (t + 1)], w[p][:, j % 2, 512 * c:512 * (c + 1)],
                                         start=(j == 0 and n == 0), stop=(j == FJ - 1 and n == 2))
                    ins.then_inc(used[0] if j % 2 else dn_done, 1)

                for j in range(FJ):
                    g = FJ * f + j
                    if g >= 4:
                        pe.wait_ge(hT_done, g - 3)
                    for half in range(2):
                        s = FFW[f][j // 2][half]
                        pe.wait_ge(lo_done[0], s + 1)
                        for k in range(KC):
                            ins = three(pb[4 + g % 4][:, S * half:S * (half + 1)], xT, both(0, s), k, k, slice(0, S),
                                        slice(P * (j % 2), P * (j % 2 + 1)), k == 0, k == KC - 1, flip=True)
                        if j % 2:
                            ins.then_inc(used[0], 1)
                        elif half:
                            ins.then_inc(gu_ready, 1)
                    if j:
                        down(j - 1)
                down(FJ - 1)

            def p_rows(f):
                pe.wait_ge(p_loaded, 16 * (f + 1))
                pe.wait_ge(hT_done, FJ * (f + 1))
                for k in range(2):
                    for t in range(NT):
                        ins = nc.tensor.transpose(pb[4][:, S * k + P * t:S * k + P * (t + 1)],
                                                  rowsP[:, t, P * k:P * (k + 1)], ident)
                ins.then_inc(p_ready, 1)

            def p_proj(f):
                pe.wait_ge(pT_v, f + 1)
                pe.wait_ge(h_done, 4 * (3 * f + 2))
                s = PLW[f][0]
                pe.wait_ge(lo_done[0], s + 1)
                w = both(0, s)
                for c in range(2):
                    for t in range(NT):
                        for k in range(2):
                            for n, (i, p) in enumerate(((0, 0), (1, 0), (0, 1))):
                                ins = mm(pb[2 * c + t][:], hidT[:, k, i, P * t:P * (t + 1)], w[p][:, k, 512 * c:512 * (c + 1)],
                                         start=(k == 0 and n == 0), stop=(k == 1 and n == 2))
                ins.then_inc(used[0], 1)

            def ple(f, m):
                wait_xT(m)
                for c in range(2):
                    for hf, s in enumerate(PLW[f][1][c]):
                        pe.wait_ge(lo_done[0], s + 1)
                        for t in range(NT):
                            for k in range(4):
                                ins = three(pb[4 + 2 * c + t][:], xT, both(0, s), 4 * hf + k, k, slice(P * t, P * (t + 1)),
                                            slice(0, 512), hf == 0 and k == 0, hf == 1 and k == 3)
                            if t:
                                ins.then_inc(used[0], 1)
                            elif hf:
                                ins.then_inc(ple_ready, 1)

            def compress():
                pe.wait_ge(pj_a, PJ_AT[2])
                pe.wait_ge(pj_v, PJ_AT[2])
                for kv in range(2):
                    for g in range(NG):
                        b = pb[4 + 2 * kv + g // 2]
                        for t in range(NT):
                            c0 = 1024 + 256 * kv + HD * g
                            ins = nc.tensor.transpose(b[0:HD, S * (g % 2) + P * t:S * (g % 2) + P * (t + 1)],
                                                      qkv_t(t)[:, c0:c0 + HD], ident)
                ins.then_inc(cT_ready, 1)
                pe.wait_ge(cT_done, 1)
                for kv in range(2):
                    for i in CMPW[kv]:
                        pe.wait_ge(arrived[0][stream[0][i][2]], 16 * (i // RAW + 1))
                    w1 = [stream[0][i][0] for i in CMPW[kv]]
                    for l in range(CMP_LEN):
                        mm(pb[kv][:, 0:60], w1[l // 16][:, l % 16, :], view(cT[:, 4 * kv, :], l, [[S, NG], [CMP_STRIDE, NCMP]]),
                           start=(l == 0), stop=(l == CMP_LEN - 1))
                    for l in range(CMP_LEN):
                        ins = mm(pb[kv][:, 64:65], w1[l // 16][:, l % 16, :], g2T[0:HD, H_POS + 32 * kv + l:H_POS + 32 * kv + l + 1],
                                 start=(l == 0), stop=(l == CMP_LEN - 1))
                    ins.then_inc(hid_ready, 1)
                for kv in range(2):
                    pe.wait_ge(gel_done, kv + 1)
                    for g in range(NG):
                        ins = mm(pb[2][0:NCMP, 256 * kv + HD * g:256 * kv + HD * (g + 1)],
                                 cmph[:, kv, 3, NCMP * g:NCMP * (g + 1)], w2[:, kv, :], start=True, stop=True)
                ins.then_inc(cmp_ready, 1)
                pe.wait_ge(cmpn_done, 2)
                for g in range(NG):
                    ins = nc.tensor.transpose(pb[3][:, 16 * g:16 * g + NCMP],
                                              cmpd[0:NCMP, g, :, :].rearrange("p a b -> p (a b)"), ident[0:NCMP, 0:NCMP])
                ins.then_inc(cmpT_ready, 1)

            def conv(l):
                seg = SEG[2 + l]
                for c in range(3):
                    for half in range(2):
                        s = CVW[l][c][half]
                        pe.wait_ge(lo_done[seg], s + 1)
                        if c == 2:
                            pe.wait_ge(gb_done, 4 * l + half + 1)
                        b = pb[4 + (2 * c + half) % 4]
                        for q in range(2):
                            for k in range(KC):
                                ins = three(b[:, S * q:S * (q + 1)], xT, both(seg, s), k, k, slice(0, S),
                                            slice(P * q, P * (q + 1)), k == 0, k == KC - 1, flip=True)
                        ins.then_inc(used[seg], 1)

            def conv_sums(l):
                pe.wait_ge(ysq_done, l + 1)
                for t in range(NT):
                    for c in range(4):
                        ins = mm(pb[7][:, t:t + 1], gcT[:, S * c + P * t:S * c + P * (t + 1)], ones[:, 0:1],
                                 start=(c == 0), stop=(c == 3))
                ins.then_inc(yss_ready, 1)

            def moe(l):
                transposes(10 + 3 * l)
                wait_xT(10 + 3 * l)
                pe.wait_ge(wr_loaded, 64)
                for t in range(NT):
                    for k in range(KC):
                        for i in range(2):
                            ins = mm(pb[0][:, 64 * t:64 * t + 36], xT[:, i, k, P * t:P * (t + 1)].bitcast(F32), wr[:, l, k, :],
                                     start=(k == 0 and i == 0), stop=(k == KC - 1 and i == 1))
                ins.then_inc(rt_ready, 1)
                a = [rt[:, 384 + NE * t:384 + NE * (t + 1)] for t in range(NT)]
                pe.wait_ge(as_done, l + 1)
                for t in range(NT):
                    ins = mm(pb[1][0:NE, 0:P], a[t], ones[:], start=(t == 0), stop=(t == 1))
                ins.then_inc(cnt_ready, 1)
                mm(pb[2][:, 0:NE], tri, a[0], start=True, stop=True)
                mm(pb[2][:, NE:2 * NE], ones[:], a[0], start=True, stop=False)
                mm(pb[2][:, NE:2 * NE], tri, a[1], start=False, stop=True)
                pe.wait_ge(cnt_done, 2 * l + 2)
                cm, wm = rt[0:NE, 512:640], rt[0:NE, 640:768]
                mm(pb[3][:, 0:NE], cm, tri[0:NE, 0:NE], start=True, stop=True)
                mm(pb[3][0:NE, NE:NE + 1], tri[0:NE, 0:NE], cm[:, 0:1], start=True, stop=True)
                mm(pb[3][0:NE, NE + 1:NE + 2], tri[0:NE, 0:NE], wm[:, 0:1], start=True, stop=True)\
                    .then_inc(pos_ready, 1)
                pe.wait_ge(job_cols, l + 1)
                ja, jo, jv = jobs_work()
                mm(pb[1][0:1, 0:JOBS], ones[0:NE, 0:1], ja, start=True, stop=True)
                mm(pb[1][0:1, 64:64 + JOBS], jv, jo, start=True, stop=True)
                mm(pb[1][0:1, 128:129], wm[:, 0:1], ones[0:NE, 0:1], start=True, stop=True).then_inc(job_ready, 1)
                pe.wait_ge(sel_done, 2 * l + 1)
                for k in range(KC):
                    if k >= 4:
                        if k % 2:
                            pe.wait_ge(xsT_v, 5 * l + 2 + (k - 4) // 2)
                        else:
                            pe.wait_ge(xsT_a, 4 * l + 1 + (k - 4) // 2)
                    for t in range(NT):
                        ins = mm(pb[4 + k % 4][:], xs[:, t, P * k:P * (k + 1)], sel[:, t, :],
                                 start=(t == 0), stop=(t == 1))
                    ins.then_inc(ga_ready, 1)
                pe.wait_ge(sel_done, 2 * l + 2)
                for c in range(4):
                    b = pb[c // 2]
                    for t in range(NT):
                        ins = nc.tensor.transpose(b[:, S * (c % 2) + P * t:S * (c % 2) + P * (t + 1)],
                                                  gsel[:, t, P * c:P * (c + 1)], ident)
                    if c % 2:
                        ins.then_inc(gct_ready, 1)
                pe.wait_ge(gct_done, 2 * l + 2)
                seg = 2 * l + 1
                more = pe.value_load(tab[0:1, 2 * JOBS:2 * JOBS + 1], min_val=NS // W - 2, max_val=JOBS - 2)

                def products(j, q, m, hf):
                    pe.wait_ge(lo_done[seg], at(j, 6, q - 1))
                    w = job_parts(l, q, SHAPES[m])
                    for k in range(4):
                        for i in range(2):
                            ins = mm(pb[m][:], xw[:, 4 * hf + k, :], w[i][:, k, :], start=(hf == 0 and k == 0 and i == 0),
                                     stop=(hf == 1 and k == 3 and i == 1))
                    ins.then_inc(used[seg], 1)

                def turn(j, back, m, src, done):
                    pe.wait_ge(done[l], at(j, 1, 1 - back))
                    for q in range(4):
                        ins = nc.tensor.transpose(pb[2 + m][:, P * q:P * (q + 1)], src[:, P * q:P * (q + 1)], ident)
                    ins.then_inc(gt_ready[l], 1)

                def results(j, back):
                    pe.wait_ge(yadd_done[l], at(j, 2, 1 - 2 * back))
                    for b in range(2):
                        pe.wait_ge(ys_done[l], at(j, 2, b + 1 - 2 * back))
                        for q in range(4):
                            ins = nc.tensor.transpose(pb[6 + b][:, P * q:P * (q + 1)], ys[:, 512 * b + P * q:512 * b + P * (q + 1)],
                                                      ident)
                        ins.then_inc(yt2_ready[l], 1)

                def down(j, back, q0):
                    pe.wait_ge(eh_done[l], at(j, 1, 1 - back))
                    for hf in range(2):
                        pe.wait_ge(lo_done[seg], at(j, 6, q0 + hf - 1))
                        w = job_parts(l, q0 + hf, SHAPES[2])
                        for k in range(2):
                            for i in range(2):
                                for c in range(2):
                                    ins = mm(pb[4 + c][:], ehl[:, 2 * hf + k, :], w[i][:, k, 512 * c:512 * (c + 1)],
                                             start=(hf == 0 and k == 0 and i == 0), stop=(hf == 1 and k == 1 and i == 1))
                        ins.then_inc(used[seg], 1)

                def step(j):
                    later = not isinstance(j, int)
                    halves = gate_up(j)
                    pe.wait_ge(xw_ready[l], at(j, 1, 1))
                    if later or j:
                        turn(j, 1, 0, gs, gs_done)
                    products(j, *halves[0])
                    if later or j:
                        turn(j, 1, 1, us, us_done)
                    products(j, *halves[1])
                    if later:
                        results(j, 2)
                    products(j, *halves[2])
                    products(j, *halves[3])
                    if later or j:
                        down(j, 1, down_at(False))

                step(0)
                step(1)
                with pe.Fori(0, more) as j:
                    step(j)
                turn(more, 1, 0, gs, gs_done)
                turn(more, 1, 1, us, us_done)
                results(more, 2)
                down(more, 1, down_at(True))
                results(more, 1)
                pe.wait_ge(yadd_done[l], at(more, 2, 1))
                for c in range(4):
                    for half in range(2):
                        i = 2 * c + half
                        if i >= 4:
                            pe.wait_ge(yt_done if half == 0 else yt_v, 4 * l + (i - 4) // 2 + 1)
                        for kk in range(4):
                            ins = nc.tensor.transpose(pb[4 + i % 4][:, P * kk:P * (kk + 1)],
                                                      ysT[:, 4 * half + kk, P * c:P * (c + 1)], ident)
                        ins.then_inc(yt_ready, 1)
                pe.wait_ge(yt_done, 4 * l + 4)
                pe.wait_ge(yt_v, 4 * l + 4)
                for c in range(2):
                    for t in range(NT):
                        for sc in range(4):
                            ins = mm(pb[2 * c + t][:], gcombT[:, sc, P * t:P * (t + 1)], ysort[:, sc, 512 * c:512 * (c + 1)],
                                     start=(sc == 0), stop=(sc == 3))
                        ins.then_inc(op_ready2, 1)

            transposes(0)
            setup_rest()
            project(0, 0)
            heads(0)
            attention(0)
            transposes(1)
            out_proj(0, 1)
            transposes(2)
            ffn(0, 2)
            p_rows(0)
            p_proj(0)
            transposes(3)
            ple(0, 3)
            transposes(4)
            project(1, 4)
            compress()
            heads(1)
            attention(1)
            transposes(5)
            out_proj(1, 5)
            transposes(6)
            ffn(1, 6)
            p_rows(1)
            p_proj(1)
            transposes(7)
            ple(1, 7)
            for l in range(2):
                transposes(8 + 3 * l)
                project(2 + l, 8 + 3 * l)
                conv(l)
                conv_sums(l)
                heads(2 + l)
                attention(2 + l)
                transposes(9 + 3 * l)
                out_proj(2 + l, 9 + 3 * l)
                moe(l)

        @block.vector
        def _(dve):
            v = nc.vector
            chain = [0]

            def link(ins):
                chain[0] += 1
                ins.then_inc(dch, 1)
                dve.wait_ge(dch, chain[0])

            def root_wait(key):
                dve.wait_ge(rstd_done, ROOT_AT[key])

            def bc(ap, dims):
                return view(ap, 0, dims)

            link(v.memset(ones[:], 1.0))
            dve.wait_ge(set_ready, 1)
            v.tensor_copy(gT[:], pb[0][:, 0:PRM_ROWS]).then_inc(set_done, 1)

            def setup_rest():
                dve.wait_ge(set_ready, 2)
                for m in range(2):
                    v.scalar_tensor_tensor(trow[:, 512 * m:512 * (m + 1)], pb[1][0:NH, :], 8.0,
                                           tmask[:, 512 * m:512 * (m + 1)], ALU.mult, ALU.add).then_inc(trow_done, 1)
                dve.wait_ge(set_ready, 3)
                v.tensor_scalar(g2T[:, 0:H_POS], pb[2][:, 0:H_POS], 8.0, None, ALU.mult).then_inc(set_done, 1)
                v.tensor_copy(g2T[:, H_POS:], pb[2][:, H_POS:HEAD_ROWS]).then_inc(set_done, 1)
                link(v.tensor_scalar(sink[:, :, 1, :], sink[:, :, 0, :], -1.0, None, ALU.mult))

            split = {0: 0, 2: 0}

            def split_to(seg, n):
                while split[seg] < min(n, len(splits[seg])):
                    k = split[seg]
                    _, _, place, _, (kk, nn) = stream[seg][splits[seg][k]]
                    dve.wait_ge(hi_done[seg], k + 1)
                    two = parts[:, (SPL0[seg] + k) % SPL, :, 0:kk * nn]
                    v.tensor_tensor(two[:, 1, :], raw[:, place, 0:kk * nn], two[:, 0, :].bitcast(F32), ALU.subtract)\
                        .then_inc(lo_done[seg], 1)
                    split[seg] += 1

            def normalise(n):
                root_wait(("norm", n))
                for t in range(NT):
                    v.tensor_scalar(xs[:, t, :], h[:, t, :], rms[:, R_NORM[n] + t:R_NORM[n] + t + 1], float(D ** 0.5),
                                    ALU.mult, ALU.mult).then_inc(xs_ready, 1)

            def evac_tp(m):
                kind, n = TP[m]
                for c in range(TPN[m]):
                    dve.wait_ge(xT_a, tp_chunks(m) + c // 2 * 2 + 2)
                    src = pb[4 + c // 2][:, S * (c % 2):S * (c % 2 + 1)]
                    hi = xT[:, 0, c, :].bitcast(F32)
                    if kind == "attn":
                        i = v.tensor_tensor(xT[:, 1, c, :], src, hi, ALU.subtract)
                    else:
                        col = G_NORM[n] if kind == "norm" else G_ATT + 4 * n
                        i = v.scalar_tensor_tensor(xT[:, 1, c, :], src, gT[:, col + c:col + c + 1], hi, ALU.mult, ALU.subtract)
                    i.then_inc(xT_v, 1)

            def evac_proj(layer, hi):
                seg = SEG[layer]
                for g in range(PJ_AT[layer], hi):
                    halves, n, dst = PJ[g]
                    split_to(seg, halves[1] + 3)
                    dve.wait_ge(used[seg], halves[1] + 1)
                    d = qkv_t(1)[:, dst:dst + n] if layer < 2 else qkv2[:, 1, dst:dst + n]
                    v.tensor_copy(d, pb[(2 * g + 1) % 4][:, 0:n]).then_inc(pj_v, 1)

            def head_norms(layer):
                base = R_HEAD[layer]
                per = 32 if layer == 0 else 24
                for t in range(NT):
                    for part in range(2):
                        dve.wait_ge(hsq, 4 * layer + 2 * t + part + 1)
                        nh = 16 if layer == 0 or part == 0 else 8
                        c0 = base + per * t + 16 * part
                        v.tensor_reduce(rms[:, c0:c0 + nh], xs[:, part, 0:HD * nh].rearrange("p (a b) -> p a b", b=HD),
                                        AX, ALU.add).then_inc(hss, 1)
                root_wait(("head", layer))
                for t in range(NT):
                    r = rms[:, base + per * t:base + per * (t + 1)]
                    if layer == 0:
                        for part in range(2):
                            x = qkv_t(t)[:, 1536 * part:1536 * part + D].rearrange("p (a b) -> p a b", b=HD)
                            v.tensor_tensor(x, x, view(r, 16 * part, [[1, 16], [0, HD]]), ALU.mult).then_inc(qn_ready, 1)
                    else:
                        x = qkv_t(t)[:, 0:D].rearrange("p (a b) -> p a b", b=HD)
                        v.tensor_tensor(x, x, view(r, 0, [[1, 16], [0, HD]]), ALU.mult).then_inc(qn_ready, 1)
                        for br in range(2):
                            kx = view(qkv_t(t), 1536 + 512 * br, [[HD, NG], [1, HD]])
                            for twice in range(2):
                                v.tensor_tensor(view(xs[:, t, :], 512 * br + HD * twice, [[2 * HD, NG], [1, HD]]), kx,
                                                view(r, 16 + 4 * br, [[1, NG], [0, HD]]), ALU.mult).then_inc(qn_ready, 1)

            def evac_heads(layer):
                for z, (_, dst, gain) in enumerate(QT[layer]):
                    if z // 2 % 2:
                        dve.wait_ge(qt_ready, (QT_AT[layer] + z) // 2 + 1)
                        src = pb[4 + (z // 2) % 4][:, S * (z % 2):S * (z % 2 + 1)]
                        if gain is None:
                            i = v.tensor_copy(dst, src)
                        else:
                            i = v.tensor_scalar(dst, src, g2T[:, gain:gain + 1], None, ALU.mult)
                        i.then_inc(qt_v, 1)

            def attention(layer):
                us = UN[layer]
                n = len(us)
                if layer == 2:
                    dve.wait_ge(band_loaded[0], 16 * (NH // 4 + 1))
                for i in range(n + 4):
                    if i < n:
                        u, g = us[i], U_AT[layer] + i
                        if layer < 2 and u.t == 0 and u.br == 0 and u.h % 4 == 0:
                            dve.wait_ge(band_loaded[u.h // 4 % 2], 16 * (2 * layer + u.h // 8 + 1))
                        dve.wait_ge(s_ready, g + 1)
                        if g >= 4:
                            dve.wait_ge(pt_ready, g - 3)
                        init = BIG if layer < 2 else sink[:, layer - 2, 1, u.h:u.h + 1]
                        v.tensor_tensor_reduce(sbuf_s[:, g % 4, 0:u.nk], pb[4 + g % 3][:, 0:u.nk], u.bias, -0.125, init,
                                               ALU.add, ALU.min, nmax[:, g:g + 1]).then_inc(s_max, 1)
                    if i >= 4:
                        u, g = us[i - 4], U_AT[layer] + i - 4
                        dve.wait_ge(e_done, g + 1)
                        r = rec[:, g % 4:g % 4 + 1]
                        if layer >= 2:
                            c = g - U_AT[2]
                            link(v.tensor_tensor(den[:, g:g + 1], den[:, g:g + 1], esink[:, c:c + 1], ALU.add))
                        link(v.reciprocal(r, den[:, g:g + 1]))
                        ob = pb[g % 2][:, 0:HD]
                        dve.wait_ge(o_ready, g + 1)
                        if layer != 1:
                            v.tensor_scalar(u.o, ob, r, None, ALU.mult).then_inc(o_done, 1)
                            continue
                        gate = gates[:, u.t, 3 * u.h + (1, 2, 0)[u.br]:][:, 0:1]
                        if u.br == 0:
                            v.tensor_scalar(u.o, ob, r, gate, ALU.mult, ALU.mult).then_inc(o_done, 1)
                        else:
                            link(v.tensor_tensor(r, r, gate, ALU.mult))
                            dve.wait_ge(o_done, g)
                            v.scalar_tensor_tensor(u.o, ob, r, u.o, ALU.mult, ALU.add).then_inc(o_done, 1)

            def residual(ready, first):
                for c in range(2):
                    for t in range(NT):
                        dve.wait_ge(ready, first + 2 * c + t + 1)
                        hh = h[:, t, 512 * c:512 * (c + 1)]
                        v.tensor_tensor(hh, hh, pb[2 * c + t][:], ALU.add).then_inc(h_done, 1)

            def out_residual(k):
                for c in range(2):
                    split_to(0, OPW[k][c][1] + 3 if c == 0 else OPW[k][1][1] + 1)
                    for t in range(NT):
                        if t:
                            dve.wait_ge(used[0], OPW[k][c][1] + 1)
                        else:
                            dve.wait_ge(op_ready, 2 * k + c + 1)
                        hh = h[:, t, 512 * c:512 * (c + 1)]
                        v.tensor_tensor(hh, hh, pb[2 * c + t][:], ALU.add).then_inc(h_done, 1)

            def ffn(f):
                for j in range(FJ):
                    g = FJ * f + j
                    q, odd = j // 2, j % 2
                    sg, su, sd = FFW[f][q]
                    b = pb[4 + g % 4]
                    split_to(0, sd + 1 if odd == 0 else su + 1)
                    dve.wait_ge(th_done, g + 1)
                    link(v.scalar_tensor_tensor(ga[:, g % 2, :], th[:, g % 2, :], 1.0, b[:, 0:S], ALU.add, ALU.mult))
                    link(v.scalar_tensor_tensor(fh[:, g % 2, :], ga[:, g % 2, :], 0.5, b[:, S:2 * S], ALU.mult, ALU.mult))
                    if j >= 2:
                        if odd:
                            dve.wait_ge(used[0], FFW[f][q - 1][2] + 1)
                        else:
                            dve.wait_ge(dn_done, (FJ // 2) * f + q)
                    x = hidT[:, g % 2, :, :]
                    link(v.tensor_copy(x[:, 0, :], fh[:, g % 2, :]))
                    v.tensor_tensor(x[:, 1, :], fh[:, g % 2, :], x[:, 0, :].bitcast(F32), ALU.subtract).then_inc(hT_done, 1)
                    if odd:
                        split_to(0, su + 3)
                dve.wait_ge(used[0], FFW[f][-1][2] + 1)
                for c in range(2):
                    for t in range(NT):
                        hh = h[:, t, 512 * c:512 * (c + 1)]
                        v.tensor_tensor(hh, hh, pb[2 * c + t][:], ALU.add).then_inc(h_done, 1)

            def transpose_p(f):
                dve.wait_ge(pT_done, f + 1)
                v.tensor_tensor(hidT[:, :, 1, :], pb[4][:].rearrange("p (a b) -> p a b", a=2), hidT[:, :, 0, :].bitcast(F32),
                                ALU.subtract).then_inc(pT_v, 1)

            def ple(f):
                split_to(0, PLW[f][1][1][1] + 1)
                for c in range(2):
                    for t in range(NT):
                        dve.wait_ge(ple_th, 4 * f + 2 * c + t + 1)
                        x = xs[:, t, 512 * c:512 * (c + 1)]
                        hh = h[:, t, 512 * c:512 * (c + 1)]
                        link(v.scalar_tensor_tensor(x, x, 1.0, pb[2 * c + t][:], ALU.add, ALU.mult))
                        v.scalar_tensor_tensor(hh, x, 0.5, hh, ALU.mult, ALU.add).then_inc(h_done, 1)

            def compress():
                dve.wait_ge(cT_ready, 1)
                for kv in range(2):
                    for half in range(2):
                        i = v.tensor_copy(cT[:, 4 * kv + 2 * half:4 * kv + 2 * half + 2, :],
                                          pb[4 + 2 * kv + half][0:HD, :].rearrange("p (a b) -> p a b", a=2))
                        if kv * half == 0:
                            link(i)
                i.then_inc(cT_done, 1)
                x = [cmph[:, kv, 0, 0:60] for kv in range(2)]
                for kv in range(2):
                    dve.wait_ge(hid_ready, kv + 1)
                    hb = cmph[:, kv, 0, 60:61]
                    link(v.tensor_tensor(hb, pb[kv][:, 64:65], gT[:, G_B1 + kv:G_B1 + kv + 1], ALU.add))
                    link(v.tensor_scalar(x[kv], pb[kv][:, 0:60], hb, None, ALU.add))
                    y = cmph[:, kv, 1, 0:60]
                    link(v.tensor_tensor(y, x[kv], x[kv], ALU.mult))
                    link(v.tensor_scalar(y, y, 0.044715, 1.0, ALU.mult, ALU.add))
                    v.tensor_tensor(y, y, x[kv], ALU.mult).then_inc(gel_in, 1)
                for kv in range(2):
                    dve.wait_ge(gel_th, kv + 1)
                    v.scalar_tensor_tensor(cmph[:, kv, 3, 0:60], cmph[:, kv, 2, 0:60], 1.0, x[kv], ALU.add, ALU.mult)\
                        .then_inc(gel_done, 1)
                dve.wait_ge(cmp_ready, 1)
                for kv in range(2):
                    link(v.scalar_tensor_tensor(cmpk[0:NCMP, kv, :, :], pb[2][0:NCMP, 256 * kv:256 * (kv + 1)].rearrange(
                        "p (g d) -> p g d", g=NG), 0.5, view(b2[0:NCMP, kv, :], 0, [[0, NG], [1, HD]]), ALU.mult, ALU.add))
                link(v.tensor_tensor(cmpd[0:NCMP, :, 0, :], cmpk[0:NCMP, 0, :, :], cmpk[0:NCMP, 0, :, :], ALU.mult))
                v.tensor_reduce(rms[0:NCMP, R_CMP:R_CMP + 4], cmpd[0:NCMP, :, 0, :], AX, ALU.add).then_inc(ss_done, 1)
                root_wait("cmp")
                for twice in range(2):
                    v.tensor_tensor(cmpd[0:NCMP, :, twice, :], cmpk[0:NCMP, 0, :, :],
                                    view(rms[0:NCMP, R_CMP:R_CMP + 4], 0, [[1, NG], [0, HD]]), ALU.mult).then_inc(cmpn_done, 1)
                dve.wait_ge(cmpT_ready, 1)
                v.tensor_scalar(cmpT[:, :, 0:NCMP], pb[3][:, 0:64].rearrange("p (g c) -> p g c", g=NG)[:, :, 0:NCMP],
                                g2T[:, 7:8], None, ALU.mult).then_inc(cmpT_done, 1)

            def nsa_gates():
                dve.wait_ge(g_th, 2)
                link(v.tensor_scalar(gates[:], gates[:], 0.5, 0.5, ALU.mult, ALU.add))
                g0 = view(gates[:, 0, :], 0, [[3, NH]])
                link(v.tensor_scalar(g0, g0, cst[:, C_VALID:C_VALID + 1], None, ALU.mult))

            def rope(l):
                dve.wait_ge(pj_a, PJ_AT[2 + l] + 2)
                dve.wait_ge(pj_v, PJ_AT[2 + l] + 2)
                nh = HEADS2 + KV2
                cos, sin = (cst[:, c:c + 16] for c in (C_COS, C_SIN))
                tmp = sbuf_p[:, :, :].rearrange("p a b -> p (a b)")
                for t in range(NT):
                    x1, x2 = (view(qkv2[:, t, :], o, [[HD, nh], [1, 8]]) for o in (0, 8))
                    cb, sbb = (view(a, 8 * t, [[0, nh], [1, 8]]) for a in (cos, sin))
                    k = [tmp[:, 80 * i:80 * (i + 1)].rearrange("p (a b) -> p a b", b=8) for i in range(4)]
                    v.tensor_tensor(k[0], x1, cb, ALU.mult)
                    v.tensor_tensor(k[1], x2, sbb, ALU.mult)
                    v.tensor_tensor(k[2], x2, cb, ALU.mult)
                    link(v.tensor_tensor(k[3], x1, sbb, ALU.mult))
                    v.tensor_tensor(x1, k[0], k[1], ALU.subtract)
                    link(v.tensor_tensor(x2, k[2], k[3], ALU.add))
                for t in range(NT):
                    for twice in range(2):
                        v.tensor_copy(view(xs[:, t, :], HD * twice, [[2 * HD, KV2], [1, HD]]),
                                      view(qkv2[:, t, :], 512, [[HD, KV2], [1, HD]])).then_inc(qn_ready, 1)

            def conv(l):
                v.memset(cuT[:, :, 0:1], 0.0)
                link(v.memset(cuT[:, :, S + 1:S + 2], 0.0))
                for half in range(2):
                    split_to(SEG[2 + l], CVW[l][2][1] + 1)
                    dve.wait_ge(used[SEG[2 + l]], CVW[l][2][half] + 1)
                    dve.wait_ge(gb_done, 4 * l + 4)
                    link(v.tensor_tensor(cuT[:, 2 * half:2 * half + 2, 1:S + 1],
                                         gcT[:, 512 * half:512 * (half + 1)].rearrange("p (a b) -> p a b", a=2),
                                         pb[4 + half][:].rearrange("p (a b) -> p a b", a=2), ALU.mult))
                for j in range(3):
                    for c in range(4):
                        y = yT[:, S * c:S * (c + 1)]
                        w = gT[:, G_CW + 12 * l + 4 * j + c:][:, 0:1]
                        x = cuT[:, c, j:j + S]
                        if j == 0:
                            i = v.tensor_scalar(y, x, w, None, ALU.mult)
                        else:
                            i = v.scalar_tensor_tensor(y, x, w, y, ALU.mult, ALU.add)
                    link(i)
                v.tensor_tensor(yT, yT, gbT, ALU.mult).then_inc(y_done, 1)
                split_to(SEG[2 + l], OPW[2 + l][0][1] + 2)
                dve.wait_ge(y_done, l + 1)
                for i in range(2):
                    for c in range(4):
                        y, g = yT[:, S * c:S * (c + 1)], gT[:, G_CONV + 4 * l + c:][:, 0:1]
                        if i == 0:
                            ins = v.tensor_scalar(xT[:, 0, 4 + c, :], y, g, None, ALU.mult)
                        else:
                            ins = v.scalar_tensor_tensor(xT[:, 1, 4 + c, :], y, g, xT[:, 0, 4 + c, :].bitcast(F32), ALU.mult,
                                                         ALU.subtract)
                        ins.then_inc(cx_done, 1)
                    if i == 0:
                        dve.wait_ge(cx_done, 8 * l + 4)
                dve.wait_ge(yss_ready, l + 1)
                v.tensor_copy(rms[:, R_CONV[l]:R_CONV[l] + 2], pb[7][:, 0:2]).then_inc(yss_done, 1)

            def attn_out(l):
                root_wait(("att", l))
                for t in range(NT):
                    x = xs[:, t, 0:CW]
                    v.tensor_scalar(x, x, rms[:, R_ATT[l] + t:R_ATT[l] + t + 1], float(CW ** 0.5), ALU.mult, ALU.mult)\
                        .then_inc(at_ready, 1)

            def residual2(l):
                root_wait(("conv", l))
                r = rms[:, R_CONV[l]:R_CONV[l] + 2]
                link(v.tensor_scalar(r, r, float(CW ** 0.5), None, ALU.mult))
                seg = SEG[2 + l]
                for c in range(2):
                    split_to(seg, OPW[2 + l][1][1] + 1)
                    for t in range(NT):
                        if t:
                            dve.wait_ge(used[seg], OPW[2 + l][c][1] + 1)
                        else:
                            dve.wait_ge(op_ready, 2 * (2 + l) + c + 1)
                        hh = h[:, t, 512 * c:512 * (c + 1)]
                        link(v.tensor_tensor(hh, hh, pb[2 * c + t][:], ALU.add))
                        v.scalar_tensor_tensor(hh, pb[4 + 2 * c + t][:], r[:, t:t + 1], hh, ALU.mult, ALU.add)\
                            .then_inc(h_done, 1)

            def route(l):
                dve.wait_ge(rt_ready, l + 1)

                def cols(a, n):
                    return rt[:, a:a + 2 * n].rearrange("p (t n) -> p t n", t=NT)

                lg = cols(0, 36)
                gmax, gidx = rt[:, 72:74], rt[:, 74:76]
                gcmp, goh, gx = cols(80, 4), cols(96, 4), cols(112, 4)
                gsum = rt[:, 120:122]
                elm, ecmp = cols(128, NE), cols(192, NE)
                oh = [cols(256, NE), cols(448, NE)]
                mx = [rt[:, 368:370], rt[:, 370:372]]
                idx = [rt[:, 372:374], rt[:, 374:376]]
                dz = rt[:, 364:366]
                asg = cols(384, NE)
                i4, i32 = cst[:, C_I4:C_I4 + 4], cst[:, C_I32:C_I32 + NE]

                def spread(x, n):
                    return view(x, 0, [[1, NT], [0, n]])

                link(v.tensor_tensor(lg, pb[0][:, 0:128].rearrange("p (t n) -> p t n", t=NT)[:, :, 0:36],
                                     view(brt[:, l, :], 0, [[0, NT], [1, 36]]), ALU.add))
                gl, el = lg[:, :, 0:NEG], lg[:, :, NEG:36]
                link(v.tensor_reduce(gmax, gl, AX, ALU.max))
                link(v.tensor_tensor(gcmp, gl, spread(gmax, 4), ALU.is_lt))
                link(v.scalar_tensor_tensor(gcmp, gcmp, 1.0e6, view(i4, 0, [[0, NT], [1, 4]]), ALU.mult, ALU.add))
                link(v.tensor_reduce(gidx, gcmp, AX, ALU.min))
                link(v.tensor_tensor(goh, view(i4, 0, [[0, NT], [1, 4]]), spread(gidx, 4), ALU.is_equal))
                v.tensor_tensor(gx, gl, spread(gmax, 4), ALU.subtract).then_inc(rt_x, 1)
                link(v.tensor_scalar(gcmp, goh, -1.0, BIG, ALU.add, ALU.mult))
                for t in range(NT):
                    o8 = view(goh, 4 * t, [[1, 4], [0, 8]])
                    e8 = view(elm, NE * t, [[8, 4], [1, 8]])
                    link(v.tensor_tensor(e8, view(el, 36 * t, [[8, 4], [1, 8]]), o8, ALU.mult))
                    link(v.tensor_tensor(e8, e8, view(gcmp, 4 * t, [[1, 4], [0, 8]]), ALU.add))
                for k in range(2):
                    link(v.tensor_reduce(mx[k], elm, AX, ALU.max))
                    link(v.tensor_tensor(ecmp, elm, spread(mx[k], NE), ALU.is_lt))
                    link(v.scalar_tensor_tensor(ecmp, ecmp, 1.0e6, view(i32, 0, [[0, NT], [1, NE]]), ALU.mult, ALU.add))
                    link(v.tensor_reduce(idx[k], ecmp, AX, ALU.min))
                    link(v.tensor_tensor(oh[k], view(i32, 0, [[0, NT], [1, NE]]), spread(idx[k], NE), ALU.is_equal))
                    if k == 0:
                        link(v.scalar_tensor_tensor(elm, oh[0], -BIG, elm, ALU.mult, ALU.add))
                v.tensor_tensor(asg, oh[0], oh[1], ALU.add).then_inc(as_done, 1)
                v.tensor_tensor(dz, mx[1], mx[0], ALU.subtract).then_inc(rt_x, 1)
                dve.wait_ge(cnt_ready, l + 1)
                cm, wm = rt[0:NE, 512:640], rt[0:NE, 640:768]
                v.tensor_copy(cm, pb[1][0:NE, 0:P]).then_inc(cnt_done, 1)
                wt = rt[0:NE, 768:896]
                link(v.tensor_scalar(wm, pb[1][0:NE, 0:P], 0.0, None, ALU.is_gt))
                for i in range(1, S // W):
                    link(v.tensor_scalar(wt, pb[1][0:NE, 0:P], float(i * W), None, ALU.is_gt))
                    link(v.tensor_tensor(wm, wm, wt, ALU.add))
                v.tensor_scalar(wm, wm, ident[0:NE, 0:1], None, ALU.max).then_inc(cnt_done, 1)
                dve.wait_ge(rt_e, 2 * l + 2)
                link(v.tensor_reduce(gsum, gx, AX, ALU.add))
                g1, g2 = rt[:, 376:378], rt[:, 378:380]
                link(v.tensor_scalar(g1, dz, 1.0, None, ALU.add))
                link(v.tensor_tensor(g1, g1, gsum, ALU.mult))
                link(v.reciprocal(g1, g1))
                link(v.tensor_tensor(g2, dz, g1, ALU.mult))
                dve.wait_ge(pos_ready, l + 1)
                ja, jo, jv = jobs_work()
                c0, w0, w1 = rt[0:NE, 1152:1153], rt[0:NE, 1153:1154], rt[0:NE, 1154:1155]
                ij = cst[0:NE, C_I512:C_I512 + JOBS]
                v.tensor_copy(c0, pb[3][0:NE, NE:NE + 1])
                link(v.tensor_copy(w0, pb[3][0:NE, NE + 1:NE + 2]))
                link(v.tensor_tensor(w1, w0, wm[:, 0:1], ALU.add))
                v.scalar_tensor_tensor(jv, w0, float(-W), c0, ALU.mult, ALU.add)
                link(v.tensor_scalar(ja, ij, w1, None, ALU.is_ge))
                v.scalar_tensor_tensor(jo, ij, w0, ja, ALU.is_ge, ALU.subtract).then_inc(job_cols, 1)
                st = rt[:, 896:896 + NE]
                link(v.tensor_copy(st, pb[3][:, 0:NE]))
                pos = cols(928, NE)
                link(v.tensor_tensor(pos, pb[2][:, 0:2 * NE].rearrange("p (t n) -> p t n", t=NT),
                                     view(st, 0, [[0, NT], [1, NE]]), ALU.add))
                sl = [rt[:, 992:994], rt[:, 994:996]]
                for k in range(2):
                    link(v.tensor_tensor(ecmp, oh[k], pos, ALU.mult))
                    link(v.tensor_reduce(sl[k], ecmp, AX, ALU.add))
                dve.wait_ge(job_ready, l + 1)
                link(v.tensor_scalar(tab[0:1, 0:JOBS], pb[1][0:1, 0:JOBS], float(NE - 1), None, ALU.min))
                link(v.scalar_tensor_tensor(tab[0:1, JOBS:2 * JOBS], cst[0:1, C_I512:C_I512 + JOBS], float(W),
                                            pb[1][0:1, 64:64 + JOBS], ALU.mult, ALU.add))
                v.tensor_scalar(tab[0:1, 2 * JOBS:2 * JOBS + 1], pb[1][0:1, 128:129], -2.0, None, ALU.add).then_inc(tab_done, 1)
                i512 = cst[:, C_I512:C_I512 + NS]
                for t in range(NT):
                    link(v.tensor_scalar(sel[:, t, :], i512, sl[0][:, t:t + 1], None, ALU.is_equal))
                    i = v.scalar_tensor_tensor(sel[:, t, :], i512, sl[1][:, t:t + 1], sel[:, t, :], ALU.is_equal, ALU.add)
                    if t == 0:
                        link(i)
                i.then_inc(sel_done, 1)
                for t in range(NT):
                    link(v.tensor_scalar(gsel[:, t, :], i512, sl[0][:, t:t + 1], g1[:, t:t + 1], ALU.is_equal, ALU.mult))
                    link(v.tensor_scalar(gtmp, i512, sl[1][:, t:t + 1], g2[:, t:t + 1], ALU.is_equal, ALU.mult))
                    i = v.tensor_tensor(gsel[:, t, :], gsel[:, t, :], gtmp, ALU.add)
                    if t == 0:
                        link(i)
                i.then_inc(sel_done, 1)

            def moe(l):
                normalise(7 + 2 * l)
                evac_tp(10 + 3 * l)
                route(l)
                col = G_NORM[7 + 2 * l]
                v.memset(xsT[:, :, NS:NSP], 0.0).then_inc(xsT_v, 1)
                for k in range(1, KC, 2):
                    dve.wait_ge(ga_ready, KC * l + k + 1)
                    v.tensor_scalar(xsT[:, k, 0:NS], pb[4 + k % 4][:], gT[:, col + k:col + k + 1], None, ALU.mult)\
                        .then_inc(xsT_v, 1)
                for c in range(2):
                    dve.wait_ge(gct_ready, 2 * l + c + 1)
                    v.tensor_copy(gcombT[:, 2 * c:2 * c + 2, :], pb[c][:].rearrange("p (a b) -> p a b", a=2))\
                        .then_inc(gct_done, 1)
                more = dve.value_load(tab[0:1, 2 * JOBS:2 * JOBS + 1], min_val=NS // W - 2, max_val=JOBS - 2)
                seg = 2 * l + 1
                dve.sem_inc(yadd_done[l], 1)
                dve.wait_ge(xsT_a, 4 * (l + 1))
                dve.wait_ge(xsT_v, 5 * (l + 1))

                def window(j):
                    s0 = dve.value_load(tab[0:1, bass.ds(at(j, 1, JOBS), 1)], min_val=0, max_val=NS)
                    dve.wait_ge(xw_rounded[l], at(j, 1, 1))
                    v.tensor_tensor(xw[:, :, W:2 * W], xsT[:, :, bass.ds(s0, W)], xw[:, :, 0:W].bitcast(F32), ALU.subtract)\
                        .then_inc(xw_ready[l], 1)

                def rest_half(j, q):
                    dve.wait_ge(hi_done[seg], at(j, 6, q - 1))
                    hi, lo = job_parts(l, q)
                    v.tensor_tensor(lo, raw[:, job_place(l, q), :], hi.bitcast(F32), ALU.subtract).then_inc(lo_done[seg], 1)

                def sums(j, back):
                    for m, dst in enumerate((eg, eu)):
                        dve.wait_ge(eg_first[l], at(j, 2, m + 1 - 2 * back))
                        d = dst.rearrange("p (k s) -> p k s", k=4)
                        v.tensor_tensor(d, d, pb[2 + m][:].rearrange("p (k i s) -> p k i s", k=4, i=2)[:, :, 1, :], ALU.add)\
                            .then_inc(g_added[l] if m == 0 else ech[l], 1)

                def hidden(j, back):
                    dve.wait_ge(eth_done[l], at(j, 1, 1 - back))
                    v.scalar_tensor_tensor(ea, ea, 1.0, eg, ALU.add, ALU.mult).then_inc(ech[l], 1)
                    dve.wait_ge(ech[l], at(j, 4, 2 - 4 * back))
                    v.scalar_tensor_tensor(eh, ea, 0.5, eu, ALU.mult, ALU.mult).then_inc(ech[l], 1)
                    dve.wait_ge(ech[l], at(j, 4, 3 - 4 * back))
                    x = eh.rearrange("p (j s) -> p j s", j=4)
                    v.tensor_copy(ehl[:, :, 0:W], x).then_inc(ech[l], 1)
                    dve.wait_ge(ech[l], at(j, 4, 4 - 4 * back))
                    v.tensor_tensor(ehl[:, :, W:2 * W], x, ehl[:, :, 0:W].bitcast(F32), ALU.subtract).then_inc(eh_done[l], 1)

                def to_slots(j, back):
                    s0 = dve.value_load(tab[0:1, bass.ds(at(j, 1, JOBS - back), 1)], min_val=0, max_val=NS)
                    for b in range(2):
                        dve.wait_ge(y_first[l], at(j, 2, b + 1 - 2 * back))
                        d = ysT[:, 4 * b:4 * b + 4, bass.ds(s0, W)]
                        v.tensor_tensor(d, d, pb[6 + b][:].rearrange("p (k i s) -> p k i s", k=4, i=2)[:, :, 1, :], ALU.add)\
                            .then_inc(yadd_done[l], 1)

                def step(j):
                    later = not isinstance(j, int)
                    g0, g1, u0, u1 = (q for q, _, _ in gate_up(j))
                    window(j)
                    rest_half(j, g0)
                    rest_half(j, g1)
                    if later or j:
                        sums(j, 1)
                    rest_half(j, u0)
                    if later or j:
                        hidden(j, 1)
                    rest_half(j, u1)
                    if later:
                        to_slots(j, 2)
                    if later or j:
                        rest_half(j, down_at(False))
                        rest_half(j, down_at(False) + 1)

                step(0)
                step(1)
                with dve.Fori(0, more) as j:
                    step(j)
                sums(more, 1)
                hidden(more, 1)
                rest_half(more, down_at(True))
                rest_half(more, down_at(True) + 1)
                to_slots(more, 2)
                to_slots(more, 1)
                for i in range(1, 8, 2):
                    dve.wait_ge(yt_ready, 8 * l + i + 1)
                    v.tensor_copy(ysort[:, i // 2, 512:1024], pb[4 + i % 4][:]).then_inc(yt_v, 1)
                residual(op_ready2, 4 * l)

            normalise(0)
            evac_tp(0)
            setup_rest()
            evac_proj(0, PJ_AT[1])
            split_to(0, OPW[0][0][0] + SPL)
            head_norms(0)
            dve.wait_ge(scr_written, 32)
            evac_heads(0)
            attention(0)
            evac_tp(1)
            out_residual(0)
            normalise(1)
            evac_tp(2)
            ffn(0)
            transpose_p(0)
            normalise(2)
            evac_tp(3)
            ple(0)
            normalise(3)
            evac_tp(4)
            evac_proj(1, PJ_AT[2])
            split_to(0, OPW[1][0][0] + RAW - 4)
            compress()
            head_norms(1)
            evac_heads(1)
            nsa_gates()
            attention(1)
            evac_tp(5)
            out_residual(1)
            normalise(4)
            evac_tp(6)
            ffn(1)
            transpose_p(1)
            normalise(5)
            evac_tp(7)
            ple(1)
            for l in range(2):
                normalise(6 + 2 * l)
                evac_tp(8 + 3 * l)
                evac_proj(2 + l, PJ_AT[2 + l] + 2)
                rope(l)
                conv(l)
                evac_heads(2 + l)
                attention(2 + l)
                attn_out(l)
                evac_tp(9 + 3 * l)
                residual2(l)
                moe(l)
            root_wait(("norm", 10))
            dve.wait_ge(gfin_loaded, 16)
            for t in range(NT):
                link(v.tensor_scalar(xs[:, t, :], h[:, t, :], rms[:, R_NORM[10] + t:R_NORM[10] + t + 1], float(D ** 0.5),
                                     ALU.mult, ALU.mult))
                v.tensor_tensor(xs[:, t, :], xs[:, t, :], gfin, ALU.mult).then_inc(out_ready, 1)


def shape_constants():
    c = np.zeros((P, C_W), np.float32)
    c[:, C_ID:C_ID + P] = np.eye(P)
    c[:, C_TRI:C_TRI + P] = np.triu(np.ones((P, P)), 1)
    c[:, C_I512:C_I512 + NS] = np.arange(NS)
    c[:, C_I32:C_I32 + NE] = np.arange(NE)
    c[:, C_I4:C_I4 + NEG] = np.arange(NEG)
    c[:, C_VALID] = np.arange(P) >= CMP_LEN - 1
    inv = np.float32(500000.0) ** (-np.arange(0, 16, 2, dtype=np.float32) / np.float32(16))
    ang = np.arange(S, dtype=np.float32)[:, None] * inv[None, :].astype(np.float32)
    for col, f in ((C_COS, np.cos), (C_SIN, np.sin)):
        a = f(ang.astype(np.float64)).astype(np.float32).reshape(NT, P, 8)
        c[:, col:col + 16] = a.transpose(1, 0, 2).reshape(P, 16)
    d = np.arange(512) - 255
    exact = BUCKETS // 2
    nf = np.maximum(d, 1).astype(np.float32)
    large = exact + (np.log(nf / np.float32(exact)) / np.float32(np.log(2048 / exact)) * np.float32(BUCKETS - exact)).astype(np.int32)
    bucket = np.where(d < exact, np.maximum(d, 0), np.minimum(large, BUCKETS - 1))
    onehot = ((bucket[None, :] == np.arange(BUCKETS)[:, None]) & (d >= 0)[None, :]).astype(np.float32)
    causal = np.where(d >= 0, 0.0, OFF)
    times = np.where(d >= 0, (d <= 128) * 1 + (d % 4 == 0) * 1 + (d % 16 == 0) * 1, 0)
    dilated = np.where(times > 0, 8.0 * np.log(np.maximum(times, 1)), OFF)
    masks = np.tile(np.concatenate([causal, dilated]).astype(np.float32), (NH, 1))
    window = np.where(np.abs(d) <= 128, 0.0, OFF).astype(np.float32)
    return {"consts": c, "onehot": onehot, "row_masks": masks, "window_band": window}


_INS = ["x", "p", "rel_bias", "norm_mix", "norm_ffn", "norm_ple", "w_ffn_gate", "w_ffn_up", "w_ffn_down", "w_ple_proj",
        "w_ple_gate", "w_in_ab", "w_out_ab", "qn_moba", "kn_moba", "qn_dil", "kn_dil", "w_in_nsa", "w_out_nsa",
        "qn_nsa", "kn_cmp", "kn_slc", "kn_win", "cmp_k_pos", "cmp_k_w1", "cmp_k_b1", "cmp_k_w2", "cmp_k_b2",
        "cmp_v_pos", "cmp_v_w1", "cmp_v_b1", "cmp_v_w2", "cmp_v_b2", "norm_mix_2", "w_in_2", "attn_sink_2",
        "conv_w_2", "norm_attn_out_2", "norm_conv_out_2", "w_out_2", "norm_ffn_2", "w_router_group_2",
        "b_router_group_2", "w_router_expert_2", "b_router_expert_2", "w_expert_gate_2", "w_expert_up_2",
        "w_expert_down_2", "norm_final_2"]


def kernel(**inputs):
    import numpy as _np
    import concourse.bacc as _bacc
    from concourse import mybir as _mybir
    from concourse.bass_utils import run_bass_kernel_spmd as _run

    nc = _bacc.Bacc("TRN2", target_bir_lowering=False, num_devices=1)
    arrays, args = {}, {}
    for name, a in [(n, inputs[n]) for n in _INS] + list(shape_constants().items()):
        a = _np.ascontiguousarray(a)
        arrays[f"in_{name}"] = a
        args[name] = nc.dram_tensor(f"in_{name}", a.shape, _mybir.dt.from_np(a.dtype), kind="ExternalInput").ap()
    out = nc.dram_tensor("out_0", (1, S, D), F32, kind="ExternalOutput").ap()
    build(nc, args, out)
    r = _run(nc, [arrays], core_ids=[0])
    return r.results[0]["out_0"]
```

```python
from contextlib import ExitStack

import concourse.bass as bass
from concourse import mybir
import numpy as np

F32 = mybir.dt.float32
F32R = mybir.dt.float32r
I32 = mybir.dt.int32
ALU = mybir.AluOpType
ACT = mybir.ActivationFunctionType
AX = mybir.AxisListType.X

P = 128
S = 256
NT = S // P
D = 1024
KC = D // P
HD = 64
NH = 16
F = 2816
NQ = F // S
BUCKETS = 32
NCMP = 15
CMP_LEN, CMP_STRIDE = 32, 16
NG = 4
HEADS2, KV2 = 8, 2
CW = 512
NE, NEG = 32, 4
DE = 512
W = 64
NS = 2 * S
NSP = NS + W
RAW = 6
SPL = 3
HALF = 2048
JOBS = NE + NS // W
EPS = 1e-6
OFF = -1.0e30
BIG = 3.0e38
NB = 384
GELU = 0.7978845608028654

G_NORM = [0, 16, 32, 8, 24, 40, 48, 64, 56, 72]
G_ATT, G_CONV, G_CW, G_B1, PRM_ROWS = 80, 88, 96, 120, 122
H_POS, HEAD_ROWS = 8, 40
C_ID, C_TRI, C_I512, C_I32, C_I4, C_VALID, C_COS, C_SIN, C_W = 0, 128, 256, 768, 800, 804, 805, 821, 837


def view(ap, off, dims):
    return bass.AP(tensor=ap.tensor, offset=ap.offset + off, ap=[list(ap.ap[0])] + [list(d) for d in dims])


def build(nc, A, out):
    ctx = ExitStack()
    with ctx:
        def sb(name, shape, dt=F32):
            return ctx.enter_context(nc.sbuf_tensor(name, shape, dt))

        def sem(name):
            return ctx.enter_context(nc.semaphore(name))

        raw = sb("raw", [P, RAW, HALF])
        parts = sb("parts", [P, SPL, 2, HALF], F32R)
        h = sb("h", [P, NT, D])
        xT = sb("xT", [P, 2, KC, S], F32R)
        xs = sb("xs", [P, NT, D])
        NBAND = 8
        work = sb("work", [P, NBAND * NB + 2 * 4 * S])
        band = work[:, 0:NBAND * NB].rearrange("p (a b) -> p a b", a=NBAND)
        qkv = sb("qkv", [P, 6144])
        qk = sb("qk", [P, 16, S])
        sbuf_s = work[:, NBAND * NB:NBAND * NB + 4 * S].rearrange("p (a b) -> p a b", a=4)
        sbuf_p = work[:, NBAND * NB + 4 * S:].rearrange("p (a b) -> p a b", a=4)
        hidT = sb("hidT", [P, 2, 2, S], F32R)
        wr = sb("wr", [P, 2, KC, NEG + NE])
        cst = sb("cst", [P, C_W])
        ones = sb("ones", [P, P])
        mhalf = sb("mhalf", [P, 64])
        gT = sb("gT", [P, PRM_ROWS])
        g2T = sb("g2T", [P, HEAD_ROWS])
        sink = sb("sink", [P, 2, 2, HEADS2])
        brt = sb("brt", [P, 2, NEG + NE])
        relb = sb("relb", [BUCKETS, NH])
        w2 = sb("w2", [P, 2, HD])
        b2 = sb("b2", [P, 2, HD])
        rms = sb("rms", [P, 256])
        NU = 32 + 96 + 16 + 16
        nmax = sb("nmax", [P, NU])
        den = sb("den", [P, NU])
        rec = sb("rec", [P, 4])
        esink = sb("esink", [P, 32])
        gates = sb("gates", [P, NT, 48])
        cmpk = sb("cmpk", [16, 2, NG, HD])
        cmpT = sb("cmpT", [P, NG, 16])
        tab = sb("tab", [1, 2 * JOBS + 1], I32)
        pb = [ctx.enter_context(nc.psum_tensor(f"pb{i}", [P, 512], F32)) for i in range(8)]
        scr = nc.dram_tensor("scr", [2 * NH, 512], F32, kind="Internal").ap()

        def qkv_t(t):
            return qkv[:, 3072 * t:3072 * (t + 1)]

        ident = cst[:, C_ID:C_ID + P]
        tri = cst[:, C_TRI:C_TRI + P]
        prm = qkv[:, 0:2 * P].rearrange("p (a b) -> p a b", a=2)
        oneh = qk[0:BUCKETS, 0:2, :].rearrange("p a b -> p (a b)")
        tmask = qk[0:NH, 2:6, :].rearrange("p a b -> p (a b)")
        trow = qk[0:NH, 6:10, :].rearrange("p a b -> p (a b)")
        rowsP = sbuf_p[:, 0:2, :]
        fh = sbuf_p[:, 2:4, :]
        th = sbuf_s[:, 0:2, :]
        ga = sbuf_s[:, 2:4, :]
        cmph = sbuf_p[:, 0:2, :].rearrange("p a (b c) -> p a b c", b=4)
        cmpd = sbuf_p[0:16, 2:4, :].rearrange("p a b -> p (a b)").rearrange("p (g t d) -> p g t d", g=NG, t=2)
        xc = xT[:, :, :, :].rearrange("p i k s -> p (i k s)").rearrange("p (v i g s) -> p v i g s", v=2, i=2, g=NG)
        posr = hidT[:, 0, 0, 0:64].rearrange("p (v i l) -> p v i l", v=2, i=2)
        kv2cols = 768
        qkv2 = qkv[:, 0:NT * kv2cols].rearrange("p (t c) -> p t c", t=NT)
        gbT = qkv[:, 1536:2560]
        gcT = qkv[:, 2560:3584]
        cuT = qkv[:, 3584:3584 + 4 * (S + 2)].rearrange("p (c s) -> p c s", c=4)
        yT = qkv[:, 4616:5640]
        ysT = work[:, NB:NB + KC * NSP].rearrange("p (k s) -> p k s", k=KC)
        qkf = qk[:, :, :].rearrange("p a b -> p (a b)")
        xsT = qkv[:, 0:KC * NSP].rearrange("p (k s) -> p k s", k=KC)
        gcombT = qkv[:, 4608:5632].rearrange("p (c s) -> p c s", c=4)
        ysort = qkv[:, 0:4096].rearrange("p (c d) -> p c d", c=4)
        hidf = hidT[:, :, :, :].rearrange("p a b s -> p (a b s)")
        wrs = hidf[:, 0:KC * 2 * (NEG + NE)].rearrange("p (k i n) -> p k i n", k=KC, i=2)
        sel = hidf.rearrange("p (t s) -> p t s", t=NT)
        xsp = [xT[:, i, :, :].rearrange("p k s -> p (k s)") for i in range(2)]
        gsel = sbuf_p.rearrange("p a b -> p (a b)").rearrange("p (t s) -> p t s", t=NT)
        rt = qkf[:, 0:2048]
        gtmp = qkf[:, 2048:2560]
        gs, us, ys = qkf[:, 0:512], qkf[:, 512:1024], qkf[:, 1024:2048]
        eg, ea, eu, eh = (qkf[:, 2048 + 256 * i:2304 + 256 * i] for i in range(4))
        xw = xT[:, 0, 0:4, :].rearrange("p a b -> p (a b)").rearrange("p (k s) -> p k s", k=KC)
        ehl = xT[:, 1, 0:2, :].rearrange("p a b -> p (a b)").rearrange("p (j s) -> p j s", j=DE // P)
        gfin = qkf[:, 0:D]

        x_loaded = sem("x_loaded")
        par_loaded = sem("par_loaded")
        cst_loaded = sem("cst_loaded")
        rel_loaded = sem("rel_loaded")
        arrived = [[sem(f"arrived{g}_{i}") for i in range(RAW)] for g in (0, 1, 3)]
        arrived = [arrived[0], arrived[1], arrived[0], arrived[2]]
        hi_done = [sem(f"hi_done{g}") for g in range(4)]
        lo_done = [sem(f"lo_done{g}") for g in range(4)]
        used = [sem(f"used{g}") for g in range(4)]
        par2_loaded, p_loaded, p_ready = sem("par2_loaded"), sem("p_loaded"), sem("p_ready")
        pT_done, pT_v = sem("pT_done"), sem("pT_v")
        set_ready, set_done = sem("set_ready"), sem("set_done")
        trow_done, scr_written, band_loaded = sem("trow_done"), sem("scr_written"), [sem(f"band_loaded{i}") for i in range(2)]
        wr_loaded = sem("wr_loaded")
        dch, ach, pch = sem("dve_chain"), sem("act_chain"), sem("pool_chain")
        sq_done, rstd_done, xs_ready = sem("sq_done"), sem("rstd_done"), sem("xs_ready")
        ss_done = sem("ss_done")
        tp_ready, xT_a, xT_v = sem("tp_ready"), sem("xT_a"), sem("xT_v")
        pj_ready, pj_a, pj_v = sem("pj_ready"), sem("pj_a"), sem("pj_v")
        op_ready, h_done = sem("op_ready"), sem("h_done")
        th_done, hT_done = sem("th_done"), sem("hT_done")
        wr_rounded, wr_ready, xs_rounded, xsp_ready = sem("wr_rounded"), sem("wr_ready"), sem("xs_rounded"), sem("xsp_ready")
        ple_ready, ple_th = sem("ple_ready"), sem("ple_th")
        hsq, hss, qn_ready = sem("head_squares"), sem("head_sums"), sem("qn_ready")
        qt_ready, qt_a, qt_v = sem("qt_ready"), sem("qt_a"), sem("qt_v")
        s_ready, s_max, e_done = sem("s_ready"), sem("s_max"), sem("e_done")
        pt_ready, pt_done, o_ready, o_done = sem("pt_ready"), sem("pt_done"), sem("o_ready"), sem("o_done")
        cT_ready, cT_rounded, cT_done, gel_in, gel_th, gel_done = (sem("cT_ready"), sem("cT_rounded"), sem("cT_done"),
                                                                 sem("gel_in"), sem("gel_th"), sem("gel_done"))
        cmp_ready, cmpn_done, cmpT_ready, cmpT_done = (sem("cmp_ready"), sem("cmpn_done"), sem("cmpT_ready"),
                                                       sem("cmpT_done"))
        g_th = sem("g_th")
        gb_done, y_done = sem("gb_done"), sem("y_done")
        ysq_done, yss_ready, yss_done = sem("ysq_done"), sem("yss_ready"), sem("yss_done")
        on_ready = sem("on_ready")
        rt_ready, rt_e, rt_x, as_done, cnt_ready, cnt_done = (sem("rt_ready"), sem("rt_e"), sem("rt_x"),
                                                              sem("as_done"), sem("cnt_ready"), sem("cnt_done"))
        pos_ready, tab_done, sel_done = sem("pos_ready"), sem("tab_done"), sem("sel_done")
        ga_ready, xsT_a, xsT_v = sem("ga_ready"), sem("xsT_a"), sem("xsT_v")
        gct_ready, gct_done = sem("gct_ready"), sem("gct_done")
        at_ready, cx_done, yt_v, op_ready2 = sem("at_ready"), sem("cx_done"), sem("yt_v"), sem("op_ready2")
        xw_ready, ys_done, gs_done, us_done, gt_ready, yt2_ready = ([sem(f"{n}{i}") for i in range(2)] for n in (
            "xw_ready", "ys_done", "gs_done", "us_done", "gt_ready", "yt2_ready"))
        g_added, eth_done, eh_done, yadd_done, ech, xw_rounded = ([sem(f"{n}{i}") for i in range(2)] for n in (
            "g_added", "eth_done", "eh_done", "yadd_done", "job_chain", "xw_rounded"))
        y_first, eg_first = ([sem(f"{n}{i}") for i in range(2)] for n in ("y_first", "eg_first"))
        job_ready, job_cols = sem("job_ready"), sem("job_cols")
        yt_ready, yt_done = sem("yt_ready"), sem("yt_done")
        out_ready, stored = sem("out_ready"), sem("stored")

        stream = {0: [], 2: []}

        def kcols(w, c0, n, k0=0, k=KC):
            return w[k0 * P:(k0 + k) * P, c0:c0 + n].rearrange("(k p) n -> p k n", p=P)

        RAW0 = [0, 0, 0, 0]

        loads = [0] * RAW

        def add(seg, src, k, n):
            i = len(stream[seg])
            place = (RAW0[seg] + i) % RAW
            loads[place] += 1
            stream[seg].append((raw[:, place, 0:k * n].rearrange("p (k n) -> p k n", k=k), src, place, 16 * loads[place], (k, n)))
            return i

        def both(seg, s):
            k, n = stream[seg][s][4]
            return [parts[:, (SPL0[seg] + s) % SPL, i, 0:k * n].rearrange("p (k n) -> p k n", k=k) for i in range(2)]

        SPL0 = [0, 0, 0, 0]
        PJ = []
        PJ_AT = {}
        SEG = [0, 0, 0, 2]
        HEADS_AT = [(1, 3), (1, 4)]

        def add_proj(layer, w, cols):
            PJ_AT[layer] = len(PJ)
            for c0, n, dst in cols:
                PJ.append(([add(SEG[layer], kcols(w, c0, n, 4 * hf, 4), 4, n) for hf in range(2)], n, dst))

        OPW, FFW, PLW, CMPW, CVW = {}, {}, {}, {}, {}

        def add_out(k, w):
            OPW[k] = [[add(SEG[k], kcols(w, 512 * c, 512, 4 * hf, 4), 4, 512) for hf in range(2)] for c in range(2)]

        def add_ffn(f):
            gate, up, down = [], [], []
            for q in range(NQ + 1):
                if q < NQ:
                    gate.append(add(0, kcols(A["w_ffn_gate"][f], q * S, S), KC, S))
                if q:
                    down.append(add(0, A["w_ffn_down"][f][(q - 1) * S:q * S, :].rearrange("(k p) n -> p k n", p=P), 2, D))
                if q < NQ:
                    up.append(add(0, kcols(A["w_ffn_up"][f], q * S, S), KC, S))
            FFW[f] = (gate, up, down)

        def add_ple(f):
            pr = add(0, A["w_ple_proj"][f].rearrange("(k p) n -> p k n", p=P), 2, D)
            PLW[f] = (pr, [[add(0, kcols(A["w_ple_gate"][f], 512 * c, 512, 4 * hf, 4), 4, 512) for hf in range(2)]
                           for c in range(2)])

        add_proj(0, A["w_in_ab"][0], [(512 * c, 512, 512 * c) for c in (0, 1, 3, 4, 2, 5)])
        add_out(0, A["w_out_ab"][0])
        add_ffn(0)
        add_ple(0)
        add_proj(1, A["w_in_nsa"][0], [(512 * c, 512, 512 * c) for c in range(5)] + [(2560, 48, 2560)])
        for kv, name in enumerate(("cmp_k_w1", "cmp_v_w1")):
            CMPW[kv] = add(0, kcols(A[name][0], 0, P, 0, CMP_LEN // 2), CMP_LEN // 2, P)
        add_out(1, A["w_out_nsa"][0])
        add_ffn(1)
        add_ple(1)
        for l in range(2):
            seg = SEG[2 + l]
            if l:
                RAW0[2] = RAW0[1]
                SPL0[2] = SPL0[1]
            add_proj(2 + l, A["w_in_2"][l], [(0, 512, 0), (512, 256, 512)])
            CVW[l] = [[add(seg, kcols(A["w_in_2"][l], 768 + 512 * c + S * hf, S), KC, S) for hf in range(2)]
                      for c in range(3)]
            add_out(2 + l, A["w_out_2"][l])
            RAW0[seg + 1] = (RAW0[seg] + len(stream[seg])) % RAW
            SPL0[seg + 1] = (SPL0[seg] + len(stream[seg])) % SPL

        def at(j, per_job, more):
            return j * per_job + more if isinstance(j, int) else j * per_job + (2 * per_job + more)

        def gate_up(j):
            q0 = 2 if isinstance(j, int) and j == 0 else 0
            return [(q0 + 2 * m + hf, m, hf) for m in range(2) for hf in range(2)]

        def down_at(last):
            return 0 if last else 4

        def job_place(l, q):
            return (RAW0[2 * l + 1] + q - 2) % RAW

        def job_parts(l, q, shape=None):
            two = [parts[:, (SPL0[2 * l + 1] + q - 2) % SPL, i, :] for i in range(2)]
            return [x.rearrange("p (k n) -> p k n", k=shape[0]) for x in two] if shape else two

        SHAPES = [(4, DE), (4, DE), (2, D)]

        NEXT = {0: (0, PJ[0][0][0]), 1: (0, FFW[0][0][0]), 2: (0, PLW[0][0]), 3: (0, PJ[PJ_AT[1]][0][0]), 4: (0, FFW[1][0][0]),
                5: (0, PLW[1][0]), 6: (0, PJ[PJ_AT[2]][0][0]), 8: (2, PJ[PJ_AT[3]][0][0])}

        TP = [("norm", 0), ("attn", 0), ("norm", 1), ("norm", 2), ("norm", 3), ("attn", 1), ("norm", 4), ("norm", 5),
              ("norm", 6), ("attn2", 0), ("norm", 7), ("norm", 8), ("attn2", 1), ("norm", 9)]
        TPN = [8 if kind != "attn2" else 4 for kind, _ in TP]

        def tp_chunks(m):
            return sum(TPN[:m])

        def head_list(layer):
            z = []
            if layer == 0:
                for part in range(2):
                    for kind in range(2):
                        for c in range(4):
                            c0 = 1536 * part + 512 * kind + 128 * c
                            z.append(([qkv_t(t)[:, c0:c0 + P] for t in range(NT)], qk[:, 8 * kind + 4 * part + c, :],
                                      2 * part + kind))
            elif layer == 1:
                for c in range(8):
                    z.append(([qkv_t(t)[:, 128 * c:128 * c + P] for t in range(NT)], qk[:, c, :], 4))
                for c in range(8):
                    z.append(([xs[:, t, 128 * c:128 * c + P] for t in range(NT)], qk[:, 8 + c, :], 5 + c // 4))
            else:
                for c in range(4):
                    z.append(([qkv2[:, t, 128 * c:128 * c + P] for t in range(NT)], qk[:, c, :], None))
                for c in range(KV2):
                    z.append(([xs[:, t, 128 * c:128 * c + P] for t in range(NT)], qk[:, 8 + c, :], None))
            return z

        QN = [4, 10, 4, 4]
        QT = [head_list(l) for l in range(4)]
        QT_AT = [sum(len(q) for q in QT[:l]) for l in range(5)]

        QT_V = [sum(2 * (len(q) // 4) for q in QT[:l]) for l in range(5)]
        QT_A = [QT_AT[l] - QT_V[l] for l in range(5)]

        class Unit:
            pass

        def unit_list(layer):
            us = []
            for hh in range(NH if layer < 2 else HEADS2):
                lo = HD * (hh % 2)
                for t in range(NT):
                    for br in range(3 if layer == 1 else 1):
                        u = Unit()
                        u.t, u.h, u.br, u.layer = t, hh, br, layer
                        u.q = qk[lo:lo + HD, hh // 2, P * t:P * (t + 1)]
                        u.nk = P * (t + 1) if layer < 2 else S
                        u.bias = view(band[:, hh % NBAND if layer < 2 else 0, :], 255 + P * t, [[-1, u.nk]])
                        kt = range(u.nk // P)
                        if layer == 0:
                            u.k = qk[lo:lo + HD, 8 + hh // 2, 0:u.nk]
                            vc = 1024 + HD * hh if hh < 8 else 2560 + HD * (hh - 8)
                            u.v = [qkv_t(i)[:, vc:vc + HD] for i in kt]
                        elif layer == 1 and br < 2:
                            g = hh // (NH // NG)
                            u.k = qk[lo:lo + HD, 8 + 4 * br + g, 0:u.nk]
                            vc = (1792 if br == 0 else 2304) + HD * g
                            u.v = [qkv_t(i)[:, vc:vc + HD] for i in kt]
                        elif layer == 1:
                            g = hh // (NH // NG)
                            u.nk = NCMP
                            u.k = cmpT[lo:lo + HD, g, 0:NCMP]
                            u.bias = view(band[:, hh % NBAND, :], 224 + P * t, [[-CMP_STRIDE, NCMP]])
                            u.v = [cmpk[0:NCMP, 1, g, :]]
                        else:
                            g = hh // (HEADS2 // KV2)
                            u.k = qk[lo:lo + HD, 8 + g, 0:u.nk]
                            u.v = [qkv2[:, i, 640 + HD * g:640 + HD * (g + 1)] for i in kt]
                        u.o = xs[:, t, HD * hh:HD * (hh + 1)]
                        us.append(u)
            return us

        UN = [unit_list(l) for l in range(4)]
        U_AT = [sum(len(u) for u in UN[:l]) for l in range(5)]

        R_NORM = [2 * n for n in range(11)]
        R_HEAD = {0: 22, 1: 86}
        R_CMP = 134
        R_ATT = [138, 142]
        R_CONV = [140, 144]
        ROOTS, ROOT_AT = [], {}

        def root(key, wait, col, n, width, parts=P):
            ROOT_AT[key] = len(ROOTS) + 1
            ROOTS.append((wait, col, n, parts, width))

        root(("norm", 0), (sq_done, 2), R_NORM[0], 2, D)
        for part in range(2):
            root(("head", 0, part), (hss, 2 * part + 2), R_HEAD[0] + 32 * part, 32, HD)
        for n in range(1, 4):
            root(("norm", n), (sq_done, 2 * n + 2), R_NORM[n], 2, D)
        for part in range(2):
            root(("head", 1, part), (hss, 4 + 2 * part + 2), R_HEAD[1] + 32 * part, 32 - 16 * part, HD)
        root("cmp", (ss_done, 1), R_CMP, 4, HD, NCMP)
        for n in range(4, 7):
            root(("norm", n), (sq_done, 2 * n + 2), R_NORM[n], 2, D)
        root(("conv", 0), (yss_done, 1), R_CONV[0], 2, CW)
        root(("att", 0), (on_ready, 2), R_ATT[0], 2, CW)
        for n in range(7, 9):
            root(("norm", n), (sq_done, 2 * n + 2), R_NORM[n], 2, D)
        root(("conv", 1), (yss_done, 2), R_CONV[1], 2, CW)
        root(("att", 1), (on_ready, 4), R_ATT[1], 2, CW)
        for n in range(9, 11):
            root(("norm", n), (sq_done, 2 * n + 2), R_NORM[n], 2, D)

        PARS = []

        def par(dst, src):
            PARS.append((dst, src))

        for r0, name in ((0, "norm_mix"), (16, "norm_ffn"), (32, "norm_ple"), (48, "norm_mix_2"), (64, "norm_ffn_2")):
            par(prm[r0:r0 + 16, 0, :], A[name].rearrange("l (k p) -> (l k) p", p=P))
        par(prm[G_ATT:G_ATT + 8, 0, :], A["norm_attn_out_2"].rearrange("l (k p) -> (l k) p", p=P))
        par(prm[G_CONV:G_CONV + 8, 0, :], A["norm_conv_out_2"].rearrange("l (k p) -> (l k) p", p=P))
        par(prm[G_CW:G_CW + 24, 0, :], A["conv_w_2"].rearrange("l j (k p) -> (l j k) p", p=P))
        for kv, name in enumerate(("cmp_k_b1", "cmp_v_b1")):
            par(prm[G_B1 + kv:G_B1 + kv + 1, 0, :], A[name])
        NPAR0 = len(PARS)
        for half in range(2):
            cols = slice(HD * half, HD * (half + 1))
            for r, name in enumerate(("qn_moba", "kn_moba", "qn_dil", "kn_dil", "qn_nsa", "kn_slc", "kn_win", "kn_cmp")):
                par(prm[r:r + 1, 1, cols], A[name])
        for kv, name in enumerate(("cmp_k_pos", "cmp_v_pos")):
            par(prm[H_POS + 16 * kv:H_POS + 16 * (kv + 1), 1, :], A[name][0].rearrange("(i l) d -> i (l d)", l=2))
        for l in range(2):
            par(sink[:, l, 0, :], A["attn_sink_2"][l:l + 1, :].broadcast_to([P, HEADS2]))
            par(brt[:, l, 0:NEG], A["b_router_group_2"][l:l + 1, :].broadcast_to([P, NEG]))
            par(brt[:, l, NEG:NEG + NE], A["b_router_expert_2"][l:l + 1, :].broadcast_to([P, NE]))
        for kv, c in enumerate("kv"):
            par(w2[:, kv, :], A[f"cmp_{c}_w2"][0])
            par(b2[:, kv, :], A[f"cmp_{c}_b2"].broadcast_to([P, HD]))

        def jobs_work():
            return rt[0:NE, 1024:1024 + JOBS], rt[0:NE, 1088:1088 + JOBS], rt[0:NE, 1150:1151]

        block = ctx.enter_context(nc.Block())

        @block.sync
        def _(sp):
            sp.dma_start(h[:], A["x"][0].rearrange("(t p) d -> p t d", p=P)).then_inc(x_loaded, 16)

            def load(seg, i):
                dst, src, place, _, _ = stream[seg][i]
                if i >= RAW:
                    sp.wait_ge(lo_done[seg], i - RAW + 1)
                elif seg:
                    sp.wait_ge(lo_done[1], at(more, 6, i - RAW + 1))
                sp.dma_start(dst, src).then_inc(arrived[seg][place], 16)

            ws = [[A[n][l] for n in ("w_expert_gate_2", "w_expert_up_2", "w_expert_down_2")] for l in range(2)]

            def load_job(l, j, e, q, m, hf):
                if isinstance(j, int) and 6 * j - 2 + q < RAW:
                    sp.wait_ge(lo_done[2 * l], len(stream[2 * l]) - RAW + 6 * j - 2 + q + 1)
                else:
                    sp.wait_ge(lo_done[2 * l + 1], at(j, 6, q - 7))
                k, n = SHAPES[m]
                place = job_place(l, q)
                w = ws[l][m][bass.ds(e, 1), :, :] if not isinstance(e, int) else ws[l][m][e:e + 1, :, :]
                src = w[:, P * k * hf:P * k * (hf + 1), :].rearrange("e (k p) n -> p (e k) n", p=P)
                sp.dma_start(raw[:, place, :].rearrange("p (k n) -> p k n", k=k), src).then_inc(arrived[2 * l + 1][place], 16)

            def expert(j):
                return sp.value_load(tab[0:1, bass.ds(j, 1)], min_val=0, max_val=NE - 1)

            for l in range(2):
                seg = 2 * l
                for i in range(len(stream[seg])):
                    load(seg, i)
                for q, m, hf in gate_up(0):
                    load_job(l, 0, 0, q, m, hf)
                sp.wait_ge(tab_done, l + 1)
                more = sp.value_load(tab[0:1, 2 * JOBS:2 * JOBS + 1], min_val=NS // W - 2, max_val=JOBS - 2)

                def step(j):
                    e, e1 = expert(at(j, 1, 0)), expert(at(j, 1, -1))
                    for q, m, hf in gate_up(j):
                        load_job(l, j, e, q, m, hf)
                    for hf in range(2):
                        load_job(l, j, e1, down_at(False) + hf, 2, hf)

                step(1)
                with sp.Fori(0, more) as j:
                    step(j)
                e1 = expert(at(more, 1, -1))
                for hf in range(2):
                    load_job(l, more, e1, down_at(True) + hf, 2, hf)
            sp.wait_ge(out_ready, 2)
            sp.dma_start(out[0].rearrange("(t p) d -> p t d", p=P), xs[:]).then_inc(stored, 16)
            sp.wait_ge(stored, 16)

        @block.gpsimd
        def _(pool):
            def bands(q0, q1):
                for q in range(q0, q1):
                    if q >= 2:
                        pool.wait_ge(s_max, U_AT[(q - 2) // 4] + ((q - 2) % 4 + 1) * (len(UN[(q - 2) // 4]) // 4))
                    row = 4 * (q % 4) + (NH if 2 <= q < 4 else 0)
                    src = bass.AP(tensor=scr.tensor, offset=512 * row, ap=[[1, P], [512, 4], [1, NB]])
                    nc.gpsimd.dma_start(band[:, 4 * (q % 2):4 * (q % 2 + 1), :], src).then_inc(band_loaded[q % 2], 16)

            def load_p(l):
                nc.gpsimd.dma_start(rowsP, A["p"][l, 0].rearrange("(t p) c -> p t c", p=P)).then_inc(p_loaded, 16)

            nc.gpsimd.memset(mhalf[:], -0.5).then_inc(pch, 1)
            for dst, src in PARS[NPAR0:]:
                nc.gpsimd.dma_start(dst, src).then_inc(par2_loaded, 16)
            for r, (wait, col, n, parts_n, width) in enumerate(ROOTS):
                for l in range(2):
                    if r == ROOT_AT["cmp" if l else ("head", 0, 1)]:
                        bands(4 * l + 2, 4 * l + 4)
                        pool.wait_ge(o_ready, U_AT[l + 1])
                        load_p(l)
                    if l and r == ROOT_AT[("head", 0, 1)]:
                        bands(4, 6)
                if r == ROOT_AT[("norm", 0)]:
                    pool.wait_ge(trow_done, 2)
                    for m in range(2):
                        nc.gpsimd.dma_start(scr[NH * m:NH * (m + 1), :], trow[:, 512 * m:512 * (m + 1)]).then_inc(scr_written, 16)
                    pool.wait_ge(scr_written, 32)
                    bands(0, 2)
                for l in range(2):
                    if r == ROOT_AT[("norm", 7 + 2 * l)]:
                        pool.wait_ge(xs_rounded, l + 1)
                        nc.gpsimd.tensor_tensor(xsp[1], xs[:].rearrange("p t d -> p (t d)"), xsp[0].bitcast(F32), ALU.subtract)\
                            .then_inc(xsp_ready, 1)
                if r == ROOT_AT[("norm", 3)]:
                    for l in range(2):
                        nc.gpsimd.dma_start(wr[:, l, :, 0:NEG], A["w_router_group_2"][l].rearrange(
                            "(k p) n -> p k n", p=P)).then_inc(wr_loaded, 16)
                        nc.gpsimd.dma_start(wr[:, l, :, NEG:], A["w_router_expert_2"][l].rearrange(
                            "(k p) n -> p k n", p=P)).then_inc(wr_loaded, 16)
                if r == ROOT_AT[("norm", 4)] - 1:
                    pool.wait_ge(s_max, U_AT[2])
                    wb = A["window_band"]
                    nc.gpsimd.dma_start(band[:, 0, :], bass.AP(tensor=wb.tensor, offset=0, ap=[[1, P], [1, NB]]))\
                        .then_inc(band_loaded[0], 16)
                if r == ROOT_AT[("norm", 10)] - 1:
                    pool.wait_ge(yt_ready, 16)
                    nc.gpsimd.dma_start(gfin, A["norm_final_2"].rearrange("(a d) -> a d", a=1).broadcast_to([P, D]))\
                        .then_inc(par2_loaded, 16)
                pool.wait_ge(*wait)
                a = rms[0:parts_n, col:col + n]
                nc.gpsimd.tensor_scalar(a, a, float(width * EPS), None, ALU.add).then_inc(pch, 1)
                pool.wait_ge(pch, r + 2)
                nc.gpsimd.tensor_tensor(a, a, mhalf[0:parts_n, 0:n], ALU.pow).then_inc(rstd_done, 1)

        @block.scalar
        def _(act):
            for dst, src in PARS[:NPAR0]:
                act.dma_start(dst, src).then_inc(par_loaded, 16)
            act.dma_start(cst[:], A["consts"]).then_inc(cst_loaded, 16)
            act.dma_start(oneh, A["onehot"]).then_inc(rel_loaded, 16)
            act.dma_start(tmask, A["row_masks"]).then_inc(rel_loaded, 16)
            act.dma_start(relb[:], A["rel_bias"]).then_inc(rel_loaded, 16)

            split = {0: 0, 2: 0}

            def split_to(seg, n):
                while split[seg] < min(n, len(stream[seg])):
                    k = split[seg]
                    _, _, place, there, (kk, nn) = stream[seg][k]
                    act.wait_ge(arrived[seg][place], there)
                    if k >= SPL:
                        act.wait_ge(used[seg], k - SPL + 1)
                    elif seg:
                        act.wait_ge(yt_ready, 8)
                    nc.scalar.activation(parts[:, (SPL0[seg] + k) % SPL, 0, 0:kk * nn], raw[:, place, 0:kk * nn],
                                         ACT.Copy).then_inc(hi_done[seg], 1)
                    split[seg] += 1

            def squares(n):
                if 0 < n <= 6:
                    split_to(0, NEXT[n][1] + 1)
                if n:
                    act.wait_ge(h_done, 4 * n)
                else:
                    act.wait_ge(x_loaded, 16)
                for t in range(NT):
                    nc.scalar.activation(xs[:, t, :], h[:, t, :], ACT.Square,
                                         accum_out=rms[:, R_NORM[n] + t:R_NORM[n] + t + 1]).then_inc(sq_done, 1)
                if n in NEXT:
                    split_to(NEXT[n][0], NEXT[n][1] + SPL)

            def evac_tp(m):
                kind, n = TP[m]
                if m == 0:
                    act.wait_ge(set_done, 1)
                for c in range(TPN[m]):
                    act.wait_ge(tp_ready, (tp_chunks(m) + c) // 2 + 1)
                    src = pb[4 + c // 2][:, S * (c % 2):S * (c % 2 + 1)]
                    if kind == "attn":
                        i = nc.scalar.activation(xT[:, 0, c, :], src, ACT.Copy)
                    else:
                        col = G_NORM[n] if kind == "norm" else G_ATT + 4 * n
                        i = nc.scalar.activation(xT[:, 0, c, :], src, ACT.Copy, scale=gT[:, col + c:col + c + 1])
                    i.then_inc(xT_a, 1)

            def evac_proj(layer, hi):
                seg = SEG[layer]
                for g in range(PJ_AT[layer], hi):
                    halves, n, dst = PJ[g]
                    split_to(seg, halves[1] + 3)
                    act.wait_ge(pj_ready, g + 1)
                    d = qkv_t(0)[:, dst:dst + n] if layer < 2 else qkv2[:, 0, dst:dst + n]
                    nc.scalar.activation(d, pb[(2 * g) % 4][:, 0:n], ACT.Copy).then_inc(pj_a, 1)
                    if layer < 2 and g - PJ_AT[layer] in HEADS_AT[layer]:
                        head_squares(layer, HEADS_AT[layer].index(g - PJ_AT[layer]), g + 1)

            def head_squares(layer, part, groups):
                act.wait_ge(pj_a, groups)
                act.wait_ge(pj_v, groups)
                for t in range(NT):
                    if part:
                        act.wait_ge(hss, 4 * layer + t + 1)
                    if layer == 0 or part == 0:
                        src, dst = qkv_t(t)[:, 1536 * part:1536 * part + D], xs[:, t, :]
                    else:
                        src = qkv_t(t)[:, 1536:2560].rearrange("p (b c) -> p b c", b=2)[:, :, 0:256]
                        dst = xs[:, t, 0:512].rearrange("p (b c) -> p b c", b=2)
                    nc.scalar.activation(dst, src, ACT.Square).then_inc(hsq, 1)

            def compress_in():
                for b in range(4):
                    act.wait_ge(cT_ready, 1)
                    kv, g = b // 2, 2 * (b % 2)
                    x = pb[4 + b][:].rearrange("p (g s) -> p g s", g=2)
                    nc.scalar.activation(xc[0:HD, kv, 0, g:g + 2, :], x[0:HD], ACT.Copy).then_inc(cT_rounded, 1)
                    nc.scalar.activation(xc[HD:P, kv, 0, g:g + 2, 0:S - 1], x[0:HD, :, 1:S], ACT.Copy).then_inc(cT_rounded, 1)
                nc.scalar.activation(posr[:, :, 0, :], g2T[:, H_POS:HEAD_ROWS].rearrange("p (v l) -> p v l", v=2), ACT.Copy)\
                    .then_inc(cT_rounded, 1)

            def evac_heads(layer):
                for z, (_, dst, gain) in enumerate(QT[layer]):
                    g = QT_AT[layer] + z
                    if z // 2 % 2 == 0:
                        act.wait_ge(qt_ready, g // 2 + 1)
                        src = pb[4 + (z // 2) % 4][:, S * (z % 2):S * (z % 2 + 1)]
                        if gain is None:
                            i = nc.scalar.activation(dst, src, ACT.Copy)
                        else:
                            i = nc.scalar.activation(dst, src, ACT.Copy, scale=g2T[:, gain:gain + 1])
                        i.then_inc(qt_a, 1)

            def attention(layer):
                us = UN[layer]
                for i in range(len(us) + 2):
                    if i < len(us):
                        u, g = us[i], U_AT[layer] + i
                        act.wait_ge(s_max, g + 1)
                        if layer >= 2:
                            c = U_AT[2]
                            nc.scalar.activation(esink[:, g - c:g - c + 1], sink[:, layer - 2, 0, u.h:u.h + 1], ACT.Exp,
                                                 bias=nmax[:, g:g + 1])
                        s = sbuf_s[:, g % 4, 0:u.nk]
                        nc.scalar.activation(s, s, ACT.Exp, scale=-1.0, bias=nmax[:, g:g + 1],
                                             accum_out=den[:, g:g + 1]).then_inc(e_done, 1)
                    if i >= 2:
                        u, g = us[i - 2], U_AT[layer] + i - 2
                        act.wait_ge(pt_ready, g + 1)
                        if g >= 4:
                            act.wait_ge(o_ready, g - 3)
                        n, kp = (P * len(u.v), P) if u.nk > NCMP else (P, NCMP)
                        nc.scalar.activation(
                            sbuf_p[0:kp, g % 4, 0:n], pb[2 + g % 2][0:kp, 0:n], ACT.Copy).then_inc(pt_done, 1)

            def ffn(f):
                gate, up, down = FFW[f]
                for q in range(NQ):
                    split_to(0, up[q] + 1)
                    act.wait_ge(used[0], gate[q] + 1)
                    if q:
                        act.wait_ge(hT_done, NQ * f + q)
                    nc.scalar.activation(th, pb[4 + q % 2][:].rearrange("p (a b) -> p a b", a=2), ACT.Tanh, scale=0.5)\
                        .then_inc(th_done, 1)
                split_to(0, down[-1] + 1)

            def out_splits(layer):
                split_to(SEG[layer], OPW[layer][1][1] + 1)

            def transpose_p(f):
                act.wait_ge(p_ready, f + 1)
                nc.scalar.activation(hidT[:, :, 0, :], pb[4][:].rearrange("p (a b) -> p a b", a=2), ACT.Copy)\
                    .then_inc(pT_done, 1)

            def ple(f):
                split_to(0, PLW[f][1][1][1] + 1)
                for c in range(2):
                    for t in range(NT):
                        if t:
                            act.wait_ge(used[0], PLW[f][1][c][1] + 1)
                        else:
                            act.wait_ge(ple_ready, 2 * f + c + 1)
                        nc.scalar.activation(xs[:, t, 512 * c:512 * (c + 1)], pb[4 + 2 * c + t][:], ACT.Tanh,
                                             scale=0.5).then_inc(ple_th, 1)

            def conv(l):
                seg = SEG[2 + l]
                for c in range(4):
                    split_to(seg, CVW[l][c // 2][c % 2] + 3)
                    act.wait_ge(used[seg], CVW[l][c // 2][c % 2] + 1)
                    dst = (gbT if c < 2 else gcT)[:, 512 * (c % 2):512 * (c % 2 + 1)]
                    nc.scalar.activation(dst, pb[4 + c][:], ACT.Copy).then_inc(gb_done, 1)
                split_to(seg, OPW[2 + l][0][1] + 2)
                act.wait_ge(y_done, l + 1)
                nc.scalar.activation(gcT, yT, ACT.Square).then_inc(ysq_done, 1)

            def moe(l):
                seg = 2 * l + 1

                def round_half(j, q):
                    place = job_place(l, q)
                    act.wait_ge(arrived[seg][place], at(j, 16, 0 if q < 2 else 16))
                    if isinstance(j, int) and j == 0 and q < SPL + 2:
                        act.wait_ge(used[2 * l], len(stream[2 * l]) - SPL + q - 1)
                    else:
                        act.wait_ge(used[seg], at(j, 6, q - SPL - 1))
                    nc.scalar.activation(job_parts(l, q)[0], raw[:, place, :], ACT.Copy).then_inc(hi_done[seg], 1)

                round_half(0, 2)
                squares(7 + 2 * l)
                act.wait_ge(wr_loaded, 64)
                nc.scalar.activation(wrs[:, :, 0, :], wr[:, l, :, :], ACT.Copy).then_inc(wr_rounded, 1)
                round_half(0, 3)
                evac_tp(10 + 3 * l)
                round_half(0, 4)
                act.wait_ge(rt_ready, l + 1)
                nc.scalar.activation(xsp[0], xs[:].rearrange("p t d -> p (t d)"), ACT.Copy).then_inc(xs_rounded, 1)
                act.wait_ge(rt_x, 2 * l + 1)
                nc.scalar.activation(rt[:, 112:120], rt[:, 112:120], ACT.Exp).then_inc(rt_e, 1)
                act.wait_ge(rt_x, 2 * l + 2)
                nc.scalar.activation(rt[:, 364:366], rt[:, 364:366], ACT.Exp).then_inc(rt_e, 1)
                col = G_NORM[7 + 2 * l]
                for k in range(0, KC, 2):
                    act.wait_ge(ga_ready, KC * l + k + 1)
                    nc.scalar.activation(xsT[:, k, 0:NS], pb[4 + k % 4][:], ACT.Copy,
                                         scale=gT[:, col + k:col + k + 1]).then_inc(xsT_a, 1)
                more = act.value_load(tab[0:1, 2 * JOBS:2 * JOBS + 1], min_val=NS // W - 2, max_val=JOBS - 2)
                act.wait_ge(xsT_a, 4 * (l + 1))
                act.wait_ge(xsT_v, 5 * (l + 1))

                def window(j):
                    s0 = act.value_load(tab[0:1, bass.ds(at(j, 1, JOBS), 1)], min_val=0, max_val=NS)
                    if not isinstance(j, int):
                        act.wait_ge(used[seg], at(j, 6, -4))
                    elif j:
                        act.wait_ge(used[seg], 4)
                    nc.scalar.activation(xw[:, :, 0:W], xsT[:, :, bass.ds(s0, W)], ACT.Copy).then_inc(xw_rounded[l], 1)

                def products(j, dst, done, bank, q):
                    act.wait_ge(used[seg], at(j, 6, q - 1))
                    nc.scalar.activation(dst, pb[bank][:], ACT.Copy).then_inc(done[l], 1)

                def first_parts(j, back, m, dst):
                    act.wait_ge(gt_ready[l], at(j, 2, m + 1 - 2 * back))
                    nc.scalar.activation(dst.rearrange("p (k s) -> p k s", k=4),
                                         pb[2 + m][:].rearrange("p (k i s) -> p k i s", k=4, i=2)[:, :, 0, :],
                                         ACT.Copy).then_inc(eg_first[l], 1)

                def tanh(j, back):
                    act.wait_ge(g_added[l], at(j, 1, 1 - back))
                    nc.scalar.activation(ea, eg, ACT.Tanh, scale=0.5).then_inc(eth_done[l], 1)

                def results(j, back):
                    act.wait_ge(used[seg], at(j, 6, -2 if back == 2 else 0))
                    for c in range(2):
                        nc.scalar.activation(ys[:, 512 * c:512 * (c + 1)], pb[4 + c][:], ACT.Copy).then_inc(ys_done[l], 1)

                def to_slots(j, back):
                    s0 = act.value_load(tab[0:1, bass.ds(at(j, 1, JOBS - back), 1)], min_val=0, max_val=NS)
                    for b in range(2):
                        act.wait_ge(yt2_ready[l], at(j, 2, b + 1 - 2 * back))
                        nc.scalar.activation(ysT[:, 4 * b:4 * b + 4, bass.ds(s0, W)],
                                             pb[6 + b][:].rearrange("p (k i s) -> p k i s", k=4, i=2)[:, :, 0, :],
                                             ACT.Copy).then_inc(y_first[l], 1)

                def step(j):
                    later = not isinstance(j, int)
                    g0, g1, u0, u1 = (q for q, _, _ in gate_up(j))
                    window(j)
                    if later:
                        round_half(j, g0)
                    if later or j:
                        round_half(j, g1)
                    if later:
                        results(j, 2)
                    if later or j:
                        round_half(j, u0)
                        first_parts(j, 1, 0, eg)
                        first_parts(j, 1, 1, eu)
                    round_half(j, u1)
                    if later or j:
                        tanh(j, 1)
                    if later:
                        to_slots(j, 2)
                    if later or j:
                        round_half(j, down_at(False))
                    products(j, gs, gs_done, 0, g1)
                    if later or j:
                        round_half(j, down_at(False) + 1)
                    if not later and j == 0:
                        round_half(1, 0)
                    products(j, us, us_done, 1, u1)

                step(0)
                step(1)
                with act.Fori(0, more) as j:
                    step(j)
                results(more, 2)
                first_parts(more, 1, 0, eg)
                first_parts(more, 1, 1, eu)
                tanh(more, 1)
                round_half(more, down_at(True))
                round_half(more, down_at(True) + 1)
                to_slots(more, 2)
                results(more, 1)
                to_slots(more, 1)
                for i in range(0, 8, 2):
                    act.wait_ge(yt_ready, 8 * l + i + 1)
                    nc.scalar.activation(ysort[:, i // 2, 0:512], pb[4 + i % 4][:], ACT.Copy).then_inc(yt_done, 1)

            squares(0)
            evac_tp(0)
            evac_proj(0, PJ_AT[1])
            act.wait_ge(scr_written, 32)
            evac_heads(0)
            split_to(0, OPW[0][0][0] + 1)
            attention(0)
            evac_tp(1)
            out_splits(0)
            squares(1)
            evac_tp(2)
            ffn(0)
            transpose_p(0)
            squares(2)
            evac_tp(3)
            ple(0)
            squares(3)
            evac_tp(4)
            evac_proj(1, PJ_AT[2])
            split_to(0, OPW[1][0][0] + 1)
            compress_in()
            act.wait_ge(pj_a, PJ_AT[2])
            act.wait_ge(pj_v, PJ_AT[2])
            for t in range(NT):
                nc.scalar.activation(gates[:, t, :], qkv_t(t)[:, 2560:2608], ACT.Tanh, scale=0.5).then_inc(g_th, 1)
            for kv in range(2):
                act.wait_ge(gel_in, kv + 1)
                nc.scalar.activation(cmph[:, kv, 2, 0:60], cmph[:, kv, 1, 0:60], ACT.Tanh, scale=GELU).then_inc(gel_th, 1)
                split_to(0, OPW[1][0][0] + kv + 2)
            evac_heads(1)
            attention(1)
            evac_tp(5)
            out_splits(1)
            squares(4)
            evac_tp(6)
            ffn(1)
            transpose_p(1)
            squares(5)
            evac_tp(7)
            ple(1)
            for l in range(2):
                squares(6 + 2 * l)
                evac_tp(8 + 3 * l)
                evac_proj(2 + l, PJ_AT[2 + l] + 2)
                conv(l)
                evac_heads(2 + l)
                attention(2 + l)
                for t in range(NT):
                    act.wait_ge(o_done, U_AT[3 + l])
                    nc.scalar.activation(sbuf_s[:, 2 * t:2 * t + 2, :], xs[:, t, 0:CW].rearrange("p (a b) -> p a b", a=2),
                                         ACT.Square, accum_out=rms[:, R_ATT[l] + t:R_ATT[l] + t + 1]).then_inc(on_ready, 1)
                evac_tp(9 + 3 * l)
                out_splits(2 + l)
                moe(l)
            squares(10)

        @block.tensor
        def _(pe):
            mm = nc.tensor.matmul
            pe.wait_ge(cst_loaded, 16)
            pe.wait_ge(par_loaded, 16 * NPAR0)
            nc.tensor.transpose(pb[0][:, 0:PRM_ROWS], prm[0:PRM_ROWS, 0, :], ident[0:PRM_ROWS, 0:PRM_ROWS])\
                .then_inc(set_ready, 1)

            def setup_rest():
                pe.wait_ge(rel_loaded, 48)
                mm(pb[1][0:NH, :], relb[:], oneh, start=True, stop=True).then_inc(set_ready, 1)
                pe.wait_ge(par2_loaded, 16 * (len(PARS) - NPAR0))
                nc.tensor.transpose(pb[2][:, 0:HEAD_ROWS], prm[0:HEAD_ROWS, 1, :], ident[0:HEAD_ROWS, 0:HEAD_ROWS])\
                    .then_inc(set_ready, 1)

            def three(out_ap, x, w, k, kw, xcols, wcols, first, last, flip=False):
                for n, (i, j) in enumerate(((0, 0), (1, 0), (0, 1))):
                    a, b = x[:, i, k, xcols], w[j][:, kw, wcols]
                    ins = mm(out_ap, b if flip else a, a if flip else b, start=first and n == 0, stop=last and n == 2)
                return ins

            def transposes(m):
                kind, n = TP[m]
                if kind == "norm":
                    pe.wait_ge(xs_ready, 2 * n + 2)
                elif kind == "attn":
                    pe.wait_ge(o_done, U_AT[n + 1])
                else:
                    pe.wait_ge(at_ready, 2 * n + 2)
                for c in range(TPN[m]):
                    b = pb[4 + c // 2]
                    for t in range(NT):
                        i = nc.tensor.transpose(b[:, S * (c % 2) + P * t:S * (c % 2) + P * (t + 1)],
                                                xs[:, t, P * c:P * (c + 1)], ident)
                    if c % 2:
                        i.then_inc(tp_ready, 1)

            def wait_xT(m):
                pe.wait_ge(xT_v, tp_chunks(m + 1))

            def project(layer, m):
                wait_xT(m)
                seg = SEG[layer]
                if layer == 0:
                    pe.wait_ge(set_done, 3)
                for g in range(PJ_AT[layer], PJ_AT[layer] + (6 if layer < 2 else 2)):
                    halves, n, _ = PJ[g]
                    for hf, s in enumerate(halves):
                        pe.wait_ge(lo_done[seg], s + 1)
                        w = both(seg, s)
                        for t in range(NT):
                            if g >= 2 and hf == 0:
                                pe.wait_ge(pj_v if t else pj_a, g - 1)
                            for k in range(4):
                                ins = three(pb[(2 * g + t) % 4][:, 0:n], xT, w, 4 * hf + k, k, slice(P * t, P * (t + 1)),
                                            slice(0, n), hf == 0 and k == 0, hf == 1 and k == 3)
                            if t:
                                ins.then_inc(used[seg], 1)
                            elif hf:
                                ins.then_inc(pj_ready, 1)
                    if layer == 1 and g == PJ_AT[1] + 4:
                        compress_turn()

            def compress_turn():
                pe.wait_ge(pj_a, PJ_AT[1] + 3)
                pe.wait_ge(pj_v, PJ_AT[1] + 3)
                for kv in range(2):
                    for g in range(NG):
                        b = pb[4 + 2 * kv + g // 2]
                        c0 = 1024 + 256 * kv + HD * g
                        for t in range(NT):
                            ins = nc.tensor.transpose(b[0:HD, S * (g % 2) + P * t:S * (g % 2) + P * (t + 1)],
                                                      qkv_t(t)[:, c0:c0 + HD], ident)
                ins.then_inc(cT_ready, 1)

            def heads(layer):
                for z, (src, _, _) in enumerate(QT[layer]):
                    if z == 0:
                        pe.wait_ge(qn_ready, sum(QN[:layer]) + QN[layer])
                    if z >= 8 and z % 2 == 0:
                        if z // 2 % 2 == 0:
                            pe.wait_ge(qt_a, QT_A[layer] + z // 2 - 2)
                        else:
                            pe.wait_ge(qt_v, QT_V[layer] + z // 2 - 3)
                    b = pb[4 + (z // 2) % 4]
                    for t in range(NT):
                        i = nc.tensor.transpose(b[:, S * (z % 2) + P * t:S * (z % 2) + P * (t + 1)], src[t], ident)
                    if z % 2:
                        i.then_inc(qt_ready, 1)

            def attention(layer):
                us = UN[layer]
                pe.wait_ge(qt_a, QT_A[layer + 1])
                pe.wait_ge(qt_v, QT_V[layer + 1])
                n = len(us)
                for i in range(n + 4):
                    if i < n:
                        u, g = us[i], U_AT[layer] + i
                        if layer == 1 and i == 2:
                            pe.wait_ge(cmpT_done, 1)
                        if g >= 3:
                            pe.wait_ge(s_max, g - 2)
                        mm(pb[4 + g % 3][:, 0:u.nk], u.q, u.k, start=True, stop=True).then_inc(s_ready, 1)
                    if 0 <= i - 3 < n:
                        u, g = us[i - 3], U_AT[layer] + i - 3
                        pe.wait_ge(e_done, g + 1)
                        if g >= 2:
                            pe.wait_ge(pt_done, g - 1)
                        if u.nk == NCMP:
                            ins = nc.tensor.transpose(pb[2 + g % 2][0:NCMP, 0:P], sbuf_s[:, g % 4, 0:NCMP], ident)
                        else:
                            for kt in range(len(u.v)):
                                ins = nc.tensor.transpose(pb[2 + g % 2][:, P * kt:P * (kt + 1)],
                                                          sbuf_s[:, g % 4, P * kt:P * (kt + 1)], ident)
                        ins.then_inc(pt_ready, 1)
                    if 0 <= i - 4 < n:
                        u, g = us[i - 4], U_AT[layer] + i - 4
                        pe.wait_ge(pt_done, g + 1)
                        if g >= 3:
                            pe.wait_ge(o_done, g - 2)
                        ob = pb[(0, 1, 7)[g % 3]][:, 0:HD]
                        kp = P if u.nk > NCMP else NCMP
                        for kt in range(len(u.v)):
                            ins = mm(ob, sbuf_p[0:kp, g % 4, P * kt:P * (kt + 1)], u.v[kt],
                                     start=(kt == 0), stop=(kt == len(u.v) - 1))
                        ins.then_inc(o_ready, 1)

            def out_proj(k, m):
                wait_xT(m)
                seg = SEG[k]
                if k >= 2:
                    pe.wait_ge(cx_done, 8 * (k - 1))
                for c in range(2):
                    for hf, s in enumerate(OPW[k][c]):
                        pe.wait_ge(lo_done[seg], s + 1)
                        w = both(seg, s)
                        apart = k >= 2
                        for t in range(NT):
                            b = pb[2 * c + t + (4 * hf if apart else 0)]
                            for kk in range(4):
                                ins = three(b[:], xT, w, 4 * hf + kk, kk, slice(P * t, P * (t + 1)), slice(0, 512),
                                            kk == 0 and (hf == 0 or apart), kk == 3 and (hf == 1 or apart))
                            if t:
                                ins.then_inc(used[seg], 1)
                            elif hf:
                                ins.then_inc(op_ready, 1)

            def ffn(f, m):
                gate, up, down = FFW[f]
                wait_xT(m)

                def into(bank, s):
                    pe.wait_ge(lo_done[0], s + 1)
                    for j in range(2):
                        for k in range(KC):
                            ins = three(bank[:, S * j:S * (j + 1)], xT, both(0, s), k, k, slice(0, S),
                                        slice(P * j, P * (j + 1)), k == 0, k == KC - 1, flip=True)
                    ins.then_inc(used[0], 1)

                for q in range(NQ + 1):
                    if q < NQ:
                        into(pb[4 + q % 2], gate[q])
                    if q:
                        pe.wait_ge(hT_done, NQ * f + q)
                        pe.wait_ge(lo_done[0], down[q - 1] + 1)
                        w = both(0, down[q - 1])
                        for j in range(2):
                            for t in range(NT):
                                for c in range(2):
                                    for n, (i, p) in enumerate(((0, 0), (1, 0), (0, 1))):
                                        ins = mm(pb[2 * c + t][:], hidT[:, j, i, P * t:P * (t + 1)],
                                                 w[p][:, j, 512 * c:512 * (c + 1)], start=(q == 1 and j == 0 and n == 0),
                                                 stop=(q == NQ and j == 1 and n == 2))
                        ins.then_inc(used[0], 1)
                    if q < NQ:
                        into(pb[6 + q % 2], up[q])

            def p_rows(f):
                pe.wait_ge(p_loaded, 16 * (f + 1))
                pe.wait_ge(hT_done, NQ * (f + 1))
                for k in range(2):
                    for t in range(NT):
                        ins = nc.tensor.transpose(pb[4][:, S * k + P * t:S * k + P * (t + 1)],
                                                  rowsP[:, t, P * k:P * (k + 1)], ident)
                ins.then_inc(p_ready, 1)

            def p_proj(f):
                pe.wait_ge(pT_v, f + 1)
                pe.wait_ge(h_done, 4 * (3 * f + 2))
                s = PLW[f][0]
                pe.wait_ge(lo_done[0], s + 1)
                w = both(0, s)
                for c in range(2):
                    for t in range(NT):
                        for k in range(2):
                            for n, (i, p) in enumerate(((0, 0), (1, 0), (0, 1))):
                                ins = mm(pb[2 * c + t][:], hidT[:, k, i, P * t:P * (t + 1)], w[p][:, k, 512 * c:512 * (c + 1)],
                                         start=(k == 0 and n == 0), stop=(k == 1 and n == 2))
                ins.then_inc(used[0], 1)

            def ple(f, m):
                wait_xT(m)
                for c in range(2):
                    for hf, s in enumerate(PLW[f][1][c]):
                        pe.wait_ge(lo_done[0], s + 1)
                        for t in range(NT):
                            for k in range(4):
                                ins = three(pb[4 + 2 * c + t][:], xT, both(0, s), 4 * hf + k, k, slice(P * t, P * (t + 1)),
                                            slice(0, 512), hf == 0 and k == 0, hf == 1 and k == 3)
                            if t:
                                ins.then_inc(used[0], 1)
                            elif hf:
                                ins.then_inc(ple_ready, 1)

            def compress():
                pe.wait_ge(pj_a, PJ_AT[2])
                pe.wait_ge(pj_v, PJ_AT[2])
                pe.wait_ge(cT_done, 9)
                for kv in range(2):
                    pe.wait_ge(lo_done[0], CMPW[kv] + 1)
                    w1 = both(0, CMPW[kv])
                    for x, cols in ((None, slice(0, 2 * NG * NCMP)), (posr[:, kv], slice(128, 130))):
                        for l in range(CMP_LEN // 2):
                            y = view(xc[:, kv], 2 * l, [[CMP_STRIDE, NCMP], [S, 2 * NG]]) if x is None else x[:, :, l]
                            for i in range(2):
                                ins = mm(pb[kv][:, cols], w1[i][:, l, :], y, start=(l == 0 and i == 0),
                                         stop=(l == CMP_LEN // 2 - 1 and i == 1))
                        if x is not None:
                            ins.then_inc(used[0], 1)
                for kv in range(2):
                    pe.wait_ge(gel_done, kv + 1)
                    for g in range(NG):
                        ins = mm(pb[2][0:NCMP, 256 * kv + HD * g:256 * kv + HD * (g + 1)],
                                 cmph[:, kv, 3, NCMP * g:NCMP * (g + 1)], w2[:, kv, :], start=True, stop=True)
                ins.then_inc(cmp_ready, 1)
                heads(1)
                pe.wait_ge(cmpn_done, 2)
                for g in range(NG):
                    ins = nc.tensor.transpose(pb[3][:, 16 * g:16 * g + NCMP],
                                              cmpd[0:NCMP, g, :, :].rearrange("p a b -> p (a b)"), ident[0:NCMP, 0:NCMP])
                ins.then_inc(cmpT_ready, 1)

            def conv(l):
                seg = SEG[2 + l]
                for c in range(3):
                    for half in range(2):
                        s = CVW[l][c][half]
                        pe.wait_ge(lo_done[seg], s + 1)
                        if c == 2:
                            pe.wait_ge(gb_done, 4 * l + half + 1)
                        b = pb[4 + (2 * c + half) % 4]
                        for q in range(2):
                            for k in range(KC):
                                ins = three(b[:, S * q:S * (q + 1)], xT, both(seg, s), k, k, slice(0, S),
                                            slice(P * q, P * (q + 1)), k == 0, k == KC - 1, flip=True)
                        ins.then_inc(used[seg], 1)

            def conv_sums(l):
                pe.wait_ge(ysq_done, l + 1)
                for t in range(NT):
                    for c in range(4):
                        ins = mm(pb[7][:, t:t + 1], gcT[:, S * c + P * t:S * c + P * (t + 1)], ones[:, 0:1],
                                 start=(c == 0), stop=(c == 3))
                ins.then_inc(yss_ready, 1)

            def moe(l):
                transposes(10 + 3 * l)
                wait_xT(10 + 3 * l)
                pe.wait_ge(wr_ready, l + 1)
                for t in range(NT):
                    for k in range(KC):
                        for i in range(2):
                            ins = mm(pb[0][:, P * t:P * t + 2 * (NEG + NE)], xT[:, i, k, P * t:P * (t + 1)],
                                     wrs[:, k, :, :].rearrange("p i n -> p (i n)"), start=(k == 0 and i == 0),
                                     stop=(k == KC - 1 and i == 1))
                ins.then_inc(rt_ready, 1)
                a = [rt[:, 384 + NE * t:384 + NE * (t + 1)] for t in range(NT)]
                pe.wait_ge(as_done, l + 1)
                for t in range(NT):
                    ins = mm(pb[1][0:NE, 0:P], a[t], ones[:], start=(t == 0), stop=(t == 1))
                ins.then_inc(cnt_ready, 1)
                mm(pb[2][:, 0:NE], tri, a[0], start=True, stop=True)
                mm(pb[2][:, NE:2 * NE], ones[:], a[0], start=True, stop=False)
                mm(pb[2][:, NE:2 * NE], tri, a[1], start=False, stop=True)
                pe.wait_ge(cnt_done, 2 * l + 2)
                cm, wm = rt[0:NE, 512:640], rt[0:NE, 640:768]
                mm(pb[3][:, 0:NE], cm, tri[0:NE, 0:NE], start=True, stop=True)
                mm(pb[3][0:NE, NE:NE + 1], tri[0:NE, 0:NE], cm[:, 0:1], start=True, stop=True)
                mm(pb[3][0:NE, NE + 1:NE + 2], tri[0:NE, 0:NE], wm[:, 0:1], start=True, stop=True)\
                    .then_inc(pos_ready, 1)
                pe.wait_ge(job_cols, l + 1)
                ja, jo, jv = jobs_work()
                mm(pb[1][0:1, 0:JOBS], ones[0:NE, 0:1], ja, start=True, stop=True)
                mm(pb[1][0:1, 64:64 + JOBS], jv, jo, start=True, stop=True)
                mm(pb[1][0:1, 128:129], wm[:, 0:1], ones[0:NE, 0:1], start=True, stop=True).then_inc(job_ready, 1)
                pe.wait_ge(sel_done, 2 * l + 1)
                pe.wait_ge(xsp_ready, l + 1)
                for k in range(KC):
                    if k >= 4:
                        if k % 2:
                            pe.wait_ge(xsT_v, 5 * l + 2 + (k - 4) // 2)
                        else:
                            pe.wait_ge(xsT_a, 4 * l + 1 + (k - 4) // 2)
                    for t in range(NT):
                        for i in range(2):
                            ins = mm(pb[4 + k % 4][:], xsp[i][:, D * t + P * k:D * t + P * (k + 1)], sel[:, t, :],
                                     start=(t == 0 and i == 0), stop=(t == 1 and i == 1))
                    ins.then_inc(ga_ready, 1)
                pe.wait_ge(sel_done, 2 * l + 2)
                for c in range(4):
                    b = pb[2 + c // 2]
                    for t in range(NT):
                        ins = nc.tensor.transpose(b[:, S * (c % 2) + P * t:S * (c % 2) + P * (t + 1)],
                                                  gsel[:, t, P * c:P * (c + 1)], ident)
                    if c % 2:
                        ins.then_inc(gct_ready, 1)
                seg = 2 * l + 1
                more = pe.value_load(tab[0:1, 2 * JOBS:2 * JOBS + 1], min_val=NS // W - 2, max_val=JOBS - 2)

                def products(j, q, m, hf):
                    pe.wait_ge(lo_done[seg], at(j, 6, q - 1))
                    w = job_parts(l, q, SHAPES[m])
                    for k in range(4):
                        for i in range(2):
                            ins = mm(pb[m][:], xw[:, 4 * hf + k, :], w[i][:, k, :], start=(hf == 0 and k == 0 and i == 0),
                                     stop=(hf == 1 and k == 3 and i == 1))
                    ins.then_inc(used[seg], 1)

                def turn(j, back, m, src, done):
                    pe.wait_ge(done[l], at(j, 1, 1 - back))
                    for q in range(4):
                        ins = nc.tensor.transpose(pb[2 + m][:, P * q:P * (q + 1)], src[:, P * q:P * (q + 1)], ident)
                    ins.then_inc(gt_ready[l], 1)

                def results(j, back):
                    pe.wait_ge(yadd_done[l], at(j, 2, 1 - 2 * back))
                    for b in range(2):
                        pe.wait_ge(ys_done[l], at(j, 2, b + 1 - 2 * back))
                        for q in range(4):
                            ins = nc.tensor.transpose(pb[6 + b][:, P * q:P * (q + 1)], ys[:, 512 * b + P * q:512 * b + P * (q + 1)],
                                                      ident)
                        ins.then_inc(yt2_ready[l], 1)

                def down(j, back, q0):
                    pe.wait_ge(eh_done[l], at(j, 1, 1 - back))
                    for hf in range(2):
                        pe.wait_ge(lo_done[seg], at(j, 6, q0 + hf - 1))
                        w = job_parts(l, q0 + hf, SHAPES[2])
                        for k in range(2):
                            for i in range(2):
                                for c in range(2):
                                    ins = mm(pb[4 + c][:], ehl[:, 2 * hf + k, :], w[i][:, k, 512 * c:512 * (c + 1)],
                                             start=(hf == 0 and k == 0 and i == 0), stop=(hf == 1 and k == 1 and i == 1))
                        ins.then_inc(used[seg], 1)

                def step(j):
                    later = not isinstance(j, int)
                    halves = gate_up(j)
                    pe.wait_ge(xw_ready[l], at(j, 1, 1))
                    if later or j:
                        turn(j, 1, 0, gs, gs_done)
                    products(j, *halves[0])
                    if later or j:
                        turn(j, 1, 1, us, us_done)
                    products(j, *halves[1])
                    if later:
                        results(j, 2)
                    products(j, *halves[2])
                    products(j, *halves[3])
                    if later or j:
                        down(j, 1, down_at(False))

                step(0)
                pe.wait_ge(gct_done, 2 * l + 2)
                step(1)
                with pe.Fori(0, more) as j:
                    step(j)
                turn(more, 1, 0, gs, gs_done)
                turn(more, 1, 1, us, us_done)
                results(more, 2)
                down(more, 1, down_at(True))
                results(more, 1)
                pe.wait_ge(yadd_done[l], at(more, 2, 1))
                for c in range(4):
                    for half in range(2):
                        i = 2 * c + half
                        if i >= 4:
                            pe.wait_ge(yt_done if half == 0 else yt_v, 4 * l + (i - 4) // 2 + 1)
                        for kk in range(4):
                            ins = nc.tensor.transpose(pb[4 + i % 4][:, P * kk:P * (kk + 1)],
                                                      ysT[:, 4 * half + kk, P * c:P * (c + 1)], ident)
                        ins.then_inc(yt_ready, 1)
                pe.wait_ge(yt_done, 4 * l + 4)
                pe.wait_ge(yt_v, 4 * l + 4)
                for c in range(2):
                    for t in range(NT):
                        for sc in range(4):
                            ins = mm(pb[2 * c + t][:], gcombT[:, sc, P * t:P * (t + 1)], ysort[:, sc, 512 * c:512 * (c + 1)],
                                     start=(sc == 0), stop=(sc == 3))
                        ins.then_inc(op_ready2, 1)

            transposes(0)
            setup_rest()
            project(0, 0)
            heads(0)
            attention(0)
            transposes(1)
            out_proj(0, 1)
            transposes(2)
            ffn(0, 2)
            p_rows(0)
            p_proj(0)
            transposes(3)
            ple(0, 3)
            transposes(4)
            project(1, 4)
            compress()
            attention(1)
            transposes(5)
            out_proj(1, 5)
            transposes(6)
            ffn(1, 6)
            p_rows(1)
            p_proj(1)
            transposes(7)
            ple(1, 7)
            for l in range(2):
                transposes(8 + 3 * l)
                project(2 + l, 8 + 3 * l)
                conv(l)
                conv_sums(l)
                heads(2 + l)
                attention(2 + l)
                transposes(9 + 3 * l)
                out_proj(2 + l, 9 + 3 * l)
                moe(l)

        @block.vector
        def _(dve):
            v = nc.vector
            chain = [0]

            def link(ins):
                chain[0] += 1
                ins.then_inc(dch, 1)
                dve.wait_ge(dch, chain[0])

            def root_wait(key):
                dve.wait_ge(rstd_done, ROOT_AT[key])

            link(v.memset(ones[:], 1.0))
            dve.wait_ge(set_ready, 1)
            v.tensor_copy(gT[:], pb[0][:, 0:PRM_ROWS]).then_inc(set_done, 1)

            def setup_rest():
                dve.wait_ge(set_ready, 2)
                for m in range(2):
                    v.scalar_tensor_tensor(trow[:, 512 * m:512 * (m + 1)], pb[1][0:NH, :], 8.0,
                                           tmask[:, 512 * m:512 * (m + 1)], ALU.mult, ALU.add).then_inc(trow_done, 1)
                dve.wait_ge(set_ready, 3)
                v.tensor_scalar(g2T[:, 0:H_POS], pb[2][:, 0:H_POS], 8.0, None, ALU.mult).then_inc(set_done, 1)
                v.tensor_copy(g2T[:, H_POS:], pb[2][:, H_POS:HEAD_ROWS]).then_inc(set_done, 1)
                link(v.tensor_scalar(sink[:, :, 1, :], sink[:, :, 0, :], -1.0, None, ALU.mult))

            split = {0: 0, 2: 0}

            def split_to(seg, n):
                while split[seg] < min(n, len(stream[seg])):
                    k = split[seg]
                    _, _, place, _, (kk, nn) = stream[seg][k]
                    dve.wait_ge(hi_done[seg], k + 1)
                    two = parts[:, (SPL0[seg] + k) % SPL, :, 0:kk * nn]
                    v.tensor_tensor(two[:, 1, :], raw[:, place, 0:kk * nn], two[:, 0, :].bitcast(F32), ALU.subtract)\
                        .then_inc(lo_done[seg], 1)
                    split[seg] += 1

            def normalise(n):
                if 0 < n <= 6:
                    split_to(0, NEXT[n][1] + 1)
                root_wait(("norm", n))
                for t in range(NT):
                    v.tensor_scalar(xs[:, t, :], h[:, t, :], rms[:, R_NORM[n] + t:R_NORM[n] + t + 1], float(D ** 0.5),
                                    ALU.mult, ALU.mult).then_inc(xs_ready, 1)
                if n in NEXT:
                    split_to(NEXT[n][0], NEXT[n][1] + 2)

            def evac_tp(m):
                kind, n = TP[m]
                for c in range(TPN[m]):
                    dve.wait_ge(xT_a, tp_chunks(m) + c // 2 * 2 + 2)
                    src = pb[4 + c // 2][:, S * (c % 2):S * (c % 2 + 1)]
                    hi = xT[:, 0, c, :].bitcast(F32)
                    if kind == "attn":
                        i = v.tensor_tensor(xT[:, 1, c, :], src, hi, ALU.subtract)
                    else:
                        col = G_NORM[n] if kind == "norm" else G_ATT + 4 * n
                        i = v.scalar_tensor_tensor(xT[:, 1, c, :], src, gT[:, col + c:col + c + 1], hi, ALU.mult, ALU.subtract)
                    i.then_inc(xT_v, 1)

            def evac_proj(layer, hi):
                seg = SEG[layer]
                for g in range(PJ_AT[layer], hi):
                    halves, n, dst = PJ[g]
                    split_to(seg, halves[1] + 3)
                    for part in range(2 if layer < 2 else 0):
                        if g - PJ_AT[layer] == HEADS_AT[layer][part] + 1:
                            head_sums(layer, part)
                        if g - PJ_AT[layer] == HEADS_AT[layer][part] + 2:
                            head_norms(layer, part)
                    dve.wait_ge(used[seg], halves[1] + 1)
                    d = qkv_t(1)[:, dst:dst + n] if layer < 2 else qkv2[:, 1, dst:dst + n]
                    v.tensor_copy(d, pb[(2 * g + 1) % 4][:, 0:n]).then_inc(pj_v, 1)

            def head_sums(layer, part):
                nh = 16 if layer == 0 or part == 0 else 8
                for t in range(NT):
                    dve.wait_ge(hsq, 4 * layer + 2 * part + t + 1)
                    c0 = R_HEAD[layer] + 32 * part + nh * t
                    v.tensor_reduce(rms[:, c0:c0 + nh], xs[:, t, 0:HD * nh].rearrange("p (a b) -> p a b", b=HD),
                                    AX, ALU.add).then_inc(hss, 1)

            def head_norms(layer, part):
                root_wait(("head", layer, part))
                for t in range(NT):
                    if layer == 0 or part == 0:
                        r = R_HEAD[layer] + 32 * part + 16 * t
                        x = qkv_t(t)[:, 1536 * part:1536 * part + D].rearrange("p (a b) -> p a b", b=HD)
                        v.tensor_tensor(x, x, view(rms[:], r, [[1, 16], [0, HD]]), ALU.mult).then_inc(qn_ready, 1)
                        continue
                    r = R_HEAD[layer] + 32 + 8 * t
                    for br in range(2):
                        kx = view(qkv_t(t), 1536 + 512 * br, [[HD, NG], [1, HD]])
                        for twice in range(2):
                            v.tensor_tensor(view(xs[:, t, :], 512 * br + HD * twice, [[2 * HD, NG], [1, HD]]), kx,
                                            view(rms[:], r + 4 * br, [[1, NG], [0, HD]]), ALU.mult).then_inc(qn_ready, 1)

            def evac_heads(layer):
                for z, (_, dst, gain) in enumerate(QT[layer]):
                    if z // 2 % 2:
                        dve.wait_ge(qt_ready, (QT_AT[layer] + z) // 2 + 1)
                        src = pb[4 + (z // 2) % 4][:, S * (z % 2):S * (z % 2 + 1)]
                        if gain is None:
                            i = v.tensor_copy(dst, src)
                        else:
                            i = v.tensor_scalar(dst, src, g2T[:, gain:gain + 1], None, ALU.mult)
                        i.then_inc(qt_v, 1)

            def attention(layer):
                us = UN[layer]
                n = len(us)
                if layer == 2:
                    dve.wait_ge(band_loaded[0], 16 * (NH // 4 + 1))
                for i in range(n + 5):
                    if i < n:
                        u, g = us[i], U_AT[layer] + i
                        if layer < 2 and u.t == 0 and u.br == 0 and u.h % 4 == 0:
                            dve.wait_ge(band_loaded[u.h // 4 % 2], 16 * (2 * layer + u.h // 8 + 1))
                        dve.wait_ge(s_ready, g + 1)
                        if g >= 4:
                            dve.wait_ge(pt_ready, g - 3)
                        init = BIG if layer < 2 else sink[:, layer - 2, 1, u.h:u.h + 1]
                        v.tensor_tensor_reduce(sbuf_s[:, g % 4, 0:u.nk], pb[4 + g % 3][:, 0:u.nk], u.bias, -0.125, init,
                                               ALU.add, ALU.min, nmax[:, g:g + 1]).then_inc(s_max, 1)
                    if i >= 5:
                        u, g = us[i - 5], U_AT[layer] + i - 5
                        dve.wait_ge(e_done, g + 1)
                        r = rec[:, g % 4:g % 4 + 1]
                        if layer >= 2:
                            c = g - U_AT[2]
                            link(v.tensor_tensor(den[:, g:g + 1], den[:, g:g + 1], esink[:, c:c + 1], ALU.add))
                        link(v.reciprocal(r, den[:, g:g + 1]))
                        ob = pb[(0, 1, 7)[g % 3]][:, 0:HD]
                        dve.wait_ge(o_ready, g + 1)
                        if layer != 1:
                            v.tensor_scalar(u.o, ob, r, None, ALU.mult).then_inc(o_done, 1)
                            continue
                        gate = gates[:, u.t, 3 * u.h + (1, 2, 0)[u.br]:][:, 0:1]
                        if u.br == 0:
                            v.tensor_scalar(u.o, ob, r, gate, ALU.mult, ALU.mult).then_inc(o_done, 1)
                        else:
                            link(v.tensor_tensor(r, r, gate, ALU.mult))
                            dve.wait_ge(o_done, g)
                            v.scalar_tensor_tensor(u.o, ob, r, u.o, ALU.mult, ALU.add).then_inc(o_done, 1)

            def residual(ready, first):
                for c in range(2):
                    for t in range(NT):
                        dve.wait_ge(ready, first + 2 * c + t + 1)
                        hh = h[:, t, 512 * c:512 * (c + 1)]
                        v.tensor_tensor(hh, hh, pb[2 * c + t][:], ALU.add).then_inc(h_done, 1)

            def out_residual(k):
                for c in range(2):
                    split_to(0, OPW[k][c][1] + 3 if c == 0 else OPW[k][1][1] + 1)
                    for t in range(NT):
                        if t:
                            dve.wait_ge(used[0], OPW[k][c][1] + 1)
                        else:
                            dve.wait_ge(op_ready, 2 * k + c + 1)
                        hh = h[:, t, 512 * c:512 * (c + 1)]
                        v.tensor_tensor(hh, hh, pb[2 * c + t][:], ALU.add).then_inc(h_done, 1)

            def ffn(f):
                gate, up, down = FFW[f]
                for q in range(NQ):
                    split_to(0, up[q] + 1)
                    dve.wait_ge(th_done, NQ * f + q + 1)
                    link(v.scalar_tensor_tensor(ga, th, 1.0, pb[4 + q % 2][:].rearrange("p (a b) -> p a b", a=2), ALU.add, ALU.mult))
                    split_to(0, gate[q + 1] + 1 if q + 1 < NQ else down[q] + 1)
                    dve.wait_ge(used[0], up[q] + 1)
                    link(v.scalar_tensor_tensor(fh, ga, 0.5, pb[6 + q % 2][:].rearrange("p (a b) -> p a b", a=2), ALU.mult, ALU.mult))
                    link(v.tensor_copy(hidT[:, :, 0, :], fh))
                    v.tensor_tensor(hidT[:, :, 1, :], fh, hidT[:, :, 0, :].bitcast(F32), ALU.subtract).then_inc(hT_done, 1)
                dve.wait_ge(used[0], down[-1] + 1)
                for c in range(2):
                    for t in range(NT):
                        hh = h[:, t, 512 * c:512 * (c + 1)]
                        v.tensor_tensor(hh, hh, pb[2 * c + t][:], ALU.add).then_inc(h_done, 1)

            def transpose_p(f):
                dve.wait_ge(pT_done, f + 1)
                v.tensor_tensor(hidT[:, :, 1, :], pb[4][:].rearrange("p (a b) -> p a b", a=2), hidT[:, :, 0, :].bitcast(F32),
                                ALU.subtract).then_inc(pT_v, 1)

            def ple(f):
                split_to(0, PLW[f][1][1][1] + 1)
                for c in range(2):
                    for t in range(NT):
                        dve.wait_ge(ple_th, 4 * f + 2 * c + t + 1)
                        x = xs[:, t, 512 * c:512 * (c + 1)]
                        hh = h[:, t, 512 * c:512 * (c + 1)]
                        link(v.scalar_tensor_tensor(x, x, 1.0, pb[2 * c + t][:], ALU.add, ALU.mult))
                        v.scalar_tensor_tensor(hh, x, 0.5, hh, ALU.mult, ALU.add).then_inc(h_done, 1)

            def compress_in():
                for b in range(4):
                    dve.wait_ge(cT_rounded, 2 * b + 2)
                    kv, g = b // 2, 2 * (b % 2)
                    x = pb[4 + b][:].rearrange("p (g s) -> p g s", g=2)
                    for rows, lo, n in ((slice(0, HD), 0, S), (slice(HD, P), 1, S - 1)):
                        v.tensor_tensor(xc[rows, kv, 1, g:g + 2, 0:n], x[0:HD, :, lo:lo + n],
                                        xc[rows, kv, 0, g:g + 2, 0:n].bitcast(F32), ALU.subtract).then_inc(cT_done, 1)
                dve.wait_ge(cT_rounded, 9)
                v.tensor_tensor(posr[:, :, 1, :], g2T[:, H_POS:HEAD_ROWS].rearrange("p (v l) -> p v l", v=2),
                                posr[:, :, 0, :].bitcast(F32), ALU.subtract).then_inc(cT_done, 1)

            def compress():
                x = [cmph[:, kv, 0, 0:60] for kv in range(2)]
                for kv in range(2):
                    dve.wait_ge(used[0], CMPW[kv] + 1)
                    hb = cmph[:, kv, 0, 60:61]
                    link(v.tensor_tensor(hb, pb[kv][:, 128:129], gT[:, G_B1 + kv:G_B1 + kv + 1], ALU.add))
                    link(v.tensor_tensor(hb, hb, pb[kv][:, 129:130], ALU.add))
                    xv = x[kv].rearrange("p (g c) -> p c g", g=NG)
                    two = pb[kv][:, 0:2 * NG * NCMP].rearrange("p (c i g) -> p c i g", i=2, g=NG)
                    link(v.tensor_scalar(xv, two[:, :, 0, :], hb, None, ALU.add))
                    link(v.tensor_tensor(xv, xv, two[:, :, 1, :], ALU.add))
                    y = cmph[:, kv, 1, 0:60]
                    link(v.tensor_tensor(y, x[kv], x[kv], ALU.mult))
                    link(v.tensor_scalar(y, y, 0.044715, 1.0, ALU.mult, ALU.add))
                    v.tensor_tensor(y, y, x[kv], ALU.mult).then_inc(gel_in, 1)
                for kv in range(2):
                    dve.wait_ge(gel_th, kv + 1)
                    v.scalar_tensor_tensor(cmph[:, kv, 3, 0:60], cmph[:, kv, 2, 0:60], 1.0, x[kv], ALU.add, ALU.mult)\
                        .then_inc(gel_done, 1)
                dve.wait_ge(cmp_ready, 1)
                for kv in range(2):
                    link(v.scalar_tensor_tensor(cmpk[0:NCMP, kv, :, :], pb[2][0:NCMP, 256 * kv:256 * (kv + 1)].rearrange(
                        "p (g d) -> p g d", g=NG), 0.5, view(b2[0:NCMP, kv, :], 0, [[0, NG], [1, HD]]), ALU.mult, ALU.add))
                link(v.tensor_tensor(cmpd[0:NCMP, :, 0, :], cmpk[0:NCMP, 0, :, :], cmpk[0:NCMP, 0, :, :], ALU.mult))
                v.tensor_reduce(rms[0:NCMP, R_CMP:R_CMP + 4], cmpd[0:NCMP, :, 0, :], AX, ALU.add).then_inc(ss_done, 1)
                evac_heads(1)
                root_wait("cmp")
                for twice in range(2):
                    v.tensor_tensor(cmpd[0:NCMP, :, twice, :], cmpk[0:NCMP, 0, :, :],
                                    view(rms[0:NCMP, R_CMP:R_CMP + 4], 0, [[1, NG], [0, HD]]), ALU.mult).then_inc(cmpn_done, 1)
                dve.wait_ge(cmpT_ready, 1)
                v.tensor_scalar(cmpT[:, :, 0:NCMP], pb[3][:, 0:64].rearrange("p (g c) -> p g c", g=NG)[:, :, 0:NCMP],
                                g2T[:, 7:8], None, ALU.mult).then_inc(cmpT_done, 1)

            def nsa_gates():
                dve.wait_ge(g_th, 2)
                link(v.tensor_scalar(gates[:], gates[:], 0.5, 0.5, ALU.mult, ALU.add))
                g0 = view(gates[:, 0, :], 0, [[3, NH]])
                link(v.tensor_scalar(g0, g0, cst[:, C_VALID:C_VALID + 1], None, ALU.mult))

            def rope(l):
                dve.wait_ge(pj_a, PJ_AT[2 + l] + 2)
                dve.wait_ge(pj_v, PJ_AT[2 + l] + 2)
                nh = HEADS2 + KV2
                cos, sin = (cst[:, c:c + 16] for c in (C_COS, C_SIN))
                tmp = sbuf_p[:, :, :].rearrange("p a b -> p (a b)")
                for t in range(NT):
                    x1, x2 = (view(qkv2[:, t, :], o, [[HD, nh], [1, 8]]) for o in (0, 8))
                    cb, sbb = (view(a, 8 * t, [[0, nh], [1, 8]]) for a in (cos, sin))
                    k = [tmp[:, 80 * i:80 * (i + 1)].rearrange("p (a b) -> p a b", b=8) for i in range(4)]
                    v.tensor_tensor(k[0], x1, cb, ALU.mult)
                    v.tensor_tensor(k[1], x2, sbb, ALU.mult)
                    v.tensor_tensor(k[2], x2, cb, ALU.mult)
                    link(v.tensor_tensor(k[3], x1, sbb, ALU.mult))
                    v.tensor_tensor(x1, k[0], k[1], ALU.subtract)
                    link(v.tensor_tensor(x2, k[2], k[3], ALU.add))
                for t in range(NT):
                    for twice in range(2):
                        v.tensor_copy(view(xs[:, t, :], HD * twice, [[2 * HD, KV2], [1, HD]]),
                                      view(qkv2[:, t, :], 512, [[HD, KV2], [1, HD]])).then_inc(qn_ready, 1)

            def conv(l):
                v.memset(cuT[:, :, 0:1], 0.0)
                link(v.memset(cuT[:, :, S + 1:S + 2], 0.0))
                for half in range(2):
                    split_to(SEG[2 + l], CVW[l][2][1] + 1)
                    dve.wait_ge(used[SEG[2 + l]], CVW[l][2][half] + 1)
                    dve.wait_ge(gb_done, 4 * l + 4)
                    link(v.tensor_tensor(cuT[:, 2 * half:2 * half + 2, 1:S + 1],
                                         gcT[:, 512 * half:512 * (half + 1)].rearrange("p (a b) -> p a b", a=2),
                                         pb[4 + half][:].rearrange("p (a b) -> p a b", a=2), ALU.mult))
                for j in range(3):
                    for c in range(4):
                        y = yT[:, S * c:S * (c + 1)]
                        w = gT[:, G_CW + 12 * l + 4 * j + c:][:, 0:1]
                        x = cuT[:, c, j:j + S]
                        if j == 0:
                            i = v.tensor_scalar(y, x, w, None, ALU.mult)
                        else:
                            i = v.scalar_tensor_tensor(y, x, w, y, ALU.mult, ALU.add)
                    link(i)
                v.tensor_tensor(yT, yT, gbT, ALU.mult).then_inc(y_done, 1)
                split_to(SEG[2 + l], OPW[2 + l][0][1] + 2)
                dve.wait_ge(y_done, l + 1)
                for i in range(2):
                    for c in range(4):
                        y, g = yT[:, S * c:S * (c + 1)], gT[:, G_CONV + 4 * l + c:][:, 0:1]
                        if i == 0:
                            ins = v.tensor_scalar(xT[:, 0, 4 + c, :], y, g, None, ALU.mult)
                        else:
                            ins = v.scalar_tensor_tensor(xT[:, 1, 4 + c, :], y, g, xT[:, 0, 4 + c, :].bitcast(F32), ALU.mult,
                                                         ALU.subtract)
                        ins.then_inc(cx_done, 1)
                    if i == 0:
                        dve.wait_ge(cx_done, 8 * l + 4)
                dve.wait_ge(yss_ready, l + 1)
                v.tensor_copy(rms[:, R_CONV[l]:R_CONV[l] + 2], pb[7][:, 0:2]).then_inc(yss_done, 1)

            def attn_out(l):
                root_wait(("att", l))
                for t in range(NT):
                    x = xs[:, t, 0:CW]
                    v.tensor_scalar(x, x, rms[:, R_ATT[l] + t:R_ATT[l] + t + 1], float(CW ** 0.5), ALU.mult, ALU.mult)\
                        .then_inc(at_ready, 1)

            def residual2(l):
                root_wait(("conv", l))
                r = rms[:, R_CONV[l]:R_CONV[l] + 2]
                link(v.tensor_scalar(r, r, float(CW ** 0.5), None, ALU.mult))
                seg = SEG[2 + l]
                for c in range(2):
                    split_to(seg, OPW[2 + l][1][1] + 1)
                    for t in range(NT):
                        if t:
                            dve.wait_ge(used[seg], OPW[2 + l][c][1] + 1)
                        else:
                            dve.wait_ge(op_ready, 2 * (2 + l) + c + 1)
                        hh = h[:, t, 512 * c:512 * (c + 1)]
                        link(v.tensor_tensor(hh, hh, pb[2 * c + t][:], ALU.add))
                        v.scalar_tensor_tensor(hh, pb[4 + 2 * c + t][:], r[:, t:t + 1], hh, ALU.mult, ALU.add)\
                            .then_inc(h_done, 1)

            def route(l):
                dve.wait_ge(rt_ready, l + 1)

                def cols(a, n):
                    return rt[:, a:a + 2 * n].rearrange("p (t n) -> p t n", t=NT)

                lg = cols(0, 36)
                gmax, gidx = rt[:, 72:74], rt[:, 74:76]
                gcmp, goh, gx = cols(80, 4), cols(96, 4), cols(112, 4)
                gsum = rt[:, 120:122]
                elm, ecmp = cols(128, NE), cols(192, NE)
                oh = [cols(256, NE), cols(448, NE)]
                mx = [rt[:, 368:370], rt[:, 370:372]]
                idx = [rt[:, 372:374], rt[:, 374:376]]
                dz = rt[:, 364:366]
                asg = cols(384, NE)
                i4, i32 = cst[:, C_I4:C_I4 + 4], cst[:, C_I32:C_I32 + NE]

                def spread(x, n):
                    return view(x, 0, [[1, NT], [0, n]])

                both_w = pb[0][:, 0:2 * P].rearrange("p (t n) -> p t n", t=NT)
                link(v.tensor_tensor(lg, both_w[:, :, 0:36], view(brt[:, l, :], 0, [[0, NT], [1, 36]]), ALU.add))
                link(v.tensor_tensor(lg, lg, both_w[:, :, 36:72], ALU.add))
                gl, el = lg[:, :, 0:NEG], lg[:, :, NEG:36]
                link(v.tensor_reduce(gmax, gl, AX, ALU.max))
                link(v.tensor_tensor(gcmp, gl, spread(gmax, 4), ALU.is_lt))
                link(v.scalar_tensor_tensor(gcmp, gcmp, 1.0e6, view(i4, 0, [[0, NT], [1, 4]]), ALU.mult, ALU.add))
                link(v.tensor_reduce(gidx, gcmp, AX, ALU.min))
                link(v.tensor_tensor(goh, view(i4, 0, [[0, NT], [1, 4]]), spread(gidx, 4), ALU.is_equal))
                v.tensor_tensor(gx, gl, spread(gmax, 4), ALU.subtract).then_inc(rt_x, 1)
                link(v.tensor_scalar(gcmp, goh, -1.0, BIG, ALU.add, ALU.mult))
                for t in range(NT):
                    o8 = view(goh, 4 * t, [[1, 4], [0, 8]])
                    e8 = view(elm, NE * t, [[8, 4], [1, 8]])
                    link(v.tensor_tensor(e8, view(el, 36 * t, [[8, 4], [1, 8]]), o8, ALU.mult))
                    link(v.tensor_tensor(e8, e8, view(gcmp, 4 * t, [[1, 4], [0, 8]]), ALU.add))
                for k in range(2):
                    link(v.tensor_reduce(mx[k], elm, AX, ALU.max))
                    link(v.tensor_tensor(ecmp, elm, spread(mx[k], NE), ALU.is_lt))
                    link(v.scalar_tensor_tensor(ecmp, ecmp, 1.0e6, view(i32, 0, [[0, NT], [1, NE]]), ALU.mult, ALU.add))
                    link(v.tensor_reduce(idx[k], ecmp, AX, ALU.min))
                    link(v.tensor_tensor(oh[k], view(i32, 0, [[0, NT], [1, NE]]), spread(idx[k], NE), ALU.is_equal))
                    if k == 0:
                        link(v.scalar_tensor_tensor(elm, oh[0], -BIG, elm, ALU.mult, ALU.add))
                v.tensor_tensor(asg, oh[0], oh[1], ALU.add).then_inc(as_done, 1)
                v.tensor_tensor(dz, mx[1], mx[0], ALU.subtract).then_inc(rt_x, 1)
                dve.wait_ge(cnt_ready, l + 1)
                cm, wm = rt[0:NE, 512:640], rt[0:NE, 640:768]
                v.tensor_copy(cm, pb[1][0:NE, 0:P]).then_inc(cnt_done, 1)
                wt = rt[0:NE, 768:896]
                link(v.tensor_scalar(wm, pb[1][0:NE, 0:P], 0.0, None, ALU.is_gt))
                for i in range(1, S // W):
                    link(v.tensor_scalar(wt, pb[1][0:NE, 0:P], float(i * W), None, ALU.is_gt))
                    link(v.tensor_tensor(wm, wm, wt, ALU.add))
                v.tensor_scalar(wm, wm, ident[0:NE, 0:1], None, ALU.max).then_inc(cnt_done, 1)
                dve.wait_ge(rt_e, 2 * l + 2)
                link(v.tensor_reduce(gsum, gx, AX, ALU.add))
                g1, g2 = rt[:, 376:378], rt[:, 378:380]
                link(v.tensor_scalar(g1, dz, 1.0, None, ALU.add))
                link(v.tensor_tensor(g1, g1, gsum, ALU.mult))
                link(v.reciprocal(g1, g1))
                link(v.tensor_tensor(g2, dz, g1, ALU.mult))
                dve.wait_ge(pos_ready, l + 1)
                ja, jo, jv = jobs_work()
                c0, w0, w1 = rt[0:NE, 1152:1153], rt[0:NE, 1153:1154], rt[0:NE, 1154:1155]
                ij = cst[0:NE, C_I512:C_I512 + JOBS]
                v.tensor_copy(c0, pb[3][0:NE, NE:NE + 1])
                link(v.tensor_copy(w0, pb[3][0:NE, NE + 1:NE + 2]))
                link(v.tensor_tensor(w1, w0, wm[:, 0:1], ALU.add))
                v.scalar_tensor_tensor(jv, w0, float(-W), c0, ALU.mult, ALU.add)
                link(v.tensor_scalar(ja, ij, w1, None, ALU.is_ge))
                v.scalar_tensor_tensor(jo, ij, w0, ja, ALU.is_ge, ALU.subtract).then_inc(job_cols, 1)
                st = rt[:, 896:896 + NE]
                link(v.tensor_copy(st, pb[3][:, 0:NE]))
                pos = cols(928, NE)
                link(v.tensor_tensor(pos, pb[2][:, 0:2 * NE].rearrange("p (t n) -> p t n", t=NT),
                                     view(st, 0, [[0, NT], [1, NE]]), ALU.add))
                sl = [rt[:, 992:994], rt[:, 994:996]]
                for k in range(2):
                    link(v.tensor_tensor(ecmp, oh[k], pos, ALU.mult))
                    link(v.tensor_reduce(sl[k], ecmp, AX, ALU.add))
                dve.wait_ge(job_ready, l + 1)
                link(v.tensor_scalar(tab[0:1, 0:JOBS], pb[1][0:1, 0:JOBS], float(NE - 1), None, ALU.min))
                link(v.scalar_tensor_tensor(tab[0:1, JOBS:2 * JOBS], cst[0:1, C_I512:C_I512 + JOBS], float(W),
                                            pb[1][0:1, 64:64 + JOBS], ALU.mult, ALU.add))
                v.tensor_scalar(tab[0:1, 2 * JOBS:2 * JOBS + 1], pb[1][0:1, 128:129], -2.0, None, ALU.add).then_inc(tab_done, 1)
                i512 = cst[:, C_I512:C_I512 + NS]
                for t in range(NT):
                    link(v.tensor_scalar(sel[:, t, :], i512, sl[0][:, t:t + 1], None, ALU.is_equal))
                    i = v.scalar_tensor_tensor(sel[:, t, :], i512, sl[1][:, t:t + 1], sel[:, t, :].bitcast(F32), ALU.is_equal, ALU.add)
                    if t == 0:
                        link(i)
                i.then_inc(sel_done, 1)
                for t in range(NT):
                    link(v.tensor_scalar(gsel[:, t, :], i512, sl[0][:, t:t + 1], g1[:, t:t + 1], ALU.is_equal, ALU.mult))
                    link(v.tensor_scalar(gtmp, i512, sl[1][:, t:t + 1], g2[:, t:t + 1], ALU.is_equal, ALU.mult))
                    i = v.tensor_tensor(gsel[:, t, :], gsel[:, t, :], gtmp, ALU.add)
                    if t == 0:
                        link(i)
                i.then_inc(sel_done, 1)

            def moe(l):
                seg = 2 * l + 1

                def rest_half(j, q):
                    dve.wait_ge(hi_done[seg], at(j, 6, q - 1))
                    hi, lo = job_parts(l, q)
                    v.tensor_tensor(lo, raw[:, job_place(l, q), :], hi.bitcast(F32), ALU.subtract).then_inc(lo_done[seg], 1)

                rest_half(0, 2)
                normalise(7 + 2 * l)
                dve.wait_ge(wr_rounded, l + 1)
                v.tensor_tensor(wrs[:, :, 1, :], wr[:, l, :, :], wrs[:, :, 0, :].bitcast(F32), ALU.subtract).then_inc(wr_ready, 1)
                rest_half(0, 3)
                evac_tp(10 + 3 * l)
                rest_half(0, 4)
                route(l)
                col = G_NORM[7 + 2 * l]
                v.memset(xsT[:, :, NS:NSP], 0.0).then_inc(xsT_v, 1)
                for k in range(1, KC, 2):
                    dve.wait_ge(ga_ready, KC * l + k + 1)
                    v.tensor_scalar(xsT[:, k, 0:NS], pb[4 + k % 4][:], gT[:, col + k:col + k + 1], None, ALU.mult)\
                        .then_inc(xsT_v, 1)
                more = dve.value_load(tab[0:1, 2 * JOBS:2 * JOBS + 1], min_val=NS // W - 2, max_val=JOBS - 2)
                dve.sem_inc(yadd_done[l], 1)
                dve.wait_ge(xsT_a, 4 * (l + 1))
                dve.wait_ge(xsT_v, 5 * (l + 1))

                def window(j):
                    s0 = dve.value_load(tab[0:1, bass.ds(at(j, 1, JOBS), 1)], min_val=0, max_val=NS)
                    dve.wait_ge(xw_rounded[l], at(j, 1, 1))
                    v.tensor_tensor(xw[:, :, W:2 * W], xsT[:, :, bass.ds(s0, W)], xw[:, :, 0:W].bitcast(F32), ALU.subtract)\
                        .then_inc(xw_ready[l], 1)

                def sums(j, back):
                    for m, dst in enumerate((eg, eu)):
                        dve.wait_ge(eg_first[l], at(j, 2, m + 1 - 2 * back))
                        d = dst.rearrange("p (k s) -> p k s", k=4)
                        v.tensor_tensor(d, d, pb[2 + m][:].rearrange("p (k i s) -> p k i s", k=4, i=2)[:, :, 1, :], ALU.add)\
                            .then_inc(g_added[l] if m == 0 else ech[l], 1)

                def hidden(j, back):
                    dve.wait_ge(eth_done[l], at(j, 1, 1 - back))
                    v.scalar_tensor_tensor(ea, ea, 1.0, eg, ALU.add, ALU.mult).then_inc(ech[l], 1)
                    dve.wait_ge(ech[l], at(j, 4, 2 - 4 * back))
                    v.scalar_tensor_tensor(eh, ea, 0.5, eu, ALU.mult, ALU.mult).then_inc(ech[l], 1)
                    dve.wait_ge(ech[l], at(j, 4, 3 - 4 * back))
                    x = eh.rearrange("p (j s) -> p j s", j=4)
                    v.tensor_copy(ehl[:, :, 0:W], x).then_inc(ech[l], 1)
                    dve.wait_ge(ech[l], at(j, 4, 4 - 4 * back))
                    v.tensor_tensor(ehl[:, :, W:2 * W], x, ehl[:, :, 0:W].bitcast(F32), ALU.subtract).then_inc(eh_done[l], 1)

                def to_slots(j, back):
                    s0 = dve.value_load(tab[0:1, bass.ds(at(j, 1, JOBS - back), 1)], min_val=0, max_val=NS)
                    for b in range(2):
                        dve.wait_ge(y_first[l], at(j, 2, b + 1 - 2 * back))
                        d = ysT[:, 4 * b:4 * b + 4, bass.ds(s0, W)]
                        v.tensor_tensor(d, d, pb[6 + b][:].rearrange("p (k i s) -> p k i s", k=4, i=2)[:, :, 1, :], ALU.add)\
                            .then_inc(yadd_done[l], 1)

                def combine():
                    for c in range(2):
                        dve.wait_ge(gct_ready, 2 * l + c + 1)
                        v.tensor_copy(gcombT[:, 2 * c:2 * c + 2, :], pb[2 + c][:].rearrange("p (a b) -> p a b", a=2))\
                            .then_inc(gct_done, 1)

                def step(j):
                    later = not isinstance(j, int)
                    g0, g1, u0, u1 = (q for q, _, _ in gate_up(j))
                    window(j)
                    if later:
                        rest_half(j, g0)
                    if later or j:
                        rest_half(j, g1)
                        sums(j, 1)
                        rest_half(j, u0)
                        hidden(j, 1)
                    else:
                        combine()
                    rest_half(j, u1)
                    if later:
                        to_slots(j, 2)
                    if later or j:
                        rest_half(j, down_at(False))
                        rest_half(j, down_at(False) + 1)
                    else:
                        rest_half(1, 0)

                step(0)
                step(1)
                with dve.Fori(0, more) as j:
                    step(j)
                sums(more, 1)
                hidden(more, 1)
                rest_half(more, down_at(True))
                rest_half(more, down_at(True) + 1)
                to_slots(more, 2)
                to_slots(more, 1)
                for i in range(1, 8, 2):
                    dve.wait_ge(yt_ready, 8 * l + i + 1)
                    v.tensor_copy(ysort[:, i // 2, 512:1024], pb[4 + i % 4][:]).then_inc(yt_v, 1)
                residual(op_ready2, 4 * l)

            normalise(0)
            evac_tp(0)
            setup_rest()
            evac_proj(0, PJ_AT[1])
            dve.wait_ge(scr_written, 32)
            evac_heads(0)
            split_to(0, OPW[0][0][0] + 1)
            attention(0)
            evac_tp(1)
            out_residual(0)
            normalise(1)
            evac_tp(2)
            ffn(0)
            transpose_p(0)
            normalise(2)
            evac_tp(3)
            ple(0)
            normalise(3)
            evac_tp(4)
            evac_proj(1, PJ_AT[2])
            split_to(0, OPW[1][0][0] + 1)
            compress_in()
            head_norms(1, 1)
            nsa_gates()
            compress()
            attention(1)
            evac_tp(5)
            out_residual(1)
            normalise(4)
            evac_tp(6)
            ffn(1)
            transpose_p(1)
            normalise(5)
            evac_tp(7)
            ple(1)
            for l in range(2):
                normalise(6 + 2 * l)
                evac_tp(8 + 3 * l)
                evac_proj(2 + l, PJ_AT[2 + l] + 2)
                rope(l)
                conv(l)
                evac_heads(2 + l)
                attention(2 + l)
                attn_out(l)
                evac_tp(9 + 3 * l)
                residual2(l)
                moe(l)
            root_wait(("norm", 10))
            dve.wait_ge(par2_loaded, 16 * (len(PARS) - NPAR0 + 1))
            for t in range(NT):
                link(v.tensor_scalar(xs[:, t, :], h[:, t, :], rms[:, R_NORM[10] + t:R_NORM[10] + t + 1], float(D ** 0.5),
                                     ALU.mult, ALU.mult))
                v.tensor_tensor(xs[:, t, :], xs[:, t, :], gfin, ALU.mult).then_inc(out_ready, 1)


def shape_constants():
    c = np.zeros((P, C_W), np.float32)
    c[:, C_ID:C_ID + P] = np.eye(P)
    c[:, C_TRI:C_TRI + P] = np.triu(np.ones((P, P)), 1)
    c[:, C_I512:C_I512 + NS] = np.arange(NS)
    c[:, C_I32:C_I32 + NE] = np.arange(NE)
    c[:, C_I4:C_I4 + NEG] = np.arange(NEG)
    c[:, C_VALID] = np.arange(P) >= CMP_LEN - 1
    inv = np.float32(500000.0) ** (-np.arange(0, 16, 2, dtype=np.float32) / np.float32(16))
    ang = np.arange(S, dtype=np.float32)[:, None] * inv[None, :].astype(np.float32)
    for col, f in ((C_COS, np.cos), (C_SIN, np.sin)):
        a = f(ang.astype(np.float64)).astype(np.float32).reshape(NT, P, 8)
        c[:, col:col + 16] = a.transpose(1, 0, 2).reshape(P, 16)
    d = np.arange(512) - 255
    exact = BUCKETS // 2
    nf = np.maximum(d, 1).astype(np.float32)
    large = exact + (np.log(nf / np.float32(exact)) / np.float32(np.log(2048 / exact)) * np.float32(BUCKETS - exact)).astype(np.int32)
    bucket = np.where(d < exact, np.maximum(d, 0), np.minimum(large, BUCKETS - 1))
    onehot = ((bucket[None, :] == np.arange(BUCKETS)[:, None]) & (d >= 0)[None, :]).astype(np.float32)
    causal = np.where(d >= 0, 0.0, OFF)
    times = np.where(d >= 0, (d <= 128) * 1 + (d % 4 == 0) * 1 + (d % 16 == 0) * 1, 0)
    dilated = np.where(times > 0, 8.0 * np.log(np.maximum(times, 1)), OFF)
    masks = np.tile(np.concatenate([causal, dilated]).astype(np.float32), (NH, 1))
    window = np.where(np.abs(d) <= 128, 0.0, OFF).astype(np.float32)
    return {"consts": c, "onehot": onehot, "row_masks": masks, "window_band": window}


_INS = ["x", "p", "rel_bias", "norm_mix", "norm_ffn", "norm_ple", "w_ffn_gate", "w_ffn_up", "w_ffn_down", "w_ple_proj",
        "w_ple_gate", "w_in_ab", "w_out_ab", "qn_moba", "kn_moba", "qn_dil", "kn_dil", "w_in_nsa", "w_out_nsa",
        "qn_nsa", "kn_cmp", "kn_slc", "kn_win", "cmp_k_pos", "cmp_k_w1", "cmp_k_b1", "cmp_k_w2", "cmp_k_b2",
        "cmp_v_pos", "cmp_v_w1", "cmp_v_b1", "cmp_v_w2", "cmp_v_b2", "norm_mix_2", "w_in_2", "attn_sink_2",
        "conv_w_2", "norm_attn_out_2", "norm_conv_out_2", "w_out_2", "norm_ffn_2", "w_router_group_2",
        "b_router_group_2", "w_router_expert_2", "b_router_expert_2", "w_expert_gate_2", "w_expert_up_2",
        "w_expert_down_2", "norm_final_2"]


def kernel(**inputs):
    import numpy as _np
    import concourse.bacc as _bacc
    from concourse import mybir as _mybir
    from concourse.bass_utils import run_bass_kernel_spmd as _run

    nc = _bacc.Bacc("TRN2", target_bir_lowering=False, num_devices=1)
    arrays, args = {}, {}
    for name, a in [(n, inputs[n]) for n in _INS] + list(shape_constants().items()):
        a = _np.ascontiguousarray(a)
        arrays[f"in_{name}"] = a
        args[name] = nc.dram_tensor(f"in_{name}", a.shape, _mybir.dt.from_np(a.dtype), kind="ExternalInput").ap()
    out = nc.dram_tensor("out_0", (1, S, D), F32, kind="ExternalOutput").ap()
    build(nc, args, out)
    r = _run(nc, [arrays], core_ids=[0])
    return r.results[0]["out_0"]
```
